# Optimizing a Trainium2 kernel written in Bass

```python
import math
import jax
import jax.numpy as jnp
from jax import lax
import numpy as np

D_MODEL = 1024
BATCH = 1
SEQ = 512
DEPTH = 2
DEC_BATCH = 8
DEC_SEQ = 8
PAST_LEN = 1024
PAGE_SIZE = 128

N_MIXERS = 2
N_CONV_LAYERS = (DEPTH + 1) // 2
N_NSA_LAYERS = DEPTH // 2
D_CONV = D_MODEL
CONV_W = 31
N_HEADS = 16
N_KV = 4
N_REP = N_HEADS // N_KV
HEAD_DIM = D_MODEL // N_HEADS
ROT_DIM = HEAD_DIM // 4
ROPE_THETA = 500000.0
L_CMP = 32
STRIDE = L_CMP // 2
CMP_HID = 2 * HEAD_DIM
L_SEL = 64
N_TOP = 16
WINDOW = 512
Q_BLOCK = 64
Q_DIM = N_HEADS * HEAD_DIM
KV_DIM = N_KV * HEAD_DIM
GATE_DIM = 3 * N_HEADS
D_IN_NSA = Q_DIM + 6 * KV_DIM + GATE_DIM
D_FF = 4 * D_MODEL
D_PLE = 256
EPS = 1e-6
NEG = -1e30
FORCE = 1e6

kernel_name = 'hybrid_conformer_conv_nsa_decoder_step'

def rms_norm(x, g):
    x32 = x.astype(jnp.float32)
    y = x32 * lax.rsqrt(jnp.mean(x32 * x32, axis=-1, keepdims=True) + EPS)
    return (y * g.astype(jnp.float32)).astype(x.dtype)

def layer_norm(x, g, b):
    x32 = x.astype(jnp.float32)
    xc = x32 - jnp.mean(x32, axis=-1, keepdims=True)
    var = jnp.mean(xc * xc, axis=-1, keepdims=True)
    return (xc * lax.rsqrt(var + EPS) * g.astype(jnp.float32) + b.astype(jnp.float32)).astype(x.dtype)

def rope(x, pos):
    half = ROT_DIM // 2
    inv = jnp.float32(ROPE_THETA) ** (-jnp.arange(half, dtype=jnp.float32) * (2.0 / ROT_DIM))
    ang = pos.astype(jnp.float32)[:, None] * inv[None, :]
    cos = jnp.cos(ang)[None, :, None, :]
    sin = jnp.sin(ang)[None, :, None, :]
    x1 = x[..., :half].astype(jnp.float32)
    x2 = x[..., half:ROT_DIM].astype(jnp.float32)
    rot = jnp.concatenate([x1 * cos - x2 * sin, x2 * cos + x1 * sin], axis=-1).astype(x.dtype)
    return jnp.concatenate([rot, x[..., ROT_DIM:]], axis=-1)

def squared_relu_mlp(h, w1, w2):
    return jnp.square(jax.nn.relu(h @ w1)) @ w2

def conv_module(h, state, w_pw1, b_pw1, w_dw, b_dw, ln_g, ln_b, w_pw2, b_pw2):
    u = h @ w_pw1 + b_pw1
    u = u[..., :D_CONV] * jax.nn.sigmoid(u[..., D_CONV:])
    ext = jnp.concatenate([state.astype(u.dtype), u], axis=1)
    y = lax.conv_general_dilated(ext, w_dw[:, None, :].astype(u.dtype), (1,), 'VALID',
                                 dimension_numbers=('NWC', 'WIO', 'NWC'),
                                 feature_group_count=D_CONV) + b_dw
    y = jax.nn.silu(layer_norm(y, ln_g, ln_b))
    return y @ w_pw2 + b_pw2, ext[:, -(CONV_W - 1):]

def nsa_project(h, pos, w_in):
    B, T, _ = h.shape
    z = h @ w_in
    cuts = np.cumsum([Q_DIM] + [KV_DIM] * 6).tolist()
    q, kc, vc, ks, vs, kw, vw, g = jnp.split(z, cuts, axis=-1)
    q = q.reshape(B, T, N_HEADS, HEAD_DIM)
    q_rot = rope(q, pos).reshape(B, T, N_KV, N_REP, HEAD_DIM)
    q = q.reshape(B, T, N_KV, N_REP, HEAD_DIM)
    kv = lambda a: a.reshape(B, T, N_KV, HEAD_DIM)
    gates = jax.nn.sigmoid(g.reshape(B, T, N_KV, N_REP, 3))
    return q, q_rot, kv(kc), kv(vc), rope(kv(ks), pos), kv(vs), rope(kv(kw), pos), kv(vw), gates

def compress(k, pe, w1, w2):
    B, S, G, Dh = k.shape
    n_ch = -(-S // STRIDE)
    kp = jnp.pad(k, ((0, 0), (0, n_ch * STRIDE - S), (0, 0), (0, 0)))
    chunks = kp.reshape(B, n_ch, STRIDE, G, Dh)
    a = jnp.einsum('bnsgd,sdh->bngh', chunks, w1[:STRIDE])
    b = jnp.einsum('bnsgd,sdh->bngh', chunks, w1[STRIDE:])
    c = jnp.einsum('ld,ldh->h', pe, w1)
    hid = jax.nn.silu(a[:, :-1] + b[:, 1:] + c)
    return jnp.einsum('bngh,hd->bngd', hid, w2)

def to_sel_blocks(k):
    B, S, G, Dh = k.shape
    n_sel = -(-S // L_SEL)
    kp = jnp.pad(k, ((0, 0), (0, n_sel * L_SEL - S), (0, 0), (0, 0)))
    return kp.reshape(B, n_sel, L_SEL, G, Dh).transpose(0, 3, 1, 2, 4)

def nsa_core(q, q_rot, gates, q_pos, kc, vc, ksb, vsb, kw, vw, kw_pos):
    B = q.shape[0]
    n_cmp = kc.shape[1]
    n_sel = ksb.shape[2]
    scale = HEAD_DIM ** -0.5
    cmp_end = jnp.arange(n_cmp) * STRIDE + (L_CMP - 1)
    cmask = (cmp_end[None, :] <= q_pos[:, None])[None, :, None, None, :]
    lc = jnp.einsum('bqgrd,bcgd->bqgrc', q, kc).astype(jnp.float32) * scale
    pc = jax.nn.softmax(jnp.where(cmask, lc, NEG), axis=-1) * cmask
    o_cmp = jnp.einsum('bqgrc,bcgd->bqgrd', pc.astype(vc.dtype), vc)
    ci = jnp.arange(n_cmp)[:, None] * STRIDE
    sj = jnp.arange(n_sel)[None, :] * L_SEL
    overlap = ((ci < sj + L_SEL) & (ci + L_CMP > sj)).astype(jnp.float32)
    imp = jnp.einsum('bqgrc,cs->bqgs', pc, overlap)
    blk = jnp.arange(n_sel)[None, :]
    cur = (q_pos // L_SEL)[:, None]
    forced = ((blk == 0) | (blk == cur) | (blk == cur - 1))[None, :, None, :]
    future = (blk * L_SEL > q_pos[:, None])[None, :, None, :]
    score = jnp.where(future, -jnp.inf, jnp.where(forced, FORCE, imp))
    _, idx = lax.top_k(score, min(N_TOP, n_sel))
    bi = jnp.arange(B)[:, None, None, None]
    gi = jnp.arange(N_KV)[None, None, :, None]
    k_g = ksb[bi, gi, idx]
    v_g = vsb[bi, gi, idx]
    sel_pos = idx[..., None] * L_SEL + jnp.arange(L_SEL)
    smask = (sel_pos <= q_pos[None, :, None, None, None])[:, :, :, None]
    ls = jnp.einsum('bqgrd,bqgkld->bqgrkl', q_rot, k_g).astype(jnp.float32) * scale
    ls = jnp.where(smask, ls, NEG)
    shp = ls.shape
    ps = jax.nn.softmax(ls.reshape(shp[:4] + (-1,)), axis=-1).reshape(shp)
    o_sel = jnp.einsum('bqgrkl,bqgkld->bqgrd', ps.astype(v_g.dtype), v_g)
    wmask = ((kw_pos[None, :] <= q_pos[:, None]) & (kw_pos[None, :] > q_pos[:, None] - WINDOW)
             & (kw_pos[None, :] >= 0))[None, :, None, None, :]
    lw = jnp.einsum('bqgrd,bkgd->bqgrk', q_rot, kw).astype(jnp.float32) * scale
    pw = jax.nn.softmax(jnp.where(wmask, lw, NEG), axis=-1)
    o_win = jnp.einsum('bqgrk,bkgd->bqgrd', pw.astype(vw.dtype), vw)
    return gates[..., 0:1] * o_cmp + gates[..., 1:2] * o_sel + gates[..., 2:3] * o_win

def nsa_prompt(h, w_in, w_out, cmp_pe, cmp_w1, cmp_w2):
    B, T, _ = h.shape
    pos = jnp.arange(T)
    q, q_rot, kc, vc, ks, vs, kw, vw, gates = nsa_project(h, pos, w_in)
    kcc = compress(kc, cmp_pe[0], cmp_w1[0], cmp_w2[0])
    vcc = compress(vc, cmp_pe[1], cmp_w1[1], cmp_w2[1])
    ksb = to_sel_blocks(ks)
    vsb = to_sel_blocks(vs)
    kw_pad = jnp.pad(kw, ((0, 0), (WINDOW, 0), (0, 0), (0, 0)))
    vw_pad = jnp.pad(vw, ((0, 0), (WINDOW, 0), (0, 0), (0, 0)))
    qb = min(Q_BLOCK, T)

    def one_block(n):
        s = n * qb
        sl = lambda a: lax.dynamic_slice_in_dim(a, s, qb, axis=1)
        q_pos = s + jnp.arange(qb)
        kw_pos = s - WINDOW + jnp.arange(WINDOW + qb)
        kw_b = lax.dynamic_slice_in_dim(kw_pad, s, WINDOW + qb, axis=1)
        vw_b = lax.dynamic_slice_in_dim(vw_pad, s, WINDOW + qb, axis=1)
        return nsa_core(sl(q), sl(q_rot), sl(gates), q_pos, kcc, vcc, ksb, vsb, kw_b, vw_b, kw_pos)

    o = lax.map(one_block, jnp.arange(T // qb))
    o = jnp.moveaxis(o, 0, 1).reshape(B, T, Q_DIM)
    n_win = min(WINDOW, T)
    win_rows = jnp.stack([kw, vw], axis=2)[:, T - n_win:]
    return o @ w_out, jnp.stack([kc, vc], axis=2), jnp.stack([ks, vs], axis=2), win_rows

def nsa_sample(h, cache_cmp_l, cache_sel_l, cache_win_l, page_table, w_in, w_out, cmp_pe, cmp_w1, cmp_w2):
    B, T, _ = h.shape
    past_len = page_table.shape[1] * cache_cmp_l.shape[1]
    w_buf = cache_win_l.shape[1]
    pos = past_len + jnp.arange(T)
    q, q_rot, kc, vc, ks, vs, kw, vw, gates = nsa_project(h, pos, w_in)
    new_cmp = jnp.stack([kc, vc], axis=2)
    new_sel = jnp.stack([ks, vs], axis=2)
    new_win = jnp.stack([kw, vw], axis=2)
    past_cmp = cache_cmp_l[page_table].reshape(B, past_len, 2, N_KV, HEAD_DIM)
    past_sel = cache_sel_l[page_table].reshape(B, past_len, 2, N_KV, HEAD_DIM)
    full_cmp = jnp.concatenate([past_cmp.astype(h.dtype), new_cmp], axis=1)
    full_sel = jnp.concatenate([past_sel.astype(h.dtype), new_sel], axis=1)
    kcc = compress(full_cmp[:, :, 0], cmp_pe[0], cmp_w1[0], cmp_w2[0])
    vcc = compress(full_cmp[:, :, 1], cmp_pe[1], cmp_w1[1], cmp_w2[1])
    ksb = to_sel_blocks(full_sel[:, :, 0])
    vsb = to_sel_blocks(full_sel[:, :, 1])
    win_all = jnp.concatenate([cache_win_l.astype(h.dtype), new_win], axis=1)
    kw_pos = past_len - w_buf + jnp.arange(w_buf + T)
    o = nsa_core(q, q_rot, gates, pos, kcc, vcc, ksb, vsb, win_all[:, :, 0], win_all[:, :, 1], kw_pos)
    return o.reshape(B, T, Q_DIM) @ w_out, new_cmp, new_sel, win_all[:, -w_buf:]

def setup_inputs(seed: int = 0) -> dict:
    key = jax.random.key(seed)
    ks = jax.random.split(key, 32)

    def nrm(i, shape, scale=1.0):
        return jax.random.normal(ks[i], shape, jnp.float32) * scale

    n_pages = PAST_LEN // PAGE_SIZE
    n_pool = (DEC_BATCH * n_pages * 5) // 4
    w_buf = min(WINDOW, PAST_LEN)
    page_table = jax.random.permutation(ks[6], n_pool)[:DEC_BATCH * n_pages].reshape(DEC_BATCH, n_pages).astype(jnp.int32)
    return {
        'x_prompt': nrm(0, (BATCH, SEQ, D_MODEL)),
        'x_sample': nrm(1, (DEC_BATCH, DEC_SEQ, D_MODEL)),
        'cache_cmp': nrm(2, (N_NSA_LAYERS, n_pool, PAGE_SIZE, 2, N_KV, HEAD_DIM)),
        'cache_sel': nrm(3, (N_NSA_LAYERS, n_pool, PAGE_SIZE, 2, N_KV, HEAD_DIM)),
        'cache_win': nrm(4, (N_NSA_LAYERS, DEC_BATCH, w_buf, 2, N_KV, HEAD_DIM)),
        'state_conv': nrm(5, (N_CONV_LAYERS, DEC_BATCH, CONV_W - 1, D_CONV)),
        'page_table': page_table,
        'p_prompt': nrm(7, (DEPTH, BATCH, SEQ, D_PLE)),
        'p_sample': nrm(8, (DEPTH, DEC_BATCH, DEC_SEQ, D_PLE)),
        'norm_g': 1.0 + nrm(9, (DEPTH, 4, D_MODEL), 0.02),
        'w_ff1': nrm(10, (DEPTH, D_MODEL, D_FF), D_MODEL ** -0.5),
        'w_ff2': nrm(11, (DEPTH, D_FF, D_MODEL), D_FF ** -0.5),
        'w_ple': nrm(12, (DEPTH, D_PLE, D_MODEL), D_PLE ** -0.5),
        'w_ple_gate': nrm(13, (DEPTH, D_MODEL, D_MODEL), D_MODEL ** -0.5),
        'b_ple_gate': nrm(14, (DEPTH, D_MODEL), 0.01),
        'conv_w_pw1': nrm(15, (N_CONV_LAYERS, D_MODEL, 2 * D_CONV), D_MODEL ** -0.5),
        'conv_b_pw1': nrm(16, (N_CONV_LAYERS, 2 * D_CONV), 0.01),
        'conv_w_dw': nrm(17, (N_CONV_LAYERS, CONV_W, D_CONV), CONV_W ** -0.5),
        'conv_b_dw': nrm(18, (N_CONV_LAYERS, D_CONV), 0.01),
        'conv_ln_g': 1.0 + nrm(19, (N_CONV_LAYERS, D_CONV), 0.02),
        'conv_ln_b': nrm(20, (N_CONV_LAYERS, D_CONV), 0.01),
        'conv_w_pw2': nrm(21, (N_CONV_LAYERS, D_CONV, D_MODEL), D_CONV ** -0.5),
        'conv_b_pw2': nrm(22, (N_CONV_LAYERS, D_MODEL), 0.01),
        'nsa_w_in': nrm(23, (N_NSA_LAYERS, D_MODEL, D_IN_NSA), D_MODEL ** -0.5),
        'nsa_w_out': nrm(24, (N_NSA_LAYERS, Q_DIM, D_MODEL), Q_DIM ** -0.5),
        'nsa_cmp_pe': nrm(25, (N_NSA_LAYERS, 2, L_CMP, HEAD_DIM), 0.1),
        'nsa_cmp_w1': nrm(26, (N_NSA_LAYERS, 2, L_CMP, HEAD_DIM, CMP_HID), (L_CMP * HEAD_DIM) ** -0.5),
        'nsa_cmp_w2': nrm(27, (N_NSA_LAYERS, 2, CMP_HID, HEAD_DIM), CMP_HID ** -0.5),
    }

def reference(x_prompt, x_sample, cache_cmp, cache_sel, cache_win, state_conv, page_table, p_prompt, p_sample,
              norm_g, w_ff1, w_ff2, w_ple, w_ple_gate, b_ple_gate,
              conv_w_pw1, conv_b_pw1, conv_w_dw, conv_b_dw, conv_ln_g, conv_ln_b, conv_w_pw2, conv_b_pw2,
              nsa_w_in, nsa_w_out, nsa_cmp_pe, nsa_cmp_w1, nsa_cmp_w2):

    def run(x, p, sample):
        B = x.shape[0]
        cmp_rows, sel_rows, win_rows, conv_rows = [], [], [], []
        for i in range(DEPTH):
            h = rms_norm(x, norm_g[i, 0])
            if i % N_MIXERS == 0:
                c = i // N_MIXERS
                st = state_conv[c] if sample else jnp.zeros((B, CONV_W - 1, D_CONV), x.dtype)
                m, st_new = conv_module(h, st, conv_w_pw1[c], conv_b_pw1[c], conv_w_dw[c], conv_b_dw[c],
                                        conv_ln_g[c], conv_ln_b[c], conv_w_pw2[c], conv_b_pw2[c])
                conv_rows.append(st_new)
            else:
                a = i // N_MIXERS
                if sample:
                    m, r_c, r_s, r_w = nsa_sample(h, cache_cmp[a], cache_sel[a], cache_win[a], page_table,
                                                  nsa_w_in[a], nsa_w_out[a], nsa_cmp_pe[a], nsa_cmp_w1[a], nsa_cmp_w2[a])
                else:
                    m, r_c, r_s, r_w = nsa_prompt(h, nsa_w_in[a], nsa_w_out[a], nsa_cmp_pe[a], nsa_cmp_w1[a], nsa_cmp_w2[a])
                cmp_rows.append(r_c)
                sel_rows.append(r_s)
                win_rows.append(r_w)
            x = x + rms_norm(m, norm_g[i, 1])
            f = squared_relu_mlp(rms_norm(x, norm_g[i, 2]), w_ff1[i], w_ff2[i])
            x = x + rms_norm(f, norm_g[i, 3])
            gate = jax.nn.sigmoid(x @ w_ple_gate[i] + b_ple_gate[i])
            x = x + gate * (p[i] @ w_ple[i])
        return x, jnp.stack(cmp_rows), jnp.stack(sel_rows), jnp.stack(win_rows), jnp.stack(conv_rows)

    y_prompt, cmp_p, sel_p, win_p, conv_p = run(x_prompt, p_prompt, False)
    y_sample, cmp_s, sel_s, win_s, conv_s = run(x_sample, p_sample, True)
    return (y_prompt, y_sample, cmp_p, cmp_s, sel_p, sel_s, win_p, win_s, conv_p, conv_s)


_drawn_inputs = setup_inputs


def setup_inputs(seed=0):
    import zlib

    import numpy as np

    out = dict(_drawn_inputs(seed))
    spreads = {}
    factors = {'b_ple_gate': 44.463,
     'conv_b_pw1': 5.367,
     'conv_b_dw': 2.891,
     'conv_ln_g': 9.341,
     'conv_ln_b': 19.726,
     'conv_b_pw2': 11.29}
    for name, (base, spread) in spreads.items():
        noise = np.random.default_rng([zlib.crc32(name.encode()), seed]).standard_normal(out[name].shape)
        drawn = base * np.exp(spread * noise) if base else spread * noise
        out[name] = jnp.asarray(drawn.astype(out[name].dtype))
    for name, factor in factors.items():
        out[name] = (out[name] * factor).astype(out[name].dtype)
    return out
```

```python
import numpy as np
import concourse.bass as bass
import concourse.mybir as mybir
from concourse.alu_op_type import AluOpType as ALU

F32 = mybir.dt.float32
I32 = mybir.dt.int32
ACT = mybir.ActivationFunctionType
AX = mybir.AxisListType

P = 128
D = 1024
SEQ = 512
NB = 8
DT = 8
NS = NB * DT
T = SEQ + NS
HT = T // 2
C = D // P
TAPS = 31
PAST = 1024
PAGES = 8
POOL = 80
KV = 4
REP = 4
HD = 64
FF = 4096
FC = FF // P
WIN = 512
EPS = 1e-6
NEG = -1e30
SCALE = HD ** -0.5
BLK = 4096
RING = 3
PT = SEQ // P
TT = PT + 1
EXT_P = SEQ + TAPS - 1
EXT_S = DT + TAPS - 1
EXT = EXT_P + NB * EXT_S
NCP = 32
NCS = 64

def columns(parts):
    at, n = {}, 0
    for name, width in parts:
        at[name] = (n, n + width)
        n += width
    return at, n

PAR, NPAR = columns([("norm_g", 64), ("b_ple", 16), ("b_pw1", 16), ("w_dw", 8 * TAPS), ("b_dw", 8), ("ln_g", 8),
                     ("ln_b", 8), ("b_pw2", 8), ("pe", 2 * 16)])
CON, NCON = columns([("ident", P), ("mean", P), ("swap", P), ("cos", T), ("sin", T), ("causal", P),
                     ("same_q", P), ("cmp_add", PT * NCP), ("cmp_mul", PT * NCP), ("new_add", NB * NS),
                     ("win_add", DT), ("block_no", 16), ("own_kv", 256), ("eps", 1)])

STAGES = [("pw1", 16, "AD" * 8), ("pw2", 8, "A" * 8), ("up0", FC, "A" * FC), ("down0", 8, "A" * 8),
          ("gate0", 8, "A" * 8), ("ple0", 8, "D" * 8),
          ("q", 8, "A" * 8), ("kv_cmp", 4, "A" * 4), ("k_rot", 4, "A" * 4), ("v_tok", TT, "A" * TT),
          ("gates", TT, "A" * TT), ("swap", 12, "D" * 12),
          ("out", 8, "A" * 8), ("up1", FC, "A" * FC), ("down1", 8, "A" * 8),
          ("gate1", 8, "A" * 8), ("ple1", 8, "D" * 8)]
FIRST, FREED = {}, []
_n = {"A": 0, "D": 0}
for _name, _count, _who in STAGES:
    FIRST[_name] = len(FREED)
    for _w in _who:
        _n[_w] += 1
        FREED.append((_w, _n[_w]))

def stage_blocks(stage, source, row, n, tiles):
    return [(source, row + i, BLK, FIRST[stage] + tiles * (i + 1)) for i in range(n)]

BLOCKS = (stage_blocks("pw1", "w", 0, 4, 4) + stage_blocks("pw2", "w", 4, 2, 4) + stage_blocks("up0", "w", 6, 8, 4)
          + stage_blocks("down0", "w", 14, 8, 1) + stage_blocks("gate0", "w", 22, 2, 4)
          + [("ple", 0, BLK // 2, FIRST["ple0"] + 8)]
          + stage_blocks("q", "w", 26, 2, 4) + stage_blocks("kv_cmp", "w", 28, 1, 4)
          + stage_blocks("k_rot", "w", 29, 1, 4) + stage_blocks("v_tok", "w", 30, 1, TT)
          + [("cmp_pages", b, BLK, b + 1) for b in range(NB)]
          + [blk for b in range(NB) for blk in (("sel_pages", b, BLK, b + 1), ("win", b, BLK // 2, b + 1))]
          + stage_blocks("out", "w", 31, 2, 4) + stage_blocks("up1", "w", 33, 8, 4)
          + stage_blocks("down1", "w", 41, 8, 1) + stage_blocks("gate1", "w", 24, 2, 4)
          + [("ple", 1, BLK // 2, FIRST["ple1"] + 8)])
B_OF = {"pw1": 0, "pw2": 4, "up0": 6, "down0": 14, "gate0": 22, "ple0": 24, "q": 25, "kv_cmp": 27, "k_rot": 28,
        "v_tok": 29, "cmp_pages": 30, "sel": 38, "out": 54, "up1": 56, "down1": 64, "gate1": 72, "ple1": 74}


def t_group(b, k):
    return 5 * b + k - (b > 0)


def place(i):
    n = i - B_OF["sel"]
    if 0 <= n < 2 * NB:
        b = n // 2
        return (BLK * (b % 2), b % 2) if n % 2 == 0 else (2 * BLK + BLK // 2 * (b % 2), 2 + b % 2)
    return BLK * (i % RING), i % RING


LAST_THERE, LOADED = [], []
_at, _holds = [0] * (RING + 1), {}
for _i, (_src, _, _n, _) in enumerate(BLOCKS):
    _lo, _s = place(_i)
    _halves = range(_lo // (BLK // 2), (_lo + (_n if _n < BLK and _src == "win" else BLK)) // (BLK // 2))
    LAST_THERE.append(sorted({_holds[_k] for _k in _halves if _k in _holds}))
    for _k in _halves:
        _holds[_k] = _i
    _at[_s] += 16 * (PAGES if _src.endswith("pages") else 1)
    LOADED.append(_at[_s])


def program(nc, ext, out):
    from contextlib import ExitStack
    with ExitStack() as ctx:
        def sb(name, shape, dt=F32):
            return ctx.enter_context(nc.sbuf_tensor(name, shape, dt))

        def sem(name):
            return ctx.enter_context(nc.semaphore(name))

        x = sb("x", [P, C, T])
        h = sb("h", [P, C, T])
        mix = sb("mix", [P, C, T])
        ring = sb("ring", [P, RING, BLK])
        sq = sb("sq", [P, 4, T])
        rstd = sb("rstd", [P, T])
        par = sb("par", [P, NPAR])
        con = sb("con", [P, NCON])
        ple_in = sb("ple_in", [P, 2, T])
        big = sb("big", [P, FC * T])
        hidden = big[:, :].rearrange("p (c t) -> p c t", t=T)
        conv_in = big[:, 0:C * EXT].rearrange("p (c t) -> p c t", t=EXT)
        y = big[:, C * EXT:C * EXT + C * T].rearrange("p (c t) -> p c t", t=T)
        sig = big[:, C * EXT + C * T:C * EXT + (C + 2) * T].rearrange("p (c t) -> p c t", t=T)
        at = 0
        q = big[:, at:at + C * T].rearrange("p (c t) -> p c t", t=T); at += C * T
        q_rot = big[:, at:at + C * T].rearrange("p (c t) -> p c t", t=T); at += C * T
        kv_cmp = big[:, at:at + 4 * T].rearrange("p (c t) -> p c t", t=T); at += 4 * T
        k_rot = big[:, at:at + 4 * T].rearrange("p (c t) -> p c t", t=T); at += 4 * T
        v_tok = big[:, at:at + TT * 512].rearrange("p (n f) -> p n f", f=512); at += TT * 512
        gates = sb("gates", [P, TT, 48])
        w_gates = sb("w_gates", [P, C, 48])
        rope_tmp = sq
        k_cmp_s = big[:, at:at + NB * 2 * NCS].rearrange("p (b g c) -> p b g c", b=NB, g=2); at += NB * 2 * NCS
        v_cmp_s = big[:, at:at + NB // 2 * 256].rearrange("p (b f) -> p b f", f=256)
        w1 = mix[:, :, :].rearrange("p c t -> p (c t)")[:, 0:BLK].rearrange("p (v j h) -> p v j h", v=2, j=16)
        w1_swapped = h[:, :, :].rearrange("p c t -> p (c t)")[:, 0:BLK].rearrange("p (v j h) -> p v j h", v=2, j=16)
        acc = mix[:, :, :].rearrange("p c t -> p (c t)")[:, 0:PT * D].rearrange("p (n f) -> p n f", f=D)
        attn_t = h
        sq_flat = sq[:, :, :].rearrange("p c t -> p (c t)")
        hid_s = sq_flat[:, 0:512].rearrange("p (u n) -> p u n", u=2)
        hid_p = sq_flat[:, 512:768].rearrange("p (v e g c) -> p v e g c", v=2, e=2, g=2)
        v_cmp_p = sq_flat[:, 1792:2304].rearrange("p (g f) -> p g f", g=2)
        pc_t_p = sq_flat[:, 0:512].rearrange("p (j t) -> p j t", j=4)
        pt_s = sq_flat[:, 0:1792]
        q_flat = q.rearrange("p c t -> p (c t)")
        pc = q_flat[:, 0:2560].rearrange("p (n c) -> p n c", n=5)
        pc_t_s = q_flat[:, 4096:4608].rearrange("p (j t) -> p j t", j=4)
        p_s = q_flat[:, 0:3328].rearrange("p (u n) -> p u n", u=2)
        p_p = q_flat[:, 0:2048].rearrange("p (u n) -> p u n", u=4)
        pt_p = q_flat[:, 2048:3072].rearrange("p (u n) -> p u n", u=2)
        kvc_flat = kv_cmp.rearrange("p c t -> p (c t)")
        qbd = kvc_flat[:, 0:1024].rearrange("p (b g e m) -> p b g e m", b=NB, g=2, e=2)
        imp = kvc_flat[:, 1024:1152].rearrange("p (b s) -> p b s", b=NB)
        drop = kvc_flat[:, 1152:1280].rearrange("p (b s) -> p b s", b=NB)
        eq = kvc_flat[:, 1280:1408].rearrange("p (b s) -> p b s", b=NB)
        acc_s = kvc_flat[:, 1408:1920].rearrange("p (u n) -> p u n", u=2)
        cmax = kvc_flat[:, 1920:1992]
        csum = kvc_flat[:, 1992:2064]
        stat_s = kvc_flat[:, 2064:2128].rearrange("p (b c) -> p b c", b=NB)
        least = kvc_flat[:, 2128:2144]
        nmax_p = kvc_flat[:, 2144:2152]
        f_p = kvc_flat[:, 2152:2160]
        sum_p = kvc_flat[:, 2160:2168]
        k_cmp_p = sb("k_cmp_p", [P, 2, NCP])
        w2 = sb("w2", [P, 2, HD])
        c_vec = sb("c_vec", [P, 2])
        gate_s = sb("gate_s", [P, NB, 3])
        pages = sb("pages", [1, NB * PAGES], I32)
        gate_rows = nc.dram_tensor("gate_rows", (NS, 48), F32, kind="Internal").ap()

        ps = ctx.enter_context(nc.psum_tensor("ps", [P, 8, 512], F32))
        STAT = ps[:, 6:8, 0:HT]

        ring_flat = ring[:, :, :].rearrange("p r n -> p (r n)")

        def block_at(i, lo, n):
            return ring_flat[:, place(i)[0] + lo:place(i)[0] + lo + n]

        def slot(t):
            return ps[:, 2 * (t % 3):2 * (t % 3) + 2, 0:HT]

        def halves(ap):
            return ap.rearrange("p (a t) -> p a t", a=2)

        def sample_rows(m):
            return conv_in[:, m, EXT_P:].rearrange("p (b t) -> p b t", t=EXT_S)

        def pcol(name, i):
            a = PAR[name][0] + i
            return par[:, a:a + 1]

        def tab(name):
            a, b = CON[name]
            return con[:, a:b]

        consts_in = sem("consts_in")
        x_in = sem("x_in")
        state_in = sem("state_in")
        ple_loaded = sem("ple_loaded")
        wg_in = sem("wg_in")
        block_in = [sem(f"block_in{i}") for i in range(RING + 1)]
        tile_done = sem("tile_done")
        act_freed = sem("act_freed")
        dve_freed = sem("dve_freed")
        freed = {"A": act_freed, "D": dve_freed}
        sq_ready = sem("sq_ready")
        sq_summed = sem("sq_summed")
        mean_ready = sem("mean_ready")
        std_ready = sem("std_ready")
        rstd_ready = sem("rstd_ready")
        h_ready = sem("h_ready")
        x_ready = sem("x_ready")
        sig_ready = sem("sig_ready")
        glu_done = sem("glu_done")
        pad_done = sem("pad_done")
        conv_done = sem("conv_done")
        centred = sem("centred")
        normed = sem("normed")
        silu_ready = sem("silu_ready")
        squared = sem("squared")
        dve_step = sem("dve_step")
        stored = sem("stored")
        rot_done = sem("rot_done")

        pages_in = sem("pages_in")
        w1_in = sem("w1_in")
        w1s_in = sem("w1s_in")
        kv_cmp_stored = sem("kv_cmp_stored")
        gate_moved = sem("gate_moved")
        win_stored = [sem("win_stored0"), sem("win_stored1")]
        c_mm, c_there = sem("c_mm"), sem("c_there")
        cmp_mm, hid_a, hid_ab, hid_ready = sem("cmp_mm"), sem("hid_a"), sem("hid_ab"), sem("hid_ready")
        w2_mm, w2_out = sem("w2_mm"), sem("w2_out")
        phid_mm, phid_ready = sem("phid_mm"), sem("phid_ready")
        phid_zero = sem("phid_zero")
        pw2_mm, pw2_out = sem("pw2_mm"), sem("pw2_out")
        vbd_zero = sem("vbd_zero")
        qbd_zero, qbd_ready = sem("qbd_zero"), sem("qbd_ready")
        sc_mm = sem("sc_mm")
        sc_sub, c_exp = sem("sc_sub"), sem("c_exp")
        pc_ready = sem("pc_ready")
        imp_mm, drop_ready = sem("imp_mm"), sem("drop_ready")
        ct_mm, ct_out = sem("ct_mm"), sem("ct_out")
        co_mm, co_read = sem("co_mm"), sem("co_read")
        s_mm, s_read = sem("s_mm"), sem("s_read")
        s_win = sem("s_win")
        s_max, s_exp = sem("s_max"), sem("s_exp")
        t_mm, t_out, t_fin = sem("t_mm"), sem("t_out"), sem("t_fin")
        o_mm, o_read, acc_ready = sem("o_mm"), sem("o_read"), sem("acc_ready")
        p_mm, p_max, p_exp = sem("p_mm"), sem("p_max"), sem("p_exp")
        pt_mm, pt_out = sem("pt_mm"), sem("pt_out")
        po_mm, po_read = sem("po_mm"), sem("po_read")
        ft_mm, ft_out = sem("ft_mm"), sem("ft_out")
        pe_ple1 = sem("pe_ple1")

        block = ctx.enter_context(nc.Block())

        @block.sync
        def _(sp):
            sp.dma_start(con[:, :], ext["con"]).then_inc(consts_in, 16)
            sp.dma_start(par[:, :], ext["par"]).then_inc(consts_in, 16)
            sp.dma_start(x[:, :, :], ext["x"]).then_inc(x_in, 16)
            sp.dma_start(pages[:, :], ext["pages"]).then_inc(pages_in, 16)
            sp.wait_ge(pages_in, 16)
            done = {"cmp_pages": (hid_ab, 2), "sel_pages": (o_mm, 1), "win": (o_mm, 1)}
            for i, (src, row, n, _) in enumerate(BLOCKS):
                for last in LAST_THERE[i]:
                    last_src, _, _, v = BLOCKS[last]
                    s_done, per = done.get(last_src, (tile_done, 1))
                    sp.wait_ge(s_done, v * per)
                    if last_src == "win":
                        sp.wait_ge(win_stored[(v - 1) % 2], 16 * ((v + 1) // 2))
                lo, k = place(i)
                to = ring_flat[:, lo:lo + n]
                if src.endswith("pages"):
                    for j in range(PAGES):
                        page = sp.value_load(pages[0:1, row * PAGES + j:row * PAGES + j + 1], min_val=0, max_val=POOL - 1)
                        sp.dma_start(to[:, j * 512:(j + 1) * 512],
                                     ext[src][bass.ds(page, 1), :, :].rearrange("o p n -> (o p) n")).then_inc(block_in[k], 16)
                else:
                    sp.dma_start(to, ext[src][row]).then_inc(block_in[k], 16)
                if i == 0:
                    for m in range(C):
                        sp.dma_start(sample_rows(m)[:, :, 0:TAPS - 1], ext["state"][:, m]).then_inc(state_in, 16)
                    sp.dma_start(ple_in[:, :, :], ext["p"][0]).then_inc(ple_loaded, 16)
                    sp.dma_start(w_gates[:, :, :], ext["w_gates"]).then_inc(wg_in, 16)
                    sp.dma_start(w2[:, :, :], ext["w2"]).then_inc(wg_in, 16)
                if i == 5:
                    sp.wait_ge(glu_done, C)
                    sp.dma_start(out["conv_p"], conv_in[:, :, SEQ:EXT_P]).then_inc(stored, 16)
                    for m in range(C):
                        sp.dma_start(out["conv_s"][:, m], sample_rows(m)[:, :, DT:]).then_inc(stored, 16)
                if i == B_OF["kv_cmp"]:
                    sp.wait_ge(tile_done, FIRST["ple0"] + 8)
                    sp.dma_start(ple_in[:, :, :], ext["p"][1]).then_inc(ple_loaded, 16)
                if i == B_OF["cmp_pages"]:
                    sp.wait_ge(x_ready, 3 * C)
                    sp.dma_start(w1, ext["w1"]).then_inc(w1_in, 16)
                    sp.wait_ge(tile_done, FIRST["gates"] + TT)
                    sp.dma_start(w1_swapped, ext["w1s"]).then_inc(w1s_in, 16)
                    sp.wait_ge(act_freed, FREED[FIRST["gates"] + TT - 1][1])
                    sp.dma_start(out["kv_cmp"], kv_cmp[:, :, :]).then_inc(kv_cmp_stored, 16)
                    sp.dma_start(out["v_tok"], v_tok[:, 0:PT, :]).then_inc(stored, 16)
                    sp.dma_start(out["v_tok_s"], v_tok[0:NS, PT, :]).then_inc(stored, 16)
                    sp.wait_ge(rot_done, 12)
                    sp.dma_start(out["k_rot"], k_rot[:, :, :]).then_inc(stored, 16)
            sp.wait_ge(kv_cmp_stored, 16)
            sp.wait_ge(win_stored[0], 16 * (NB // 2))
            sp.wait_ge(win_stored[1], 16 * (NB // 2))
            for m in range(C):
                sp.wait_ge(x_ready, 5 * C + m + 1)
                sp.dma_start(out["y"][:, m], x[:, m, :]).then_inc(stored, 16)
            sp.wait_ge(stored, 16 * (12 + C))

        @block.gpsimd
        def _(pool):
            nc.gpsimd.memset(conv_in[:, :, 0:TAPS - 1], 0.0).then_inc(pad_done, 1)
            def square_hidden(layer):
                for m in range(FC):
                    pool.wait_ge(act_freed, FREED[FIRST[f"up{layer}"] + m][1])
                    nc.gpsimd.tensor_tensor(hidden[:, m, :], hidden[:, m, :], hidden[:, m, :],
                                            ALU.mult).then_inc(squared, 1)

            square_hidden(0)
            pool.wait_ge(act_freed, FREED[FIRST["gates"] + TT - 1][1])
            pool.dma_start(gate_rows, gates[0:NS, PT, :]).then_inc(gate_moved, 16)
            pool.wait_ge(gate_moved, 16)
            for n in range(KV * REP):
                g, r = n // REP, n % REP
                at = 3 * (2 * (g // 2 * REP + r) + g % 2)
                pool.dma_start(gate_s[n * DT:(n + 1) * DT, :, :],
                               gate_rows.rearrange("(b i) c -> i b c", i=DT)[:, :, at:at + 3]).then_inc(gate_moved, 16)
            pool.wait_ge(rot_done, 12)
            pool.wait_ge(dve_freed, FREED[FIRST["swap"] + 11][1])
            nc.gpsimd.memset(hid_p[:, :, :, :, NCP - 1:NCP], 0.0).then_inc(phid_zero, 1)
            nc.gpsimd.memset(v_cmp_p, 0.0).then_inc(vbd_zero, 1)
            pool.wait_ge(kv_cmp_stored, 16)
            pool.wait_ge(phid_mm, 2)
            nc.gpsimd.memset(qbd, 0.0).then_inc(qbd_zero, 1)
            for b in range(NB):
                i = B_OF["sel"] + 2 * b + 1
                lo, k = place(i)
                pool.wait_ge(block_in[k], LOADED[i])
                pool.dma_start(out["win"][b], ring_flat[:, lo:lo + BLK // 2]).then_inc(win_stored[b % 2], 16)
            square_hidden(1)

        @block.tensor
        def _(pe):
            def slot_free(t):
                if t >= 3:
                    who, n = FREED[t - 3]
                    pe.wait_ge(freed[who], n)

            def block_there(i):
                pe.wait_ge(block_in[place(i)[1]], LOADED[i])

            def dense(stage, blk, per_block, nk, rhs, k_wait=None):
                n = dict((s[0], s[1]) for s in STAGES)[stage]
                for m in range(n):
                    b = blk + m // per_block
                    if m % per_block == 0:
                        block_there(b)
                    w = ring[:, b % RING, 0:nk * per_block * P].rearrange("p (k c) -> p k c", k=nk)
                    t = FIRST[stage] + m
                    slot_free(t)
                    for a in range(2):
                        for k in range(nk):
                            if k_wait and m == 0 and a == 0:
                                k_wait(k)
                            last = nc.tensor.matmul(slot(t)[:, a, :], w[:, k, (m % per_block) * P:(m % per_block + 1) * P],
                                                    rhs(k)[:, a * HT:(a + 1) * HT], start=k == 0, stop=k == nk - 1)
                    last.then_inc(tile_done, 1)

            def stats(n, extra=None):
                for m in range(C):
                    pe.wait_ge(sq_ready, C * n + m + 1)
                    if m == 0 and n >= 1:
                        pe.wait_ge(rstd_ready, n)
                    if m == 0 and n == 1:
                        pe.wait_ge(centred, C)
                    for a in range(2):
                        last = nc.tensor.matmul(STAT[:, a, :], tab("mean"), sq[:, (C * n + m) % 4, a * HT:(a + 1) * HT],
                                                start=m == 0, stop=m == C - 1)
                    last.then_inc(sq_summed, 1)

            def on(s, base):
                return lambda k: pe.wait_ge(s, base + k + 1)

            pe.wait_ge(consts_in, 32)
            stats(0)
            dense("pw1", B_OF["pw1"], 4, C, lambda k: h[:, k, :], on(h_ready, 0))
            pe.wait_ge(rstd_ready, 1)
            for m in range(C):
                pe.wait_ge(conv_done, m + 1)
                for a in range(2):
                    last = nc.tensor.matmul(STAT[:, a, :], tab("mean"), y[:, m, a * HT:(a + 1) * HT],
                                            start=m == 0, stop=m == C - 1)
            last.then_inc(mean_ready, 1)
            stats(1)
            dense("pw2", B_OF["pw2"], 4, C, lambda k: h[:, k, :], on(silu_ready, 0))
            stats(2)
            stats(3)
            dense("up0", B_OF["up0"], 4, C, lambda k: h[:, k, :], on(h_ready, C))
            dense("down0", B_OF["down0"], 1, FC, lambda k: hidden[:, k, :], on(squared, 0))
            stats(4)
            dense("gate0", B_OF["gate0"], 4, C, lambda k: x[:, k, :], on(x_ready, C))
            pe.wait_ge(ple_loaded, 16)
            dense("ple0", B_OF["ple0"], 8, 2, lambda k: ple_in[:, k, :])
            stats(5)
            dense("q", B_OF["q"], 4, C, lambda k: h[:, k, :], on(h_ready, 2 * C))
            dense("kv_cmp", B_OF["kv_cmp"], 4, C, lambda k: h[:, k, :])
            dense("k_rot", B_OF["k_rot"], 4, C, lambda k: h[:, k, :])
            b = B_OF["v_tok"]
            block_there(b)
            pe.wait_ge(wg_in, 32)
            for stage, w, n in (("v_tok", ring[:, b % RING, :].rearrange("p (k c) -> p k c", k=C), 512),
                                ("gates", w_gates, 48)):
                for i in range(TT):
                    t = FIRST[stage] + i
                    rows = P if i < PT else NS
                    slot_free(t)
                    for k in range(C):
                        last = nc.tensor.matmul(ps[0:rows, 2 * (t % 3), 0:n], h[:, k, i * P:i * P + rows], w[:, k, :],
                                                start=k == 0, stop=k == C - 1)
                    last.then_inc(tile_done, 1)
            for i in range(12):
                t = FIRST["swap"] + i
                src = q[:, i, :] if i < 8 else k_rot[:, i - 8, :]
                slot_free(t)
                pe.wait_ge(act_freed, FREED[FIRST["q"] + i if i < 8 else FIRST["k_rot"] + i - 8][1])
                for a in range(2):
                    last = nc.tensor.matmul(slot(t)[:, a, :], tab("swap"), src[:, a * HT:(a + 1) * HT],
                                            start=True, stop=True)
                last.then_inc(tile_done, 1)

            pe.wait_ge(w1_in, 16)
            lo, _ = PAR["pe"]
            for v in range(2):
                for j in range(16):
                    last = nc.tensor.matmul(ps[:, 7, v:v + 1], w1[:, v, j, :], par[:, lo + 16 * v + j:lo + 16 * v + j + 1],
                                            start=j == 0, stop=j == 15)
                last.then_inc(c_mm, 1)
            pe.wait_ge(w1s_in, 16)
            pe.wait_ge(c_there, 1)
            for v in range(2):
                for e in range(2):
                    for s in range(32):
                        part = slice(64 * e, 64 * e + 64)
                        w = w1 if s % 2 == e else w1_swapped
                        rhs = kv_cmp[part, 2 * v:2 * v + 2, s:s + 16 * (NCP - 2) + 1:16]
                        last = nc.tensor.matmul(ps[:, 6 + e, 128 * v:128 * v + 62].rearrange("p (g c) -> p g c", g=2),
                                                w[part, v, s // 2, :], rhs, start=s == 0, stop=s == 31)
                last.then_inc(phid_mm, 1)
            pe.wait_ge(phid_ready, 2)
            for e in range(2):
                nc.tensor.matmul(ps[64 * e:64 * e + 64, 7, 0:64].rearrange("p (g c) -> p g c", g=2), w2[:, 0, :],
                                 hid_p[:, 0, e, :, :], start=True, stop=True)
            for g in range(2):
                for k in range(4):
                    last = nc.tensor.matmul(ps[32 * k:32 * k + 32, 7, 64 + 64 * g:128 + 64 * g],
                                            hid_p[:, 1, k % 2, g, :], w2[:, 1, :], start=True, stop=True)
            last.then_inc(pw2_mm, 1)

            def compress_out(u):
                b, v = u // 2, u % 2
                pe.wait_ge(hid_ready, u + 1)
                if u == 1:
                    pe.wait_ge(pw2_out, 2)
                if u >= 2:
                    pe.wait_ge(w2_out, u - 1)
                hid = hid_s[:, u % 2, :].rearrange("p (c g) -> p g c", g=KV)
                if v == 0:
                    for e in range(2):
                        last = nc.tensor.matmul(ps[64 * e:64 * e + 64, 6, 0:128].rearrange("p (g c) -> p g c", g=2),
                                                w2[:, 0, :], hid[:, e:e + 3:2, :], start=True, stop=True)
                else:
                    lo = 64 * (b % 2)
                    for g in range(KV):
                        last = nc.tensor.matmul(ps[lo:lo + 64, 7, 64 * g:64 * g + 64], hid[:, g, :], w2[:, 1, :],
                                                start=True, stop=True)
                last.then_inc(w2_mm, 1)

            slot_free(FIRST["out"] + 0)
            slot_free(FIRST["out"] + 1)
            slot_free(FIRST["out"] + 2)
            for u in range(2 * NB):
                b, v = u // 2, u % 2
                i = B_OF["cmp_pages"] + b
                block_there(i)
                if u >= 3:
                    pe.wait_ge(hid_ab, u - 2)
                for half in range(2):
                    for j in range(8):
                        rhs = ring[:, i % RING, :].rearrange("p (a n) -> p a n", a=PAGES)[:, :, 256 * v + 32 * j:256 * v + 32 * j + 32]
                        last = nc.tensor.matmul(ps[:, 2 * (u % 3) + half, 0:256], w1[:, v, 8 * half + j, :], rhs,
                                                start=j == 0, stop=j == 7)
                last.then_inc(cmp_mm, 1)
                if u >= 1:
                    compress_out(u - 1)
            compress_out(2 * NB - 1)

            pe.wait_ge(w2_out, 2 * NB - 1)
            pe.wait_ge(hid_ab, 2 * NB)
            pe.wait_ge(qbd_ready, 1)
            for b in range(NB):
                for g in range(2):
                    last = nc.tensor.matmul(ps[64 * g:64 * g + 64, 4, 64 * b:64 * b + 64],
                                            qbd[:, b, g, :, :].rearrange("p e m -> p (e m)"), k_cmp_s[:, b, g, :],
                                            start=True, stop=True)
            last.then_inc(sc_mm, 1)
            for n in range(PT):
                for c in range(C):
                    for e in range(2):
                        part = slice(64 * e, 64 * e + 64)
                        at = 256 * (n % 2) + NCP * c
                        last = nc.tensor.matmul(ps[:, 2 * (n // 2) + e, at:at + NCP], q[part, c, n * P:(n + 1) * P],
                                                k_cmp_p[part, c // 4, :], start=True, stop=True)
                last.then_inc(sc_mm, 1)
            pe.wait_ge(pc_ready, 1)
            pe.wait_ge(w2_out, 2 * NB)
            nc.tensor.matmul(ps[:, 5, :], tab("same_q"), pc[:, 0, :], start=True, stop=True).then_inc(imp_mm, 1)
            for j in range(4):
                last = nc.tensor.transpose(ps[:, 6, 128 * j:128 * j + 128], pc[:, 0, 128 * j:128 * j + 128], tab("ident"))
            last.then_inc(ct_mm, 1)
            for n in range(PT):
                pe.wait_ge(pc_ready, n + 2)
                pe.wait_ge(sc_sub, n + 2)
                if n == 0:
                    pe.wait_ge(drop_ready, 1)
                pe.wait_ge(ct_out, n + 1)
                if n >= 1:
                    pe.wait_ge(co_read, n)
                for j in range(4):
                    last = nc.tensor.transpose(ps[:, 4 + n % 2, 128 * j:128 * j + 128], pc[:, n + 1, 128 * j:128 * j + 128],
                                               tab("ident"))
                last.then_inc(ct_mm, 1)
                pe.wait_ge(ct_out, n + 2)
                for j in range(4):
                    last = nc.tensor.matmul(ps[:, 6 + j // 2, 256 * (j % 2):256 * (j % 2) + 256], pc_t_p[:, j, :],
                                            v_cmp_p[:, j // 2, :], start=True, stop=True)
                last.then_inc(co_mm, 1)

            def scores_s(b):
                i = B_OF["sel"] + 2 * b
                block_there(i)
                block_there(i + 1)
                if b >= 1:
                    pe.wait_ge(s_read, b)
                    pe.wait_ge(s_win, b)
                sel = block_at(i, 0, BLK).rearrange("p (a n) -> p a n", a=PAGES)
                win = block_at(i + 1, 0, 1024).rearrange("p (g n) -> p g n", g=2)
                for g in range(2):
                    part = slice(64 * g, 64 * g + 64)
                    qq = qbd[:, b, g, :, :].rearrange("p e m -> p (e m)")
                    for a in range(2):
                        nc.tensor.matmul(ps[part, a, :], qq, sel[:, 4 * a:4 * a + 4, P * g:P * g + P], start=True, stop=True)
                    nc.tensor.matmul(ps[part, 2, :], qq, win[:, g, :], start=True, stop=True)
                    nc.tensor.matmul(ps[part, 3, 0:NS], qq, k_rot[:, g, SEQ:T], start=True, stop=True)
                    last = nc.tensor.matmul(ps[part, 3, NS:2 * NS], qq, k_rot[:, 2 + g, SEQ:T], start=True, stop=True)
                last.then_inc(s_mm, 1)

            def t_slot(n):
                if n >= 2:
                    b, k = [(b, k) for b in range(NB + 1) for k in range(5) if (b, k) != (0, 4)][n - 2]
                    if k == 4:
                        pe.wait_ge(t_fin, b)
                    else:
                        pe.wait_ge(t_out, 4 * b + k + 1)
                return ps[:, 4 + n % 2, :]

            def finish_s(b, n):
                to = t_slot(n)
                pe.wait_ge(acc_ready, b + 1)
                for g in range(2):
                    last = nc.tensor.transpose(to[:, 128 * g:128 * g + 128], acc_s[:, b % 2, 128 * g:128 * g + 128], tab("ident"))
                last.then_inc(t_mm, 1)

            pe.wait_ge(co_read, PT)
            pe.wait_ge(qbd_ready, 2)
            pe.wait_ge(rot_done, 12)
            scores_s(0)
            for b in range(NB):
                if b + 1 < NB:
                    scores_s(b + 1)
                i = B_OF["sel"] + 2 * b
                sel = block_at(i, 0, BLK).rearrange("p (a n) -> p a n", a=PAGES)[:, :, 256:512]
                win = block_at(i + 1, 1024, 1024).rearrange("p (a n) -> p a n", a=4)
                pp = p_s[:, b % 2, :]
                pe.wait_ge(s_exp, b + 1)
                for k, tiles in enumerate(([0, 128, 256, 384], [512, 640, 768, 896], [1088, 1216, 1344, 1472], [1024, 1600])):
                    to = t_slot(t_group(b, k))
                    w = P if k < 3 else NS
                    for j, at in enumerate(tiles):
                        last = nc.tensor.transpose(to[0:w, 128 * j:128 * j + 128], pp[:, at:at + w], tab("ident"))
                    last.then_inc(t_mm, 1)
                if b >= 1:
                    finish_s(b - 1, t_group(b, 4))
                if b >= 1:
                    pe.wait_ge(o_read, b)
                pe.wait_ge(t_out, 4 * b + 4)
                for j in range(8):
                    nc.tensor.matmul(ps[:, 6, 0:256], pt_s[:, 128 * j:128 * j + 128], sel[:, j, :], start=j == 0, stop=False)
                nc.tensor.matmul(ps[:, 6, 0:256], pt_s[0:NS, 1536:1664], v_tok[0:NS, PT, 0:256], start=False, stop=True)
                for j in range(4):
                    nc.tensor.matmul(ps[:, 6, 256:512], pt_s[:, 1024 + 128 * j:1152 + 128 * j], win[:, j, :],
                                     start=j == 0, stop=False)
                nc.tensor.matmul(ps[:, 6, 256:512], pt_s[0:NS, 1664:1792], v_tok[0:NS, PT, 256:512], start=False, stop=True)
                half = slice(64 * (b % 2), 64 * (b % 2) + 64)
                nc.tensor.matmul(ps[:, 7, 0:256], pc_t_s[half, b // 2, :], v_cmp_s[half, b // 2, :],
                                 start=True, stop=True).then_inc(o_mm, 1)
            finish_s(NB - 1, t_group(NB, 0))

            items = [(n, c, e, r) for n in range(PT) for c in range(C) for e in range(2) for r in range(2)]

            def p_scores(i):
                n, c, e, r = items[i]
                if i >= 4:
                    pe.wait_ge(p_exp, i - 3)
                part = slice(64 * e, 64 * e + 64)
                nc.tensor.matmul(ps[:, i % 4, 0:(n + 1) * P], q_rot[part, c, n * P:(n + 1) * P],
                                 k_rot[part, 2 * r + c // 4, 0:(n + 1) * P], start=True, stop=True).then_inc(p_mm, 1)

            def p_transpose(i):
                n = items[i][0]
                pe.wait_ge(p_exp, i + 1)
                if i >= 2:
                    pe.wait_ge(pt_out, i - 1)
                for j in range(n + 1):
                    last = nc.tensor.transpose(ps[:, 4 + i % 2, 128 * j:128 * j + 128], p_p[:, i % 4, 128 * j:128 * j + 128],
                                               tab("ident"))
                last.then_inc(pt_mm, 1)

            def p_out(i):
                n, c, e, r = items[i]
                pe.wait_ge(pt_out, i + 1)
                if i >= 2:
                    pe.wait_ge(po_read, i - 1)
                at = 256 * r + 64 * (2 * (c // 4) + e)
                for j in range(n + 1):
                    last = nc.tensor.matmul(ps[:, 6 + i % 2, 0:HD], pt_p[:, i % 2, 128 * j:128 * j + 128],
                                            v_tok[:, j, at:at + HD], start=j == 0, stop=j == n)
                last.then_inc(po_mm, 1)

            pe.wait_ge(t_fin, NB)
            N = len(items)
            p_scores(0)
            p_scores(1)
            for i in range(N):
                if i + 2 < N:
                    p_scores(i + 2)
                p_transpose(i)
                if i >= 1:
                    p_out(i - 1)
            p_out(N - 1)
            for n in range(PT):
                for k in range(2):
                    i = 2 * n + k
                    if n == 0 and k == 0:
                        pe.wait_ge(po_read, N)
                    if i >= 2:
                        pe.wait_ge(ft_out, i - 1)
                    for c in range(4):
                        last = nc.tensor.transpose(ps[:, 4 + i % 2, 128 * c:128 * c + 128],
                                                   acc[:, n, 512 * k + 128 * c:512 * k + 128 * c + 128], tab("ident"))
                    last.then_inc(ft_mm, 1)

            pe.wait_ge(ft_out, 2 * PT)
            dense("out", B_OF["out"], 4, C, lambda k: attn_t[:, k, :])
            stats(6)
            stats(7)
            dense("up1", B_OF["up1"], 4, C, lambda k: h[:, k, :], on(h_ready, 3 * C))
            dense("down1", B_OF["down1"], 1, FC, lambda k: hidden[:, k, :], on(squared, FC))
            stats(8)
            dense("gate1", B_OF["gate1"], 4, C, lambda k: x[:, k, :], on(x_ready, 4 * C))
            pe.wait_ge(ple_loaded, 32)
            dense("ple1", B_OF["ple1"], 8, 2, lambda k: ple_in[:, k, :])

        @block.scalar
        def _(act):
            def tile(stage, m):
                t = FIRST[stage] + m
                act.wait_ge(tile_done, t + 1)
                return slot(t)

            def square(n, m, src):
                i = C * n + m
                if i >= 4:
                    act.wait_ge(sq_summed, i - 3)
                dst = sq[:, i % 4, :]
                if len(src.shape) == 3:
                    dst = halves(dst)
                nc.scalar.activation(dst, src, ACT.Square).then_inc(sq_ready, 1)

            def std(n):
                act.wait_ge(sq_summed, C * (n + 1))
                nc.scalar.activation(halves(rstd[:, :]), STAT, ACT.Sqrt, bias=tab("eps")).then_inc(std_ready, 1)

            def square_x(n, update):
                for m in range(C):
                    act.wait_ge(x_ready, C * update + m + 1)
                    square(n, m, x[:, m, :])
                std(n)

            def to_mix(stage, n, bias=None):
                for m in range(C):
                    p = tile(stage, m)
                    if bias is None:
                        nc.scalar.activation(halves(mix[:, m, :]), p, ACT.Copy).then_inc(act_freed, 1)
                    else:
                        nc.scalar.activation(halves(mix[:, m, :]), p, ACT.Identity, bias=pcol(bias, m)).then_inc(act_freed, 1)
                    act.wait_ge(act_freed, FREED[FIRST[stage] + m][1])
                    square(n, m, mix[:, m, :])
                std(n)

            def relu(layer):
                for m in range(FC):
                    p = tile(f"up{layer}", m)
                    nc.scalar.activation(halves(hidden[:, m, :]), p, ACT.Relu).then_inc(act_freed, 1)

            def gate(layer):
                for m in range(C):
                    p = tile(f"gate{layer}", m)
                    nc.scalar.activation(halves(mix[:, m, :]), p, ACT.Sigmoid,
                                         bias=pcol("b_ple", C * layer + m)).then_inc(act_freed, 1)

            act.wait_ge(consts_in, 32)
            act.wait_ge(x_in, 16)
            for m in range(C):
                square(0, m, x[:, m, :])
            std(0)
            for m in range(C):
                p = tile("pw1", 2 * m)
                if m >= 2:
                    act.wait_ge(glu_done, m - 1)
                nc.scalar.activation(halves(sig[:, m % 2, :]), p, ACT.Sigmoid,
                                     bias=pcol("b_pw1", 2 * m)).then_inc(act_freed, 1)
            for m in range(C):
                act.wait_ge(centred, m + 1)
                square(1, m, y[:, m, :])
            std(1)
            for m in range(C):
                act.wait_ge(normed, m + 1)
                nc.scalar.activation(h[:, m, :], y[:, m, :], ACT.Silu, scale=pcol("ln_g", m),
                                     bias=pcol("ln_b", m)).then_inc(silu_ready, 1)
            to_mix("pw2", 2, "b_pw2")
            square_x(3, 0)
            relu(0)
            to_mix("down0", 4)
            gate(0)
            square_x(5, 2)
            for stage, dst in (("q", q), ("kv_cmp", kv_cmp), ("k_rot", k_rot)):
                for m in range(C if stage == "q" else 4):
                    p = tile(stage, m)
                    nc.scalar.activation(halves(dst[:, m, :]), p, ACT.Copy,
                                         scale=SCALE if stage == "q" else 1.0).then_inc(act_freed, 1)
            for i in range(TT):
                rows = P if i < PT else NS
                t = FIRST["v_tok"] + i
                act.wait_ge(tile_done, t + 1)
                nc.scalar.activation(v_tok[0:rows, i, :], ps[0:rows, 2 * (t % 3), :], ACT.Copy).then_inc(act_freed, 1)
            for i in range(TT):
                rows = P if i < PT else NS
                t = FIRST["gates"] + i
                act.wait_ge(tile_done, t + 1)
                nc.scalar.activation(gates[0:rows, i, :], ps[0:rows, 2 * (t % 3), 0:48], ACT.Sigmoid).then_inc(act_freed, 1)

            act.wait_ge(c_mm, 2)
            nc.scalar.activation(c_vec[:, :], ps[:, 7, 0:2], ACT.Copy).then_inc(c_there, 1)
            act.wait_ge(c_there, 1)
            act.wait_ge(phid_zero, 1)
            act.wait_ge(phid_mm, 2)
            for v in range(2):
                nc.scalar.activation(hid_p[:, v, :, :, 0:NCP - 1],
                                     ps[:, 6:8, 128 * v:128 * v + 62].rearrange("p e (g c) -> p e g c", g=2),
                                     ACT.Silu, bias=c_vec[:, v:v + 1]).then_inc(phid_ready, 1)
            act.wait_ge(pw2_mm, 1)
            nc.scalar.activation(k_cmp_p[:, :, :], ps[:, 7, 0:64].rearrange("p (g c) -> p g c", g=2),
                                 ACT.Copy).then_inc(pw2_out, 1)
            act.wait_ge(vbd_zero, 1)
            for k in range(4):
                last = nc.scalar.activation(v_cmp_p[32 * k:32 * k + 32, :, 64 * k:64 * k + 64],
                                            ps[32 * k:32 * k + 32, 7, 64:192].rearrange("p (g f) -> p g f", g=2), ACT.Copy)
            last.then_inc(pw2_out, 1)
            act.wait_ge(rot_done, 12)

            def hid_silu(u):
                act.wait_ge(hid_ab, u + 1)
                nc.scalar.activation(hid_s[:, u % 2, :], hid_s[:, u % 2, :], ACT.Silu).then_inc(hid_ready, 1)

            for u in range(2 * NB):
                act.wait_ge(cmp_mm, u + 1)
                if u >= 2:
                    act.wait_ge(w2_mm, u - 1)
                nc.scalar.activation(hid_s[:, u % 2, :], ps[:, 2 * (u % 3), 0:256], ACT.Identity,
                                     bias=c_vec[:, u % 2:u % 2 + 1]).then_inc(hid_a, 1)
                hid_silu(u)

            for n in range(5):
                act.wait_ge(sc_sub, n + 1)
                nc.scalar.activation(pc[:, n, :], pc[:, n, :], ACT.Exp).then_inc(c_exp, 1)
            act.wait_ge(ct_mm, 1)
            nc.scalar.activation(pc_t_s, ps[:, 6, :].rearrange("p (j t) -> p j t", j=4), ACT.Copy).then_inc(ct_out, 1)
            act.wait_ge(w2_mm, 2 * NB)
            for n in range(PT):
                act.wait_ge(ct_mm, n + 2)
                if n >= 1:
                    act.wait_ge(co_mm, n)
                nc.scalar.activation(pc_t_p, ps[:, 4 + n % 2, :].rearrange("p (j t) -> p j t", j=4),
                                     ACT.Copy).then_inc(ct_out, 1)

            def window_out(b):
                act.wait_ge(s_mm, b + 1)
                if b == 0:
                    act.wait_ge(co_mm, PT)
                if b >= 2:
                    act.wait_ge(t_mm, t_group(b - 2, 3) + 1)
                nc.scalar.activation(p_s[:, b % 2, 1088:1600], ps[:, 2, :], ACT.Copy).then_inc(s_win, 1)

            act.wait_ge(co_mm, PT)
            window_out(0)
            for b in range(NB):
                pp = p_s[:, b % 2, :]
                act.wait_ge(s_max, 2 * b + 1)
                nc.scalar.activation(pp[:, 0:1088], pp[:, 0:1088], ACT.Exp, bias=stat_s[:, b, 0:1],
                                     accum_out=stat_s[:, b, 2:3])
                act.wait_ge(s_max, 2 * b + 2)
                nc.scalar.activation(pp[:, 1088:1664], pp[:, 1088:1664], ACT.Exp, bias=stat_s[:, b, 1:2],
                                     accum_out=stat_s[:, b, 3:4]).then_inc(s_exp, 1)
                if b + 1 < NB:
                    window_out(b + 1)
                for k in range(4):
                    act.wait_ge(t_mm, t_group(b, k) + 1)
                    if k == 0 and b >= 1:
                        act.wait_ge(o_mm, b)
                    w, n = (P, 512) if k < 3 else (NS, 256)
                    nc.scalar.activation(pt_s[0:w, 512 * k:512 * k + n], ps[0:w, 4 + t_group(b, k) % 2, 0:n],
                                         ACT.Copy).then_inc(t_out, 1)

            items = [(n, c, e, r) for n in range(PT) for c in range(C) for e in range(2) for r in range(2)]

            def p_move(i):
                n = items[i][0]
                act.wait_ge(pt_mm, i + 1)
                if i >= 2:
                    act.wait_ge(po_mm, i - 1)
                nc.scalar.activation(pt_p[:, i % 2, 0:(n + 1) * P], ps[:, 4 + i % 2, 0:(n + 1) * P],
                                     ACT.Copy).then_inc(pt_out, 1)

            act.wait_ge(t_mm, 5 * NB)
            for i, (n, c, e, r) in enumerate(items):
                act.wait_ge(p_max, i + 1)
                if i >= 4:
                    act.wait_ge(pt_mm, i - 3)
                    act.wait_ge(po_read, i - 3)
                nc.scalar.activation(p_p[:, i % 4, 0:(n + 1) * P], ps[:, i % 4, 0:(n + 1) * P], ACT.Exp,
                                     bias=nmax_p[:, i % 8:i % 8 + 1], accum_out=sum_p[:, i % 8:i % 8 + 1]).then_inc(p_exp, 1)
                if i >= 1:
                    p_move(i - 1)
            p_move(len(items) - 1)
            for i in range(2 * PT):
                n, k = i // 2, i % 2
                act.wait_ge(ft_mm, i + 1)
                nc.scalar.activation(attn_t[:, 4 * k:4 * k + 4, n * P:(n + 1) * P],
                                     ps[:, 4 + i % 2, :].rearrange("p (c t) -> p c t", c=4), ACT.Copy).then_inc(ft_out, 1)

            to_mix("out", 6)
            square_x(7, 3)
            relu(1)
            to_mix("down1", 8)
            gate(1)

        @block.vector
        def _(dve):
            steps = [0]

            def step(ins):
                steps[0] += 1
                ins.then_inc(dve_step, 1)
                return steps[0]

            def after(n):
                dve.wait_ge(dve_step, n)

            def get_rstd(n):
                dve.wait_ge(std_ready, n + 1)
                nc.vector.reciprocal(rstd[:, :], rstd[:, :]).then_inc(rstd_ready, 1)
                dve.wait_ge(rstd_ready, n + 1)

            def pre_norm(n, g, last_reader):
                get_rstd(n)
                if last_reader is not None:
                    dve.wait_ge(tile_done, last_reader)
                for m in range(C):
                    nc.vector.scalar_tensor_tensor(h[:, m, :], x[:, m, :], pcol("norm_g", C * g + m), rstd[:, :],
                                                   ALU.mult, ALU.mult).then_inc(h_ready, 1)

            def post_norm(n, g):
                get_rstd(n)
                done = []
                for m in range(C + 1):
                    if m < C:
                        done.append(step(nc.vector.scalar_tensor_tensor(
                            mix[:, m, :], mix[:, m, :], pcol("norm_g", C * g + m), rstd[:, :], ALU.mult, ALU.mult)))
                    if m >= 1:
                        after(done[m - 1])
                        nc.vector.tensor_tensor(x[:, m - 1, :], x[:, m - 1, :], mix[:, m - 1, :],
                                                ALU.add).then_inc(x_ready, 1)

            def ple(layer):
                for m in range(C):
                    t = FIRST[f"ple{layer}"] + m
                    dve.wait_ge(tile_done, t + 1)
                    dve.wait_ge(act_freed, FREED[FIRST[f"gate{layer}"] + m][1])
                    nc.vector.tensor_tensor(halves(mix[:, m, :]), slot(t), halves(mix[:, m, :]),
                                            ALU.mult).then_inc(dve_freed, 1)
                    dve.wait_ge(dve_freed, FREED[t][1])
                    nc.vector.tensor_tensor(x[:, m, :], x[:, m, :], mix[:, m, :], ALU.add).then_inc(x_ready, 1)

            dve.wait_ge(consts_in, 32)
            dve.wait_ge(x_in, 16)
            pre_norm(0, 0, None)
            dve.wait_ge(state_in, 16 * C)
            dve.wait_ge(pad_done, 1)
            for m in range(C):
                t = FIRST["pw1"] + 2 * m + 1
                dve.wait_ge(tile_done, t + 1)
                dve.wait_ge(act_freed, FREED[t - 1][1])
                p, s = slot(t), halves(sig[:, m % 2, :])
                e = conv_in[:, m, :]
                es = e[:, EXT_P:].rearrange("p (b t) -> p b t", t=EXT_S)
                rest = SEQ - HT
                step(nc.vector.scalar_tensor_tensor(e[:, TAPS - 1:TAPS - 1 + HT], p[:, 0, :], pcol("b_pw1", 2 * m + 1),
                                                    s[:, 0, :], ALU.add, ALU.mult))
                step(nc.vector.scalar_tensor_tensor(es[:, :, TAPS - 1:],
                                                    p[:, 1, rest:].rearrange("p (b t) -> p b t", t=DT),
                                                    pcol("b_pw1", 2 * m + 1),
                                                    s[:, 1, rest:].rearrange("p (b t) -> p b t", t=DT), ALU.add, ALU.mult))
                k = step(nc.vector.scalar_tensor_tensor(e[:, TAPS - 1 + HT:EXT_P], p[:, 1, 0:rest],
                                                    pcol("b_pw1", 2 * m + 1), s[:, 1, 0:rest], ALU.add, ALU.mult))
                after(k)
                yp, ys = y[:, m, 0:SEQ], y[:, m, SEQ:].rearrange("p (b t) -> p b t", t=DT)
                for j in range(TAPS):
                    w = pcol("w_dw", TAPS * m + j)
                    ep, esj = e[:, j:j + SEQ], es[:, :, j:j + DT]
                    if j == 0:
                        nc.vector.tensor_scalar(yp, ep, w, pcol("b_dw", m), ALU.mult, ALU.add).then_inc(dve_freed, 1)
                        k0 = None
                        k1 = step(nc.vector.tensor_scalar(ys, esj, w, pcol("b_dw", m), ALU.mult, ALU.add))
                        dve.wait_ge(dve_freed, FREED[t][1])
                    else:
                        if k0 is not None:
                            after(k0)
                        if j < TAPS - 1:
                            k0 = step(nc.vector.scalar_tensor_tensor(yp, ep, w, yp, ALU.mult, ALU.add))
                        else:
                            nc.vector.scalar_tensor_tensor(yp, ep, w, yp, ALU.mult, ALU.add).then_inc(glu_done, 1)
                        after(k1)
                        if j < TAPS - 1:
                            k1 = step(nc.vector.scalar_tensor_tensor(ys, esj, w, ys, ALU.mult, ALU.add))
                        else:
                            nc.vector.scalar_tensor_tensor(ys, esj, w, ys, ALU.mult, ALU.add).then_inc(conv_done, 1)
            dve.wait_ge(mean_ready, 1)
            for m in range(C):
                nc.vector.tensor_tensor(halves(y[:, m, :]), halves(y[:, m, :]), STAT, ALU.subtract).then_inc(centred, 1)
            get_rstd(1)
            for m in range(C):
                nc.vector.tensor_tensor(y[:, m, :], y[:, m, :], rstd[:, :], ALU.mult).then_inc(normed, 1)
            post_norm(2, 1)
            pre_norm(3, 2, FIRST["up0"])
            post_norm(4, 3)
            ple(0)
            pre_norm(5, 4, FIRST["down0"])
            for i in range(12):
                t = FIRST["swap"] + i
                raw = q[:, i, :] if i < 8 else k_rot[:, i - 8, :]
                dst = q_rot[:, i, :] if i < 8 else raw
                dve.wait_ge(tile_done, t + 1)
                nc.vector.tensor_tensor(halves(rope_tmp[:, i % 4, :]), slot(t), halves(tab("sin")), ALU.mult).then_inc(dve_freed, 1)
                k = step(nc.vector.tensor_tensor(dst, raw, tab("cos"), ALU.mult))
                dve.wait_ge(dve_freed, FREED[t][1])
                after(k)
                nc.vector.tensor_tensor(dst, dst, rope_tmp[:, i % 4, :], ALU.add).then_inc(rot_done, 1)

            def chain(ins):
                after(step(ins))

            for u in range(2 * NB):
                b, v = u // 2, u % 2
                dve.wait_ge(hid_a, u + 1)
                nc.vector.tensor_tensor(hid_s[:, u % 2, 0:252], ps[:, 2 * (u % 3) + 1, 4:256], hid_s[:, u % 2, 0:252],
                                        ALU.add).then_inc(hid_ab, 1)
                for w in ([u - 1] if u >= 1 else []) + ([u] if u == 2 * NB - 1 else []):
                    b, v = w // 2, w % 2
                    dve.wait_ge(w2_mm, w + 1)
                    if v == 0:
                        nc.vector.tensor_copy(k_cmp_s[:, b, :, :].rearrange("p g c -> p (g c)"), ps[:, 6, 0:128]).then_inc(w2_out, 1)
                    else:
                        half = slice(64 * (b % 2), 64 * (b % 2) + 64)
                        nc.vector.tensor_copy(v_cmp_s[half, b // 2, :], ps[half, 7, 0:256]).then_inc(w2_out, 1)

            def block_queries(src):
                for g in range(2):
                    for e in range(2):
                        part = slice(64 * e, 64 * e + 64)
                        last = nc.vector.tensor_copy(
                            qbd[part, :, g, e, :].rearrange("p b (r i) -> p b r i", r=REP),
                            src[part, 4 * g:4 * g + 4, SEQ:T].rearrange("p r (b i) -> p b r i", b=NB))
                last.then_inc(qbd_ready, 1)

            dve.wait_ge(qbd_zero, 1)
            block_queries(q)

            dve.wait_ge(sc_mm, 5)
            def groups(n):
                k, w, at = (NB, NCS, 0) if n == 0 else (16, NCP, 8 + 16 * (n - 1))
                return (pc[:, n, :].rearrange("p (k w) -> p k w", k=k), cmax[:, at:at + k].rearrange("p (k o) -> p k o", o=1),
                        csum[:, at:at + k].rearrange("p (k o) -> p k o", o=1), (P, k, w))

            for n in range(5):
                pr, mx, _, shape = groups(n)
                if n == 0:
                    raw = ps[:, 4, :].rearrange("p (k w) -> p k w", k=NB)
                    chain(nc.vector.tensor_copy(pr, raw))
                    chain(nc.vector.memset(pr[:, :, NCS - 1:NCS], NEG))
                else:
                    a = CON["cmp_add"][0] + NCP * (n - 1)
                    m = con[:, a:a + NCP].rearrange("p (o w) -> p o w", o=1).to_broadcast((P, C, NCP))
                    for e in range(2):
                        raw = ps[:, 2 * ((n - 1) // 2) + e, 256 * ((n - 1) % 2):256 * ((n - 1) % 2) + 256]
                        chain(nc.vector.tensor_tensor(pr[:, e:e + 15:2, :], raw.rearrange("p (k w) -> p k w", k=C), m, ALU.add))
                chain(nc.vector.tensor_reduce(mx, pr, AX.X, ALU.max))
                nc.vector.tensor_tensor(pr, pr, mx.to_broadcast(shape), ALU.subtract).then_inc(sc_sub, 1)
            for n in range(5):
                pr, mx, sm, shape = groups(n)
                dve.wait_ge(c_exp, n + 1)
                chain(nc.vector.tensor_reduce(sm, pr, AX.X, ALU.add))
                chain(nc.vector.reciprocal(sm, sm))
                if n == 0:
                    nc.vector.tensor_tensor(pr, pr, sm.to_broadcast(shape), ALU.mult).then_inc(pc_ready, 1)
                else:
                    g = gates[:, n - 1, :].rearrange("p (k o) -> p k o", o=3)[:, :, 0:1]
                    chain(nc.vector.tensor_tensor(sm, sm, g, ALU.mult))
                    a = CON["cmp_mul"][0] + NCP * (n - 1)
                    m = con[:, a:a + NCP].rearrange("p (o w) -> p o w", o=1).to_broadcast(shape)
                    nc.vector.tensor_tensor(pr, pr, m, ALU.mult).then_inc(pc_ready, 1)
                if n == 0:
                    dve.wait_ge(imp_mm, 1)
                    both = ps[:, 5, :].rearrange("p (b s w) -> p b s w", b=NB, w=4)
                    chain(nc.vector.tensor_reduce(imp.rearrange("p b (s o) -> p b s o", o=1), both, AX.X, ALU.add))
                    chain(nc.vector.tensor_tensor(imp[:, :, 1:16], both[:, :, 0:15, 3], imp[:, :, 1:16], ALU.add))
                    lo = least[:, 0:8].rearrange("p (b o) -> p b o", o=1)
                    hi = least[:, 8:16].rearrange("p (b o) -> p b o", o=1)
                    no = tab("block_no").rearrange("p (o s) -> p o s", o=1).to_broadcast((P, NB, 16))
                    chain(nc.vector.tensor_reduce(lo, imp[:, :, 1:15], AX.X, ALU.min))
                    chain(nc.vector.tensor_tensor(eq[:, :, 1:15], imp[:, :, 1:15], lo.to_broadcast((P, NB, 14)), ALU.is_equal))
                    chain(nc.vector.tensor_tensor(eq[:, :, 1:15], eq[:, :, 1:15], no[:, :, 1:15], ALU.mult))
                    chain(nc.vector.tensor_reduce(hi, eq[:, :, 1:15], AX.X, ALU.max))
                    chain(nc.vector.tensor_tensor(drop, no, hi.to_broadcast((P, NB, 16)), ALU.is_equal))
                    nc.vector.tensor_scalar(drop, drop, NEG, None, ALU.mult).then_inc(drop_ready, 1)
            for n in range(PT):
                dve.wait_ge(co_mm, n + 1)
                _, _, sm, _ = groups(n + 1)
                nc.vector.tensor_tensor(acc[:, n, :].rearrange("p (k d) -> p k d", d=HD),
                                        ps[:, 6:8, :].rearrange("p a (k d) -> p (a k) d", d=HD),
                                        sm.to_broadcast((P, 16, HD)), ALU.mult).then_inc(co_read, 1)
            block_queries(q_rot)

            def scores_out(b):
                pp = p_s[:, b % 2, :]
                dve.wait_ge(s_mm, b + 1)
                if b >= 2:
                    dve.wait_ge(t_mm, t_group(b - 2, 3) + 1)
                d = drop[:, b, :].rearrange("p (s o) -> p s o", o=1).to_broadcast((P, 16, HD))
                step(nc.vector.tensor_tensor(pp[:, 0:1024].rearrange("p (s w) -> p s w", w=HD),
                                             ps[:, 0:2, :].rearrange("p a (s w) -> p (a s) w", w=HD), d, ALU.add))
                a = CON["new_add"][0] + NS * b
                step(nc.vector.tensor_tensor(pp[:, 1024:1088], ps[:, 3, 0:NS], con[:, a:a + NS], ALU.add))
                nc.vector.tensor_tensor(pp[:, 1600:1664], ps[:, 3, NS:2 * NS], con[:, a:a + NS], ALU.add).then_inc(s_read, 1)
                after(steps[0])
                nc.vector.tensor_reduce(stat_s[:, b, 0:1], pp[:, 0:1088], AX.X, ALU.max, negate=True).then_inc(s_max, 1)
                dve.wait_ge(s_win, b + 1)
                chain(nc.vector.tensor_tensor(pp[:, 1088:1096], pp[:, 1088:1096], tab("win_add"), ALU.add))
                dve.wait_ge(s_read, b + 1)
                nc.vector.tensor_reduce(stat_s[:, b, 1:2], pp[:, 1088:1664], AX.X, ALU.max, negate=True).then_inc(s_max, 1)

            def rows_out(b):
                a = acc_s[:, b % 2, :]
                dve.wait_ge(gate_moved, 16 * 17)
                dve.wait_ge(s_exp, b + 1)
                chain(nc.vector.reciprocal(stat_s[:, b, 4:6], stat_s[:, b, 2:4]))
                chain(nc.vector.tensor_tensor(stat_s[:, b, 4:6], stat_s[:, b, 4:6], gate_s[:, b, 1:3], ALU.mult))
                dve.wait_ge(o_mm, b + 1)
                if b >= 2:
                    dve.wait_ge(t_fin, b - 1)
                chain(nc.vector.tensor_scalar(a, ps[:, 7, 0:256], gate_s[:, b, 0:1], None, ALU.mult))
                chain(nc.vector.scalar_tensor_tensor(a, ps[:, 6, 0:256], stat_s[:, b, 4:5], a, ALU.mult, ALU.add))
                nc.vector.scalar_tensor_tensor(a, ps[:, 6, 256:512], stat_s[:, b, 5:6], a, ALU.mult, ALU.add).then_inc(o_read, 1)
                dve.wait_ge(o_read, b + 1)
                nc.vector.tensor_tensor(a, a, tab("own_kv"), ALU.mult).then_inc(acc_ready, 1)

            def heads_out(b, n):
                dve.wait_ge(t_mm, n + 1)
                for g in range(2):
                    lo = 128 * g + 64 * g
                    src = ps[:, 4 + n % 2, lo:lo + 64].rearrange("p (e r i) -> p r i e", e=2, r=REP)
                    last = nc.vector.tensor_reduce(
                        attn_t[:, 4 * g:4 * g + 4, SEQ + DT * b:SEQ + DT * b + DT].rearrange("p r (i o) -> p r i o", o=1),
                        src, AX.X, ALU.add)
                last.then_inc(t_fin, 1)

            scores_out(0)
            for b in range(NB):
                if b + 1 < NB:
                    scores_out(b + 1)
                if b >= 1:
                    heads_out(b - 1, t_group(b, 4))
                rows_out(b)
            heads_out(NB - 1, t_group(NB, 0))

            items = [(n, c, e, r) for n in range(PT) for c in range(C) for e in range(2) for r in range(2)]

            def p_top(i):
                n = items[i][0]
                dve.wait_ge(p_mm, i + 1)
                s = ps[:, i % 4, :]
                chain(nc.vector.tensor_tensor(s[:, n * P:(n + 1) * P], s[:, n * P:(n + 1) * P], tab("causal"), ALU.add))
                nc.vector.tensor_reduce(nmax_p[:, i % 8:i % 8 + 1], s[:, 0:(n + 1) * P], AX.X, ALU.max,
                                        negate=True).then_inc(p_max, 1)

            def p_acc(i):
                n, c, e, r = items[i]
                f, s = f_p[:, i % 8:i % 8 + 1], sum_p[:, i % 8:i % 8 + 1]
                dve.wait_ge(p_exp, i + 1)
                chain(nc.vector.reciprocal(f, s))
                head = 2 * c + e
                g = gates[:, n, 3 * head + 1 + r:3 * head + 2 + r]
                chain(nc.vector.tensor_tensor(f, f, g, ALU.mult))
                dve.wait_ge(po_mm, i + 1)
                a = acc[:, n, HD * (2 * c + e):HD * (2 * c + e + 1)]
                if i >= 1:
                    dve.wait_ge(po_read, i)
                nc.vector.scalar_tensor_tensor(a, ps[:, 6 + i % 2, 0:HD], f, a, ALU.mult, ALU.add).then_inc(po_read, 1)

            LAG = 3
            for i in range(len(items) + LAG):
                if i < len(items):
                    p_top(i)
                if i >= LAG:
                    p_acc(i - LAG)

            post_norm(6, 5)
            pre_norm(7, 6, FIRST["up1"])
            post_norm(8, 7)
            ple(1)


def feature_major(a):
    a = np.asarray(a)
    r = a.reshape(a.shape[:-1] + (a.shape[-1] // P, P))
    n = a.ndim - 2
    return np.ascontiguousarray(np.moveaxis(r, [n, n + 1, n + 2], [n + 2, n + 1, n]))


def weight_blocks(w, width):
    k, m = w.shape
    return w.reshape(k // P, P, m // width, width).transpose(2, 1, 0, 3).reshape(m // width, P, -1)


HEAD_ORDER = np.arange(D).reshape(2, 2, REP, HD).transpose(0, 2, 1, 3).reshape(-1)


def constants():
    t = np.zeros((P, NCON), np.float32)

    def put(name, v):
        a, b = CON[name]
        t[:v.shape[0], a:b] = v.reshape(v.shape[0], -1)

    p = np.arange(P)
    put("ident", np.eye(P))
    put("eps", np.full((P, 1), EPS))
    put("mean", np.full((P, P), 1.0 / D))
    d = p % HD
    half = 8
    partner = np.where(d < half, p + half, np.where(d < 2 * half, p - half, p))
    swap = np.zeros((P, P))
    swap[partner, p] = 1.0
    put("swap", swap)
    pos = np.concatenate([np.arange(SEQ), np.tile(PAST + np.arange(DT), NB)]).astype(np.float32)
    inv = np.power(np.float32(500000.0), -np.arange(half, dtype=np.float32) * np.float32(2.0 / 16))
    ang = (pos[None, :] * inv[:, None].astype(np.float32)).astype(np.float32)
    cos, sin = np.cos(ang), np.sin(ang)
    rot = d < 2 * half
    put("cos", np.where(rot[:, None], cos[d % half], 1.0))
    put("sin", np.where(rot[:, None], np.where(d < half, -1.0, 1.0)[:, None] * sin[d % half], 0.0))
    qq = np.arange(P)
    put("causal", np.where(qq[None, :] <= qq[:, None], 0.0, NEG))
    g, i = p // 32, p % DT
    put("same_q", (g[:, None] == g[None, :]) & (i[:, None] == i[None, :]))
    qpos = np.arange(PT)[None, :] * P + qq[:, None]
    c = np.arange(NCP)
    ok = (16 * c + 31)[None, None, :] <= qpos[:, :, None]
    put("cmp_add", np.where(ok, 0.0, NEG))
    put("cmp_mul", ok.astype(np.float32))
    kb, kj = np.arange(NS) // DT, np.arange(NS) % DT
    ok = (kb[None, None, :] == np.arange(NB)[None, :, None]) & (kj[None, None, :] <= i[:, None, None])
    put("new_add", np.where(ok, 0.0, NEG))
    put("win_add", np.where(np.arange(DT)[None, :] > i[:, None], 0.0, NEG))
    put("block_no", np.tile(np.arange(16), (P, 1)))
    put("own_kv", (np.arange(256) // HD)[None, :] == g[:, None])
    return t


def kernel(**inputs):
    import concourse.bacc as bacc
    from concourse.bass_utils import run_bass_kernel_spmd

    v = {k: np.asarray(a) for k, a in inputs.items()}
    tokens = np.concatenate([v["x_prompt"].reshape(SEQ, D), v["x_sample"].reshape(NS, D)])
    p_tokens = np.concatenate([v["p_prompt"].reshape(2, SEQ, 256), v["p_sample"].reshape(2, NS, 256)], axis=1)
    par = np.zeros((P, NPAR), np.float32)

    def put(name, a):
        lo, hi = PAR[name]
        par[:, lo:hi] = a.reshape(-1, P).T

    glu = np.arange(2 * D).reshape(2, C, P)[::-1].transpose(1, 0, 2).reshape(-1)
    put("norm_g", v["norm_g"])
    put("b_ple", v["b_ple_gate"])
    put("b_pw1", v["conv_b_pw1"][0][glu])
    lo, hi = PAR["w_dw"]
    par[:, lo:hi] = v["conv_w_dw"][0].reshape(TAPS, C, P).transpose(2, 1, 0).reshape(P, -1)
    put("b_dw", v["conv_b_dw"])
    put("ln_g", v["conv_ln_g"])
    put("ln_b", v["conv_ln_b"])
    put("b_pw2", v["conv_b_pw2"])
    lo, hi = PAR["pe"]
    par[:, lo:hi] = v["nsa_cmp_pe"][0].reshape(2, 16, 2, HD).transpose(2, 3, 0, 1).reshape(P, -1)
    w_in = v["nsa_w_in"][0]
    kv_at = lambda i: w_in[:, D + 256 * i:D + 256 * (i + 1)]
    w_g = w_in[:, D + 6 * 256:].reshape(D, 2, 2, REP, 3).transpose(0, 1, 3, 2, 4).reshape(D, 48)
    w_q = w_in[:, :D][:, HEAD_ORDER]
    w = np.concatenate([
        weight_blocks(v["conv_w_pw1"][0][:, glu], 512), weight_blocks(v["conv_w_pw2"][0], 512),
        weight_blocks(v["w_ff1"][0], 512), weight_blocks(v["w_ff2"][0], P), weight_blocks(v["w_ple_gate"][0], 512),
        weight_blocks(v["w_ple_gate"][1], 512), weight_blocks(w_q, 512), weight_blocks(np.concatenate([kv_at(0), kv_at(1)], 1), 512),
        weight_blocks(np.concatenate([kv_at(2), kv_at(4)], 1), 512),
        weight_blocks(np.concatenate([kv_at(3), kv_at(5)], 1), 512),
        weight_blocks(v["nsa_w_out"][0][HEAD_ORDER], 512),
        weight_blocks(v["w_ff1"][1], 512), weight_blocks(v["w_ff2"][1], P),
    ])
    arrays = {
        "x": feature_major(tokens), "p": feature_major(p_tokens), "par": par, "con": constants(), "w": w,
        "ple": np.stack([weight_blocks(v["w_ple"][i], D)[0] for i in range(2)]),
        "state": np.ascontiguousarray(v["state_conv"][0].reshape(NB, TAPS - 1, C, P).transpose(3, 2, 0, 1)),
        "w_gates": weight_blocks(w_g, 48)[0].reshape(P, C, 48),
    }
    cc = v["cache_cmp"][0].reshape(POOL, 8, 8, 2, 2, KV, HD).transpose(0, 3, 6, 4, 2, 1, 5)
    arrays["cmp_pages"] = cc.reshape(POOL, P, 512)
    cs = v["cache_sel"][0]
    keys = cs[:, :, 0].reshape(POOL, P, 2, 2, HD).transpose(0, 3, 4, 2, 1).reshape(POOL, P, 256)
    arrays["sel_pages"] = np.concatenate([keys, cs[:, :, 1].reshape(POOL, P, 256)], 2)
    cw = v["cache_win"][0]
    keys = cw[:, :, 0].reshape(NB, WIN, 2, 2, HD).transpose(0, 3, 4, 2, 1).reshape(NB, P, 1024)
    vals = cw[:, :, 1].reshape(NB, 4, P, 256).transpose(0, 2, 1, 3).reshape(NB, P, 1024)
    arrays["win"] = np.concatenate([keys, vals], 2)
    arrays["pages"] = v["page_table"].reshape(1, NB * PAGES)
    w1 = v["nsa_cmp_w1"][0].reshape(2, 16, 2, HD, P)
    arrays["w1"] = w1.transpose(2, 3, 0, 1, 4).reshape(P, 2, 16, P)
    arrays["w1s"] = w1[:, :, ::-1].transpose(2, 3, 0, 1, 4).reshape(P, 2, 16, P)
    arrays["w2"] = v["nsa_cmp_w2"][0].transpose(1, 0, 2)
    outs = {"win": (NB, P, BLK // 2), "y": (P, C, T), "conv_p": (P, C, TAPS - 1), "conv_s": (P, C, NB, TAPS - 1), "kv_cmp": (P, 4, T), "k_rot": (P, 4, T),
            "v_tok": (P, PT, 512), "v_tok_s": (NS, 512)}
    nc = bacc.Bacc("TRN2", target_bir_lowering=False, num_devices=1)
    arrays = {f"in_{k}": np.ascontiguousarray(a) for k, a in arrays.items()}
    ext = {k[3:]: nc.dram_tensor(k, a.shape, mybir.dt.from_np(a.dtype), kind="ExternalInput").ap()
           for k, a in arrays.items()}
    out = {k: nc.dram_tensor(f"out_{k}", s, F32, kind="ExternalOutput").ap() for k, s in outs.items()}
    program(nc, ext, out)
    r = run_bass_kernel_spmd(nc, [arrays], core_ids=[0]).results[0]
    got = {k: r[f"out_{k}"] for k in outs}

    def kv_rows(a, i):
        return a[:, 2 * i:2 * i + 2].transpose(2, 1, 0).reshape(T, KV, HD)

    v_all = np.concatenate([got["v_tok"].transpose(1, 0, 2).reshape(SEQ, 512), got["v_tok_s"]])
    cmp_rows = np.stack([kv_rows(got["kv_cmp"], 0), kv_rows(got["kv_cmp"], 1)], 1)
    sel_rows = np.stack([kv_rows(got["k_rot"], 0), v_all[:, :256].reshape(T, KV, HD)], 1)
    win_rows = np.stack([kv_rows(got["k_rot"], 1), v_all[:, 256:].reshape(T, KV, HD)], 1)
    split = lambda a: (a[:SEQ][None, None], a[SEQ:].reshape((1, NB, DT) + a.shape[1:]))
    cmp_p, cmp_s = split(cmp_rows)
    sel_p, sel_s = split(sel_rows)
    win_p, win_s = split(win_rows)
    y = got["y"].transpose(2, 1, 0).reshape(T, D)
    y_p, y_s = y[:SEQ].reshape(1, SEQ, D), y[SEQ:].reshape(NB, DT, D)
    wk = got["win"][:, :, :1024].reshape(NB, 2, HD, 2, WIN).transpose(0, 4, 3, 1, 2).reshape(NB, WIN, KV, HD)
    wv = got["win"][:, :, 1024:].reshape(NB, P, 4, KV, HD).transpose(0, 2, 1, 3, 4).reshape(NB, WIN, KV, HD)
    win_all = np.concatenate([np.stack([wk, wv], 2)[None][:, :, DT:], win_s], 2)
    conv_p = got["conv_p"].transpose(2, 1, 0).reshape(1, 1, TAPS - 1, D)
    conv_s = got["conv_s"].transpose(2, 3, 1, 0).reshape(1, NB, TAPS - 1, D)
    return y_p, y_s, cmp_p, cmp_s, sel_p, sel_s, win_p, win_all, conv_p, conv_s
```

```python
import numpy as np
import concourse.bass as bass
import concourse.mybir as mybir
from concourse.alu_op_type import AluOpType as ALU

F32 = mybir.dt.float32
F32R = mybir.dt.float32r
I32 = mybir.dt.int32
ACT = mybir.ActivationFunctionType
AX = mybir.AxisListType

P = 128
D = 1024
SEQ = 512
NB = 8
DT = 8
NS = NB * DT
T = SEQ + NS
HT = T // 2
C = D // P
TAPS = 31
PAST = 1024
PAGES = 8
POOL = 80
KV = 4
REP = 4
HD = 64
FF = 4096
FC = FF // P
WIN = 512
EPS = 1e-6
NEG = -1e30
SCALE = HD ** -0.5
WB = 2048
BLK = 4096
Q4 = 4
PT = SEQ // P
TT = PT + 1
EXT_P = SEQ + TAPS - 1
EXT_S = DT + TAPS - 1
EXT = EXT_P + NB * EXT_S
NCP = 32
NCS = 64

def columns(parts):
    at, n = {}, 0
    for name, width in parts:
        at[name] = (n, n + width)
        n += width
    return at, n

PAR, NPAR = columns([("norm_g", 64), ("b_ple", 16), ("b_pw1", 16), ("w_dw", 8 * TAPS), ("b_dw", 8), ("ln_g", 8),
                     ("ln_b", 8), ("b_pw2", 8), ("pe", 2 * 16)])
CON, NCON = columns([("ident", P), ("mean", P), ("swap", P), ("cos", T), ("sin", T), ("causal", P),
                     ("same_q", P), ("cmp_add", PT * NCP), ("cmp_mul", PT * NCP), ("new_add", NB * NS),
                     ("win_add", DT), ("block_no", 16), ("own_kv", 256), ("eps", 1)])

def mlp_stages(layer):
    return [s for n in range(Q4) for s in ((f"up{layer}{n}", C, "A" * C),
                                           (f"down{layer}{n}", C, ("A" if n == 0 else "D") * C))]


STAGES = ([("pw1", 16, "A" * 16), ("taps", 2, "AA"), ("pw2", C, "A" * C)] + mlp_stages(0) + [("ple0", C, "A" * C), ("gate0", C, "A" * C),
          ("q", C, "A" * C), ("kv_cmp", 4, "A" * 4), ("k_rot", 4, "A" * 4), ("v_tok", 2 * TT, "A" * 2 * TT),
          ("gates", TT, "A" * TT), ("swap", 12, "D" * 12), ("out", C, "A" * C)] + mlp_stages(1)
          + [("ple1", C, "A" * C), ("gate1", C, "A" * C)])
FIRST, FREED = {}, []
_n = {"A": 0, "D": 0}
for _name, _count, _who in STAGES:
    FIRST[_name] = len(FREED)
    for _w in _who:
        _n[_w] += 1
        FREED.append((_w, _n[_w]))

STAGED = {name: C * n for n, name in enumerate(
    ["conv", "silu", "mlp0", "hid00", "hid01", "hid02", "hid03", "x0", "nsa", "attn",
     "mlp1", "hid10", "hid11", "hid12", "hid13", "x1"])}
INPUT = {"pw1": "conv", "pw2": "silu", "gate0": "x0", "gate1": "x1", "q": "nsa", "kv_cmp": "nsa", "k_rot": "nsa",
         "v_tok": "nsa", "out": "attn"}
for _l in range(2):
    for _q in range(Q4):
        INPUT[f"up{_l}{_q}"] = f"mlp{_l}"
        INPUT[f"down{_l}{_q}"] = f"hid{_l}{_q}"

RAW_OF = {name: C * n for n, name in enumerate(
    ["conv", "mlp0", "hid00", "hid01", "hid02", "hid03", "nsa", "mlp1", "hid10", "hid11", "hid12", "hid13"])}

W_STAGES = ([("pw1", 8), ("pw2", 4)] + [(s, 4) for s, _, _ in mlp_stages(0)] + [("gate0", 4), ("q", 4), ("kv_cmp", 2),
            ("k_rot", 2), ("v_tok", 2), ("out", 4)] + [(s, 4) for s, _, _ in mlp_stages(1)] + [("gate1", 4)])
W_OF, W_END, BLOCKS = {}, [], []
for _s, _c in W_STAGES:
    W_OF[_s] = len(W_END)
    _per = TT if _s == "v_tok" else 2
    if _s == "out":
        BLOCKS += [("cmp_pages", b) for b in range(NB)]
        BLOCKS += [("sel_pages", 0), ("sel_pages", 1)]
        BLOCKS += [("win_k", 0), ("win_k", 1), ("win_v", 0), ("sel_pages", 2), ("win_v", 1)]
        for _b in range(2, NB):
            BLOCKS += [("win_k", _b)] + [("sel_pages", _b + 1)] * (_b + 1 < NB) + [("win_v", _b)]
    if _s.startswith("gate"):
        BLOCKS.append(("ple", int(_s[-1])))
    for _i in range(_c):
        BLOCKS.append(("w", len(W_END)))
        W_END.append(FIRST[_s] + _per * (_i + 1))
SIZE = {"w": WB, "ple": WB, "cmp_pages": BLK, "sel_pages": BLK, "win_k": BLK // 4, "win_v": BLK // 4}
B_OF = {b: i for i, b in reversed(list(enumerate(BLOCKS)))}

RAW, SPLIT, RING = 0, 2 * WB, 6 * WB
PLACE, _raw = [], 0
for _src, _row in BLOCKS:
    if _src in ("w", "ple"):
        PLACE.append((WB * (_raw % 2), _raw % 2))
        _raw += 1
    elif _src == "cmp_pages":
        PLACE.append((BLK * (_row % 3), 2 + _row % 3))
    elif _src == "sel_pages":
        PLACE.append((BLK * ((_row + 2) % 3), 2 + (_row + 2) % 3))
    else:
        PLACE.append((None, {"win_k": 5, "win_v": 7}[_src] + _row % 2))
LAST_THERE, LOADED = [], []
_at, _holds = [0] * 9, {}
for _i, (_src, _row) in enumerate(BLOCKS):
    _lo, _sem = PLACE[_i]
    _parts = range(0) if _src.startswith("win") else range(_lo // WB, (_lo + SIZE[_src]) // WB)
    LAST_THERE.append(sorted({_holds[_k] for _k in _parts if _k in _holds}))
    for _k in _parts:
        _holds[_k] = ("loaded", _i)
    if _src == "w":
        for _k in (0, 1):
            _holds[SPLIT // WB + 2 * (_row % 2) + _k] = ("split", _row)
    _at[_sem] += 16 * (PAGES if _src.endswith("pages") else 1)
    LOADED.append(_at[_sem])


ADDED = (2, 4, 6, 8)


def adds(n):
    return (C - 1) * sum(a < n for a in ADDED)


def summed(n):
    return sum(1 if a in ADDED else C for a in range(n))


def t_group(b, k):
    return 5 * b + k - (b > 0)


def program(nc, ext, out):
    from contextlib import ExitStack
    with ExitStack() as ctx:
        def sb(name, shape, dt=F32):
            return ctx.enter_context(nc.sbuf_tensor(name, shape, dt))

        def sem(name):
            return ctx.enter_context(nc.semaphore(name))

        arena = [16512]

        def at_byte(name, shape, byte, dt=F32):
            return nc.alloc_sbuf_tensor_at(name, shape, dt, offset=byte)

        def sb(name, shape, dt=F32):
            n = 4 * int(np.prod(shape[1:]))
            byte = arena[0]
            arena[0] += (n + 31) // 32 * 32
            return at_byte(name, shape, byte, dt)

        ring_byte = arena[0]
        w_raw = sb("w_raw", [P, 2, WB])
        w_hi = [sb("w_hi0", [P, WB], F32R), None]
        w_lo = [sb("w_lo0", [P, WB], F32R), None]
        w_hi[1] = sb("w_hi1", [P, WB], F32R)
        w_lo[1] = sb("w_lo1", [P, WB], F32R)
        ring = at_byte("ring", [P, RING], ring_byte)
        x = sb("x", [P, C, T])
        ha_byte = arena[0]
        ha = sb("ha", [P, C * T + NS], F32R)
        hb_byte = arena[0]
        hb = sb("hb", [P, C * T + NS], F32R)
        big_byte = arena[0]
        big = sb("big", [P, 4 * C * T])
        hid_hi = at_byte("hid_hi", [P, C * T], big_byte, F32R)
        hid_lo = at_byte("hid_lo", [P, C * T], big_byte + 4 * C * T, F32R)
        mix = at_byte("mix", [P, C, T], big_byte + 8 * C * T)
        ple_in = at_byte("ple_in", [P, 2, T], big_byte + 12 * C * T)
        emb = at_byte("emb", [P, C, T], big_byte)
        diag = at_byte("diag", [P, 18, P], arena[0])
        sq = sb("sq", [P, 4, T])
        rstd = sb("rstd", [P, T])
        par = sb("par", [P, NPAR])
        con = sb("con", [P, NCON])
        conv_in = big[:, 0:C * EXT].rearrange("p (c t) -> p c t", t=EXT)
        y = big[:, C * EXT:C * EXT + C * T].rearrange("p (c t) -> p c t", t=T)
        at = C * EXT + C * T
        sig = big[:, at:at + 2 * T].rearrange("p (c t) -> p c t", t=T)
        odd_taps = big[:, at + 2 * T:at + 2 * T + SEQ]
        at = 3 * C * T + 2 * T
        val = big[:, at:at + 2 * T].rearrange("p (c t) -> p c t", t=T)
        at += 2 * T
        tap_prod = big[:, at:at + NS * TAPS].rearrange("p (b t j) -> p b t j", b=NB, t=DT)
        at = 0
        q = big[:, at:at + C * T].rearrange("p (c t) -> p c t", t=T); at += C * T
        q_rot = big[:, at:at + C * T].rearrange("p (c t) -> p c t", t=T); at += C * T
        kv_cmp = big[:, at:at + 4 * T].rearrange("p (c t) -> p c t", t=T); at += 4 * T
        k_rot = big[:, at:at + 4 * T].rearrange("p (c t) -> p c t", t=T); at += 4 * T
        v_tok = big[:, at:at + TT * 512].rearrange("p (n f) -> p n f", f=512); at += TT * 512
        gates = sb("gates", [P, TT, 48])
        w_gates = sb("w_gates", [P, C * 48])
        wg_hi = sb("wg_hi", [P, C * 48], F32R)
        wg_lo = sb("wg_lo", [P, C * 48], F32R)
        rope_tmp = sq
        k_cmp_s = big[:, at:at + NB * 2 * NCS].rearrange("p (b g c) -> p b g c", b=NB, g=2); at += NB * 2 * NCS
        v_cmp_s = big[:, at:at + NB // 2 * 256].rearrange("p (b f) -> p b f", f=256)
        w1 = at_byte("w1", [P, 2, 16, P], ha_byte)
        kv_pairs = at_byte("kv_pairs", [P, 2, KV, SEQ], hb_byte)
        acc = at_byte("acc", [P, PT, D], hb_byte)
        attn_t = at_byte("attn_t", [P, C, T], ha_byte)
        sq_flat = sq[:, :, :].rearrange("p c t -> p (c t)")
        hid_s = sq_flat[:, 0:512].rearrange("p (u n) -> p u n", u=2)
        hid_p = sq_flat[:, 512:768].rearrange("p (v e g c) -> p v e g c", v=2, e=2, g=2)
        v_cmp_p = sq_flat[:, 1792:2304].rearrange("p (g f) -> p g f", g=2)
        pc_t_p = sq_flat[:, 0:512].rearrange("p (j t) -> p j t", j=4)
        pt_s = sq_flat[:, 0:1792]
        q_flat = q.rearrange("p c t -> p (c t)")
        pc = q_flat[:, 0:2560].rearrange("p (n c) -> p n c", n=5)
        pc_t_s = q_flat[:, 4096:4608].rearrange("p (j t) -> p j t", j=4)
        p_s = q_flat[:, 0:3328].rearrange("p (u n) -> p u n", u=2)
        p_p = q_flat[:, 0:2048].rearrange("p (u n) -> p u n", u=4)
        pt_p = q_flat[:, 2048:3072].rearrange("p (u n) -> p u n", u=2)
        kvc_flat = kv_cmp.rearrange("p c t -> p (c t)")
        qbd = kvc_flat[:, 0:1024].rearrange("p (b g e m) -> p b g e m", b=NB, g=2, e=2)
        imp = kvc_flat[:, 1024:1152].rearrange("p (b s) -> p b s", b=NB)
        drop = kvc_flat[:, 1152:1280].rearrange("p (b s) -> p b s", b=NB)
        eq = kvc_flat[:, 1280:1408].rearrange("p (b s) -> p b s", b=NB)
        acc_s = kvc_flat[:, 1408:1920].rearrange("p (u n) -> p u n", u=2)
        cmax = kvc_flat[:, 1920:1992]
        csum = kvc_flat[:, 1992:2064]
        stat_s = kvc_flat[:, 2064:2128].rearrange("p (b c) -> p b c", b=NB)
        least = kvc_flat[:, 2128:2144]
        nmax_p = kvc_flat[:, 2144:2152]
        f_p = kvc_flat[:, 2152:2160]
        sum_p = kvc_flat[:, 2160:2168]
        k_cmp_p = sb("k_cmp_p", [P, 2, 2, NCP])
        w2 = sb("w2", [P, 2, HD])
        c_vec = sb("c_vec", [P, 2])
        gate_s = sb("gate_s", [P, NB, 3])
        pages = sb("pages", [1, NB * PAGES], I32)
        assert arena[0] <= 229344, arena[0]
        gate_rows = nc.dram_tensor("gate_rows", (NS, 48), F32, kind="Internal").ap()

        ps = ctx.enter_context(nc.psum_tensor("ps", [P, 8, 512], F32))
        STAT = ps[:, 6:8, 0:HT]

        def split_input(name):
            return (hb, ha) if name == "attn" else (hid_hi, hid_lo) if name.startswith("hid") else (ha, hb)

        def chunk(a, k, lo=0, n=T):
            return a[:, k * T + lo:k * T + lo + n]

        def block_at(i, lo, n):
            return ring[:, PLACE[i][0] + lo:PLACE[i][0] + lo + n]

        def window(b):
            return attn_t[:, 4 * (b % 2):4 * (b % 2) + 4, 0:SEQ]

        def slot(t):
            return ps[:, 2 * (t % 3):2 * (t % 3) + 2, 0:HT]

        def halves(ap):
            return ap.rearrange("p (a t) -> p a t", a=2)

        def sample_rows(m):
            return conv_in[:, m, EXT_P:].rearrange("p (b t) -> p b t", t=EXT_S)

        def pcol(name, i):
            a = PAR[name][0] + i
            return par[:, a:a + 1]

        def tab(name):
            a, b = CON[name]
            return con[:, a:b]

        consts_in = sem("consts_in")
        x_in = [sem(f"x_in{i}") for i in range(4)]
        state_in = sem("state_in")
        ple_loaded = sem("ple_loaded")
        wg_in = sem("wg_in")
        block_in = [sem(f"block_in{i}") for i in range(9)]
        tile_done = sem("tile_done")
        act_freed = sem("act_freed")
        dve_freed = sem("dve_freed")
        freed = {"A": act_freed, "D": dve_freed}
        sq_ready = sem("sq_ready")
        sq_added = sem("sq_added")
        sq_summed = sem("sq_summed")
        mean_ready = sem("mean_ready")
        std_ready = sem("std_ready")
        rstd_ready = sem("rstd_ready")
        w_hi_ready = sem("w_hi_ready")
        w_ready = sem("w_ready")
        raw_ready = sem("raw_ready")
        hi_ready = sem("hi_ready")
        lo_ready = sem("lo_ready")
        wg_hi_ready, wg_ready = sem("wg_hi_ready"), sem("wg_ready")
        silu_done = sem("silu_done")
        pad_zero = sem("pad_zero")
        x_ready = sem("x_ready")
        glu_done = sem("glu_done")
        tap_products = sem("tap_products")
        sample_conv = sem("sample_conv")
        diag_ready = sem("diag_ready")
        diag_used = sem("diag_used")
        pad_done = sem("pad_done")
        conv_done = sem("conv_done")
        centred = sem("centred")
        normed = sem("normed")
        dve_step = sem("dve_step")
        stored = sem("stored")
        rot_done = sem("rot_done")

        pages_in = sem("pages_in")
        w1_in = sem("w1_in")
        pairs_in = sem("pairs_in")
        kv_cmp_stored = sem("kv_cmp_stored")
        gate_moved = sem("gate_moved")
        win_stored = [sem("win_stored0"), sem("win_stored1")]
        c_mm, c_there = sem("c_mm"), sem("c_there")
        cmp_mm, hid_a, hid_ab, hid_ready = sem("cmp_mm"), sem("hid_a"), sem("hid_ab"), sem("hid_ready")
        w2_mm, w2_out = sem("w2_mm"), sem("w2_out")
        phid_mm, phid_ready = sem("phid_mm"), sem("phid_ready")
        phid_zero = sem("phid_zero")
        pw2_mm, pw2_out = sem("pw2_mm"), sem("pw2_out")
        bd_zero = sem("bd_zero")
        qbd_zero, qbd_ready = sem("qbd_zero"), sem("qbd_ready")
        sc_mm = sem("sc_mm")
        sc_sub, c_exp = sem("sc_sub"), sem("c_exp")
        pc_ready = sem("pc_ready")
        imp_mm, drop_ready = sem("imp_mm"), sem("drop_ready")
        ct_mm, ct_out = sem("ct_mm"), sem("ct_out")
        co_mm, co_read = sem("co_mm"), sem("co_read")
        s_mm, s_read = sem("s_mm"), sem("s_read")
        s_win = sem("s_win")
        s_max, s_exp = sem("s_max"), sem("s_exp")
        t_mm, t_out, t_fin = sem("t_mm"), sem("t_out"), sem("t_fin")
        o_mm, o_read, acc_ready = sem("o_mm"), sem("o_read"), sem("acc_ready")
        p_mm, p_max, p_exp = sem("p_mm"), sem("p_max"), sem("p_exp")
        pt_mm, pt_out = sem("pt_mm"), sem("pt_out")
        po_mm, po_read = sem("po_mm"), sem("po_read")
        ft_mm, ft_out = sem("ft_mm"), sem("ft_out")
        pe_ple1 = sem("pe_ple1")

        block = ctx.enter_context(nc.Block())

        @block.sync
        def _(sp):
            sp.dma_start(con[:, :], ext["con"]).then_inc(consts_in, 16)
            sp.dma_start(par[:, :], ext["par"]).then_inc(consts_in, 16)
            for i in range(4):
                sp.dma_start(x[:, 2 * i:2 * i + 2, :], ext["x"][:, 2 * i:2 * i + 2, :]).then_inc(x_in[i], 16)
            sp.dma_start(pages[:, :], ext["pages"]).then_inc(pages_in, 16)
            sp.wait_ge(pages_in, 16)
            for i, (src, row) in enumerate(BLOCKS):
                for what, last in LAST_THERE[i]:
                    if what == "split":
                        sp.wait_ge(tile_done, W_END[last])
                        continue
                    was, n = BLOCKS[last]
                    if was == "w":
                        sp.wait_ge(w_ready, n + 1)
                    elif was == "ple":
                        sp.wait_ge(tile_done, FIRST[f"ple{n}"] + C)
                    elif was == "cmp_pages":
                        sp.wait_ge(hid_ab, 2 * n + 2)
                    else:
                        sp.wait_ge(o_mm, n + 1)
                lo, k = PLACE[i]
                if src.startswith("win"):
                    if row < 2:
                        sp.wait_ge(cmp_mm, 2 * NB)
                    else:
                        sp.wait_ge(s_mm if src == "win_k" else o_mm, row - 1)
                        sp.wait_ge(win_stored[row % 2], 16 * (row // 2))
                if src in ("w", "ple"):
                    to = w_raw[:, k, :]
                elif src == "win_k":
                    to = window(row)[:, 0:2, :]
                elif src == "win_v":
                    to = window(row)[:, 2:4, :]
                else:
                    to = ring[:, lo:lo + SIZE[src]]
                if src.endswith("pages"):
                    for j in range(PAGES):
                        page = sp.value_load(pages[0:1, row * PAGES + j:row * PAGES + j + 1], min_val=0, max_val=POOL - 1)
                        sp.dma_start(to[:, j * 512:(j + 1) * 512],
                                     ext[src][bass.ds(page, 1), :, :].rearrange("o p n -> (o p) n")).then_inc(block_in[k], 16)
                else:
                    if src.startswith("win"):
                        rows = ext["win"][row].rearrange("p (c n) -> p c n", n=SEQ)
                        rows = rows[:, 0:2, :] if src == "win_k" else rows[:, 2:4, :]
                    else:
                        rows = ext[src][row]
                    sp.dma_start(to, rows).then_inc(block_in[k], 16)
                if i == 0:
                    for m in range(C):
                        sp.dma_start(sample_rows(m)[:, :, 0:TAPS - 1], ext["state"][:, m]).then_inc(state_in, 16)
                    sp.dma_start(ple_in[:, :, :], ext["p"][0]).then_inc(ple_loaded, 16)
                    sp.dma_start(w_gates[:, :], ext["w_gates"]).then_inc(wg_in, 16)
                    sp.dma_start(w2[:, :, :], ext["w2"]).then_inc(wg_in, 16)
                if i == 9:
                    sp.wait_ge(glu_done, 2 * C)
                    sp.dma_start(out["conv_p"], conv_in[:, :, SEQ:EXT_P]).then_inc(stored, 16)
                    for m in range(C):
                        sp.dma_start(out["conv_s"][:, m], sample_rows(m)[:, :, DT:]).then_inc(stored, 16)
                if (src, row) == ("w", W_OF["out"] + 3):
                    sp.wait_ge(tile_done, FIRST["out"] + 1)
                    sp.dma_start(ple_in[:, :, :], ext["p"][1]).then_inc(ple_loaded, 16)
                if (src, row) == ("cmp_pages", 0):
                    sp.wait_ge(tile_done, FIRST["gates"] + TT)
                    sp.dma_start(w1[:, :, :, :], ext["w1"]).then_inc(w1_in, 16)
                    sp.wait_ge(act_freed, FREED[FIRST["gates"] + TT - 1][1])
                    for e in range(2):
                        for later in range(2):
                            sp.dma_start(kv_pairs[64 * later:64 * later + 64, :, e:e + 3:2, 0:SEQ - later].rearrange(
                                             "p v g t -> p (v g) t"),
                                         kv_cmp[64 * e:64 * e + 64, :, later:SEQ]).then_inc(pairs_in, 16)
                    sp.dma_start(out["kv_cmp"], kv_cmp[:, :, :]).then_inc(kv_cmp_stored, 16)
                    sp.dma_start(out["v_tok"], v_tok[:, 0:PT, :]).then_inc(stored, 16)
                    sp.dma_start(out["v_tok_s"], v_tok[0:NS, PT, :]).then_inc(stored, 16)
                    sp.wait_ge(rot_done, 12)
                    sp.dma_start(out["k_rot"], k_rot[:, :, :]).then_inc(stored, 16)
            sp.wait_ge(kv_cmp_stored, 16)
            sp.wait_ge(win_stored[0], 16 * (NB // 2))
            sp.wait_ge(win_stored[1], 16 * (NB // 2))
            for m in range(C):
                sp.wait_ge(x_ready, 5 * C + m + 1)
                sp.dma_start(out["y"][:, m], x[:, m, :]).then_inc(stored, 16)
            sp.wait_ge(stored, 16 * (12 + C))

        @block.gpsimd
        def _(pool):
            nc.gpsimd.memset(conv_in[:, :, 0:TAPS - 1], 0.0).then_inc(pad_done, 1)
            nc.gpsimd.memset(ha[:, C * T:].bitcast(F32), 0.0).then_inc(pad_zero, 1)
            nc.gpsimd.memset(hb[:, C * T:].bitcast(F32), 0.0).then_inc(pad_zero, 1)

            def sample_products(m):
                pool.wait_ge(glu_done, 2 * m + 2)
                pool.wait_ge(state_in, 16 * C)
                if m > 0:
                    pool.wait_ge(sample_conv, m)
                es = sample_rows(m)
                rows = es[:, :, 0:TAPS]
                windows = bass.AP(tensor=rows.tensor, offset=rows.offset,
                                  ap=[rows.ap[0], rows.ap[1], [1, DT], [1, TAPS]])
                a = PAR["w_dw"][0] + TAPS * m
                taps = par[:, a:a + TAPS].rearrange("p (b t j) -> p b t j", b=1, t=1).to_broadcast((P, NB, DT, TAPS))
                nc.gpsimd.tensor_tensor(tap_prod, windows, taps, ALU.mult).then_inc(tap_products, 1)

            pool.wait_ge(consts_in, 32)

            def split_weights(first, last):
                for j in range(first, last):
                    k = PLACE[B_OF["w", j]][1]
                    pool.wait_ge(w_hi_ready, j + 1)
                    nc.gpsimd.tensor_tensor(w_lo[j % 2][:, :], w_raw[:, k, :], w_hi[j % 2][:, :].bitcast(F32),
                                            ALU.subtract).then_inc(w_ready, 1)

            pool.wait_ge(wg_hi_ready, 1)
            nc.gpsimd.tensor_tensor(wg_lo[:, :], w_gates[:, :], wg_hi[:, :].bitcast(F32), ALU.subtract).then_inc(wg_ready, 1)
            split_weights(0, 1)
            for m in range(C):
                split_weights(m + 1, m + 2)
                t = FIRST["pw1"] + 2 * m + 1
                pool.wait_ge(act_freed, FREED[t][1])
                e, es = conv_in[:, m, :], sample_rows(m)
                nc.gpsimd.tensor_tensor(e[:, TAPS - 1:EXT_P], val[:, m % 2, 0:SEQ], sig[:, m % 2, 0:SEQ],
                                        ALU.mult).then_inc(glu_done, 1)
                split_s = lambda a: a[:, m % 2, SEQ:].rearrange("p (b t) -> p b t", t=DT)
                nc.gpsimd.tensor_tensor(es[:, :, TAPS - 1:], split_s(val), split_s(sig), ALU.mult).then_inc(glu_done, 1)
                if m in (0, 3, 5, 7):
                    sample_products(m // 2)
            for m in range(4, C):
                sample_products(m)
            split_weights(C + 1, W_OF["out"])
            pool.wait_ge(act_freed, FREED[FIRST["gates"] + TT - 1][1])
            pool.dma_start(gate_rows, gates[0:NS, PT, :]).then_inc(gate_moved, 16)
            pool.wait_ge(gate_moved, 16)
            for n in range(KV * REP):
                g, r = n // REP, n % REP
                at = 3 * (2 * (g // 2 * REP + r) + g % 2)
                pool.dma_start(gate_s[n * DT:(n + 1) * DT, :, :],
                               gate_rows.rearrange("(b i) c -> i b c", i=DT)[:, :, at:at + 3]).then_inc(gate_moved, 16)
            pool.wait_ge(rot_done, 12)
            pool.wait_ge(dve_freed, FREED[FIRST["swap"] + 11][1])
            nc.gpsimd.memset(hid_p[:, :, :, :, NCP - 1:NCP], 0.0).then_inc(phid_zero, 1)
            nc.gpsimd.memset(v_cmp_p, 0.0).then_inc(bd_zero, 1)
            nc.gpsimd.memset(k_cmp_p[:, :, :, :], 0.0).then_inc(bd_zero, 1)
            pool.wait_ge(kv_cmp_stored, 16)
            pool.wait_ge(phid_mm, 2)
            nc.gpsimd.memset(qbd, 0.0).then_inc(qbd_zero, 1)
            for b in range(NB):
                for src in ("win_k", "win_v"):
                    i = B_OF[src, b]
                    pool.wait_ge(block_in[PLACE[i][1]], LOADED[i])
                pool.dma_start(out["win"][b].rearrange("p (c n) -> p c n", n=SEQ), window(b)).then_inc(win_stored[b % 2], 16)
            split_weights(W_OF["out"], len(W_END))

        @block.tensor
        def _(pe):
            def slot_free(t):
                if t >= 3:
                    who, n = FREED[t - 3]
                    pe.wait_ge(freed[who], n)

            def block_there(i):
                pe.wait_ge(block_in[PLACE[i][1]], LOADED[i])

            def dense(stage):
                name = INPUT[stage]
                hi, lo = split_input(name)
                for m in range(dict((s[0], s[1]) for s in STAGES)[stage]):
                    j = W_OF[stage] + m // 2
                    if m % 2 == 0:
                        pe.wait_ge(w_ready, j + 1)
                    t = FIRST[stage] + m
                    slot_free(t)
                    for a in range(2):
                        for k in range(C):
                            if m == 0 and a == 0:
                                pe.wait_ge(lo_ready, STAGED[name] + k + 1)
                            at = 2 * P * k + P * (m % 2)
                            wh, wl = w_hi[j % 2][:, at:at + P], w_lo[j % 2][:, at:at + P]
                            to = slot(t)[:, a, :]
                            nc.tensor.matmul(to, wh, chunk(hi, k, a * HT, HT), start=k == 0, stop=False)
                            nc.tensor.matmul(to, wh, chunk(lo, k, a * HT, HT), start=False, stop=False)
                            last = nc.tensor.matmul(to, wl, chunk(hi, k, a * HT, HT), start=False, stop=k == C - 1)
                    last.then_inc(tile_done, 1)

            def ple(layer):
                i = B_OF["ple", layer]
                block_there(i)
                pe.wait_ge(ple_loaded, 16 * (layer + 1))
                w = w_raw[:, PLACE[i][1], :].rearrange("p (k c) -> p k c", k=2)
                for m in range(C):
                    t = FIRST[f"ple{layer}"] + m
                    slot_free(t)
                    for a in range(2):
                        for k in range(2):
                            last = nc.tensor.matmul(slot(t)[:, a, :], w[:, k, m * P:(m + 1) * P],
                                                    ple_in[:, k, a * HT:(a + 1) * HT], start=k == 0, stop=k == 1)
                    last.then_inc(tile_done, 1)

            def mlp(layer):
                for n in range(Q4):
                    dense(f"up{layer}{n}")
                    dense(f"down{layer}{n}")

            def stats(n, extra=None):
                if n in ADDED:
                    pe.wait_ge(sq_added, adds(n + 1))
                    pe.wait_ge(rstd_ready, n)
                    for a in range(2):
                        last = nc.tensor.matmul(STAT[:, a, :], tab("mean"), rstd[:, a * HT:(a + 1) * HT],
                                                start=True, stop=True)
                    last.then_inc(sq_summed, 1)
                    return
                for m in range(C):
                    pe.wait_ge(sq_ready, C * n + m + 1)
                    if m == 0 and n >= 1:
                        pe.wait_ge(rstd_ready, n)
                    if m == 0 and n == 1:
                        pe.wait_ge(centred, C)
                    for a in range(2):
                        last = nc.tensor.matmul(STAT[:, a, :], tab("mean"), sq[:, (C * n + m) % 4, a * HT:(a + 1) * HT],
                                                start=m == 0, stop=m == C - 1)
                    last.then_inc(sq_summed, 1)

            pe.wait_ge(consts_in, 32)
            stats(0)
            dense("pw1")
            pe.wait_ge(rstd_ready, 1)
            for i in range(2):
                t = FIRST["taps"] + i
                slot_free(t)
                m = C - 2 + i
                pe.wait_ge(glu_done, 2 * m + 1)
                for j in range(TAPS):
                    n = TAPS * i + j
                    pe.wait_ge(diag_ready, n + 1)
                    last = nc.tensor.matmul(ps[:, 2 * (t % 3), :], diag[:, n % 18, :], conv_in[:, m, j:j + SEQ],
                                            start=j == 0, stop=j == TAPS - 1)
                    last.then_inc(diag_used if j < TAPS - 1 else tile_done, 1)
            for m in range(C):
                if m < C - 2:
                    pe.wait_ge(conv_done, m + 1)
                else:
                    pe.wait_ge(act_freed, FREED[FIRST["taps"] + m - (C - 2)][1])
                pe.wait_ge(sample_conv, m + 1)
                for a in range(2):
                    last = nc.tensor.matmul(STAT[:, a, :], tab("mean"), y[:, m, a * HT:(a + 1) * HT],
                                            start=m == 0, stop=m == C - 1)
            last.then_inc(mean_ready, 1)
            stats(1)
            dense("pw2")
            stats(2)
            stats(3)
            mlp(0)
            stats(4)
            ple(0)
            dense("gate0")
            stats(5)
            dense("q")
            dense("kv_cmp")
            dense("k_rot")
            pe.wait_ge(wg_ready, 1)
            pe.wait_ge(pad_zero, 2)
            for stage, part in (("v_tok", 0), ("v_tok", 1), ("gates", 0)):
                j = W_OF["v_tok"] + part
                n = 256 if stage == "v_tok" else 48
                wh, wl = (w_hi[j % 2], w_lo[j % 2]) if stage == "v_tok" else (wg_hi, wg_lo)
                if stage == "v_tok":
                    pe.wait_ge(w_ready, j + 1)
                for i in range(TT):
                    t = FIRST[stage] + TT * part + i
                    slot_free(t)
                    to = ps[:, 2 * (t % 3), 0:n]
                    for k in range(C):
                        nc.tensor.matmul(to, chunk(ha, k, i * P, P), wh[:, n * k:n * k + n], start=k == 0, stop=False)
                        nc.tensor.matmul(to, chunk(ha, k, i * P, P), wl[:, n * k:n * k + n], start=False, stop=False)
                        last = nc.tensor.matmul(to, chunk(hb, k, i * P, P), wh[:, n * k:n * k + n], start=False,
                                                stop=k == C - 1)
                    last.then_inc(tile_done, 1)
            for i in range(12):
                t = FIRST["swap"] + i
                src = q[:, i, :] if i < 8 else k_rot[:, i - 8, :]
                slot_free(t)
                pe.wait_ge(act_freed, FREED[FIRST["q"] + i if i < 8 else FIRST["k_rot"] + i - 8][1])
                for a in range(2):
                    last = nc.tensor.matmul(slot(t)[:, a, :], tab("swap"), src[:, a * HT:(a + 1) * HT],
                                            start=True, stop=True)
                last.then_inc(tile_done, 1)

            pe.wait_ge(w1_in, 16)
            lo, _ = PAR["pe"]
            for v in range(2):
                for j in range(16):
                    last = nc.tensor.matmul(ps[:, 7, v:v + 1], w1[:, v, j, :], par[:, lo + 16 * v + j:lo + 16 * v + j + 1],
                                            start=j == 0, stop=j == 15)
                last.then_inc(c_mm, 1)
            pe.wait_ge(pairs_in, 16 * 4)
            for v in range(2):
                for j in range(16):
                    last = nc.tensor.matmul(ps[:, 6, 128 * v:128 * v + 124].rearrange("p (g c) -> p g c", g=KV),
                                            w1[:, v, j, :], kv_pairs[:, v, :, 2 * j:2 * j + 16 * (NCP - 2) + 1:16],
                                            start=j == 0, stop=j == 15)
                last.then_inc(phid_mm, 1)
            pe.wait_ge(c_there, 1)
            pe.wait_ge(phid_ready, 2)
            for e in range(2):
                nc.tensor.matmul(ps[64 * e:64 * e + 64, 7, 0:64].rearrange("p (g c) -> p g c", g=2), w2[:, 0, :],
                                 hid_p[:, 0, e, :, :], start=True, stop=True)
            for g in range(2):
                for k in range(4):
                    last = nc.tensor.matmul(ps[32 * k:32 * k + 32, 7, 64 + 64 * g:128 + 64 * g],
                                            hid_p[:, 1, k % 2, g, :], w2[:, 1, :], start=True, stop=True)
            last.then_inc(pw2_mm, 1)

            def compress_out(u):
                b, v = u // 2, u % 2
                pe.wait_ge(hid_ready, u + 1)
                if u == 1:
                    pe.wait_ge(pw2_out, 2)
                if u >= 2:
                    pe.wait_ge(w2_out, u - 1)
                hid = hid_s[:, u % 2, :].rearrange("p (c g) -> p g c", g=KV)
                if v == 0:
                    for e in range(2):
                        last = nc.tensor.matmul(ps[64 * e:64 * e + 64, 6, 0:128].rearrange("p (g c) -> p g c", g=2),
                                                w2[:, 0, :], hid[:, e:e + 3:2, :], start=True, stop=True)
                else:
                    lo = 64 * (b % 2)
                    for g in range(KV):
                        last = nc.tensor.matmul(ps[lo:lo + 64, 7, 64 * g:64 * g + 64], hid[:, g, :], w2[:, 1, :],
                                                start=True, stop=True)
                last.then_inc(w2_mm, 1)

            slot_free(FIRST["out"] + 0)
            slot_free(FIRST["out"] + 1)
            slot_free(FIRST["out"] + 2)
            for u in range(2 * NB):
                b, v = u // 2, u % 2
                i = B_OF["cmp_pages", b]
                block_there(i)
                if u >= 3:
                    pe.wait_ge(hid_ab, u - 2)
                for half in range(2):
                    for j in range(8):
                        rhs = block_at(i, 0, BLK).rearrange("p (a n) -> p a n", a=PAGES)[:, :, 256 * v + 32 * j:256 * v + 32 * j + 32]
                        last = nc.tensor.matmul(ps[:, 2 * (u % 3) + half, 0:256], w1[:, v, 8 * half + j, :], rhs,
                                                start=j == 0, stop=j == 7)
                last.then_inc(cmp_mm, 1)
                if u >= 1:
                    compress_out(u - 1)
            compress_out(2 * NB - 1)

            pe.wait_ge(w2_out, 2 * NB - 1)
            pe.wait_ge(hid_ab, 2 * NB)
            pe.wait_ge(qbd_ready, 1)
            for b in range(NB):
                for g in range(2):
                    last = nc.tensor.matmul(ps[64 * g:64 * g + 64, 4, 64 * b:64 * b + 64],
                                            qbd[:, b, g, :, :].rearrange("p e m -> p (e m)"), k_cmp_s[:, b, g, :],
                                            start=True, stop=True)
            last.then_inc(sc_mm, 1)
            for n in range(PT):
                for c in range(C):
                    last = nc.tensor.matmul(ps[:, n, 2 * NCP * c:2 * NCP * (c + 1)], q[:, c, n * P:(n + 1) * P],
                                            k_cmp_p[:, c // 4, :, :].rearrange("p e c -> p (e c)"), start=True, stop=True)
                last.then_inc(sc_mm, 1)
            pe.wait_ge(pc_ready, 1)
            pe.wait_ge(w2_out, 2 * NB)
            nc.tensor.matmul(ps[:, 5, :], tab("same_q"), pc[:, 0, :], start=True, stop=True).then_inc(imp_mm, 1)
            for j in range(4):
                last = nc.tensor.transpose(ps[:, 6, 128 * j:128 * j + 128], pc[:, 0, 128 * j:128 * j + 128], tab("ident"))
            last.then_inc(ct_mm, 1)
            for n in range(PT):
                pe.wait_ge(pc_ready, n + 2)
                pe.wait_ge(sc_sub, n + 2)
                if n == 0:
                    pe.wait_ge(drop_ready, 1)
                pe.wait_ge(ct_out, n + 1)
                if n >= 1:
                    pe.wait_ge(co_read, n)
                for j in range(4):
                    last = nc.tensor.transpose(ps[:, 4 + n % 2, 128 * j:128 * j + 128], pc[:, n + 1, 128 * j:128 * j + 128],
                                               tab("ident"))
                last.then_inc(ct_mm, 1)
                pe.wait_ge(ct_out, n + 2)
                for j in range(4):
                    last = nc.tensor.matmul(ps[:, 6 + j // 2, 256 * (j % 2):256 * (j % 2) + 256], pc_t_p[:, j, :],
                                            v_cmp_p[:, j // 2, :], start=True, stop=True)
                last.then_inc(co_mm, 1)

            def scores_s(b):
                i = B_OF["sel_pages", b]
                block_there(i)
                block_there(B_OF["win_k", b])
                if b >= 1:
                    pe.wait_ge(s_read, b)
                    pe.wait_ge(s_win, b)
                sel = block_at(i, 0, BLK).rearrange("p (a n) -> p a n", a=PAGES)
                win = window(b)
                for g in range(2):
                    part = slice(64 * g, 64 * g + 64)
                    qq = qbd[:, b, g, :, :].rearrange("p e m -> p (e m)")
                    for a in range(2):
                        nc.tensor.matmul(ps[part, a, :], qq, sel[:, 4 * a:4 * a + 4, P * g:P * g + P], start=True, stop=True)
                    nc.tensor.matmul(ps[part, 2, :], qq, win[:, g, :], start=True, stop=True)
                    nc.tensor.matmul(ps[part, 3, 0:NS], qq, k_rot[:, g, SEQ:T], start=True, stop=True)
                    last = nc.tensor.matmul(ps[part, 3, NS:2 * NS], qq, k_rot[:, 2 + g, SEQ:T], start=True, stop=True)
                last.then_inc(s_mm, 1)

            def t_slot(n):
                if n >= 2:
                    b, k = [(b, k) for b in range(NB + 1) for k in range(5) if (b, k) != (0, 4)][n - 2]
                    if k == 4:
                        pe.wait_ge(t_fin, b)
                    else:
                        pe.wait_ge(t_out, 4 * b + k + 1)
                return ps[:, 4 + n % 2, :]

            def finish_s(b, n):
                to = t_slot(n)
                pe.wait_ge(acc_ready, b + 1)
                for g in range(2):
                    last = nc.tensor.transpose(to[:, 128 * g:128 * g + 128], acc_s[:, b % 2, 128 * g:128 * g + 128], tab("ident"))
                last.then_inc(t_mm, 1)

            pe.wait_ge(co_read, PT)
            pe.wait_ge(qbd_ready, 2)
            pe.wait_ge(rot_done, 12)
            scores_s(0)
            for b in range(NB):
                if b + 1 < NB:
                    scores_s(b + 1)
                i = B_OF["sel_pages", b]
                sel = block_at(i, 0, BLK).rearrange("p (a n) -> p a n", a=PAGES)[:, :, 256:512]
                win = window(b)
                pp = p_s[:, b % 2, :]
                pe.wait_ge(s_exp, b + 1)
                for k, tiles in enumerate(([0, 128, 256, 384], [512, 640, 768, 896], [1088, 1216, 1344, 1472], [1024, 1600])):
                    to = t_slot(t_group(b, k))
                    w = P if k < 3 else NS
                    for j, at in enumerate(tiles):
                        last = nc.tensor.transpose(to[0:w, 128 * j:128 * j + 128], pp[:, at:at + w], tab("ident"))
                    last.then_inc(t_mm, 1)
                if b >= 1:
                    finish_s(b - 1, t_group(b, 4))
                if b >= 1:
                    pe.wait_ge(o_read, b)
                pe.wait_ge(t_out, 4 * b + 4)
                block_there(B_OF["win_v", b])
                for j in range(8):
                    nc.tensor.matmul(ps[:, 6, 0:256], pt_s[:, 128 * j:128 * j + 128], sel[:, j, :], start=j == 0, stop=False)
                nc.tensor.matmul(ps[:, 6, 0:256], pt_s[0:NS, 1536:1664], v_tok[0:NS, PT, 0:256], start=False, stop=True)
                for j in range(4):
                    nc.tensor.matmul(ps[:, 6, 256:512], pt_s[:, 1024 + 128 * j:1152 + 128 * j],
                                     win[:, 2 + j // 2, 256 * (j % 2):256 * (j % 2) + 256],
                                     start=j == 0, stop=False)
                nc.tensor.matmul(ps[:, 6, 256:512], pt_s[0:NS, 1664:1792], v_tok[0:NS, PT, 256:512], start=False, stop=True)
                half = slice(64 * (b % 2), 64 * (b % 2) + 64)
                nc.tensor.matmul(ps[:, 7, 0:256], pc_t_s[half, b // 2, :], v_cmp_s[half, b // 2, :],
                                 start=True, stop=True).then_inc(o_mm, 1)
            finish_s(NB - 1, t_group(NB, 0))

            items = [(n, c, e, r) for n in range(PT) for c in range(C) for e in range(2) for r in range(2)]

            def p_scores(i):
                n, c, e, r = items[i]
                if i >= 4:
                    pe.wait_ge(p_exp, i - 3)
                part = slice(64 * e, 64 * e + 64)
                nc.tensor.matmul(ps[:, i % 4, 0:(n + 1) * P], q_rot[part, c, n * P:(n + 1) * P],
                                 k_rot[part, 2 * r + c // 4, 0:(n + 1) * P], start=True, stop=True).then_inc(p_mm, 1)

            def p_transpose(i):
                n = items[i][0]
                pe.wait_ge(p_exp, i + 1)
                if i >= 2:
                    pe.wait_ge(pt_out, i - 1)
                for j in range(n + 1):
                    last = nc.tensor.transpose(ps[:, 4 + i % 2, 128 * j:128 * j + 128], p_p[:, i % 4, 128 * j:128 * j + 128],
                                               tab("ident"))
                last.then_inc(pt_mm, 1)

            def p_out(i):
                n, c, e, r = items[i]
                pe.wait_ge(pt_out, i + 1)
                if i >= 2:
                    pe.wait_ge(po_read, i - 1)
                at = 256 * r + 64 * (2 * (c // 4) + e)
                for j in range(n + 1):
                    last = nc.tensor.matmul(ps[:, 6 + i % 2, 0:HD], pt_p[:, i % 2, 128 * j:128 * j + 128],
                                            v_tok[:, j, at:at + HD], start=j == 0, stop=j == n)
                last.then_inc(po_mm, 1)

            pe.wait_ge(t_fin, NB)
            N = len(items)
            p_scores(0)
            p_scores(1)
            for i in range(N):
                if i + 2 < N:
                    p_scores(i + 2)
                p_transpose(i)
                if i >= 1:
                    p_out(i - 1)
            p_out(N - 1)
            for n in range(PT):
                for k in range(2):
                    i = 2 * n + k
                    if n == 0 and k == 0:
                        pe.wait_ge(po_read, N)
                    if i >= 2:
                        pe.wait_ge(ft_out, i - 1)
                    for c in range(4):
                        last = nc.tensor.transpose(ps[:, 4 + i % 2, 128 * c:128 * c + 128],
                                                   acc[:, n, 512 * k + 128 * c:512 * k + 128 * c + 128], tab("ident"))
                    last.then_inc(ft_mm, 1)

            dense("out")
            stats(6)
            stats(7)
            mlp(1)
            stats(8)
            ple(1)
            dense("gate1")

        @block.scalar
        def _(act):
            def split_weight(j):
                i = B_OF["w", j]
                k = PLACE[i][1]
                if j >= 2:
                    act.wait_ge(tile_done, W_END[j - 2])
                act.wait_ge(block_in[k], LOADED[i])
                nc.scalar.activation(w_hi[j % 2][:, :], w_raw[:, k, :], ACT.Copy).then_inc(w_hi_ready, 1)

            def tile(stage, m):
                t = FIRST[stage] + m
                per = TT if stage == "v_tok" else 2
                if stage in W_OF and m % per == 0:
                    j = W_OF[stage] + m // per + 1
                    if j != W_OF["out"] and j < len(W_END):
                        split_weight(j)
                act.wait_ge(tile_done, t + 1)
                return slot(t)

            def hi_part(name, k, src, src_ready=None):
                hi, _ = split_input(name)
                if src_ready is not None:
                    act.wait_ge(*src_ready)
                nc.scalar.activation(chunk(hi, k), src, ACT.Copy).then_inc(hi_ready, 1)

            def raw(name, k):
                i = STAGED[name] + k
                return sq[:, i % 4, :]

            def norm_hi(name, count, last_reader=None):
                if last_reader is not None:
                    act.wait_ge(tile_done, last_reader)
                for k in range(C):
                    hi_part(name, k, raw(name, k), (raw_ready, count + k + 1))

            def square(n, m, src):
                i = C * n + m
                if i >= 4:
                    was_n, was_m = (i - 4) // C, (i - 4) % C
                    if was_n in ADDED:
                        act.wait_ge(sq_added, adds(was_n) + max(was_m, 1))
                    else:
                        act.wait_ge(sq_summed, summed(was_n) + was_m + 1)
                dst = sq[:, i % 4, :]
                if len(src.shape) == 3:
                    dst = halves(dst)
                nc.scalar.activation(dst, src, ACT.Square).then_inc(sq_ready, 1)

            def std(n):
                act.wait_ge(sq_summed, summed(n + 1))
                nc.scalar.activation(halves(rstd[:, :]), STAT, ACT.Sqrt, bias=tab("eps")).then_inc(std_ready, 1)

            def square_x(n, update):
                for m in range(C):
                    act.wait_ge(x_ready, C * update + m + 1)
                    square(n, m, x[:, m, :])
                std(n)

            def to_mix(stage, n, bias=None):
                for m in range(C):
                    p = tile(stage, m)
                    if bias is None:
                        nc.scalar.activation(halves(mix[:, m, :]), p, ACT.Copy).then_inc(act_freed, 1)
                    else:
                        nc.scalar.activation(halves(mix[:, m, :]), p, ACT.Identity, bias=pcol(bias, m)).then_inc(act_freed, 1)
                    act.wait_ge(act_freed, FREED[FIRST[stage] + m][1])
                    square(n, m, mix[:, m, :])
                std(n)

            def mlp(layer, norm):
                for n in range(Q4):
                    name = f"hid{layer}{n}"
                    for m in range(C):
                        p = tile(f"up{layer}{n}", m)
                        i = STAGED[name] + m
                        act.wait_ge(lo_ready, i - 3)
                        nc.scalar.activation(halves(raw(name, m)), p, ACT.Relu).then_inc(act_freed, 1)
                        hi_part(name, m, raw(name, m), (raw_ready, RAW_OF[name] + m + 1))
                    for m in range(C):
                        p = tile(f"down{layer}{n}", m)
                        if n == 0:
                            nc.scalar.activation(halves(mix[:, m, :]), p, ACT.Copy).then_inc(act_freed, 1)
                        if n == Q4 - 1:
                            act.wait_ge(dve_freed, FREED[FIRST[f"down{layer}{n}"] + m][1])
                            square(norm, m, mix[:, m, :])
                std(norm)

            def x_hi(name, update):
                for k in range(C):
                    hi_part(name, k, x[:, k, :], (x_ready, C * update + k + 1))

            def ple(layer):
                for m in range(C):
                    p = tile(f"ple{layer}", m)
                    nc.scalar.activation(halves(emb[:, m, :]), p, ACT.Copy).then_inc(act_freed, 1)

            def gate(layer):
                for m in range(C):
                    p = tile(f"gate{layer}", m)
                    nc.scalar.activation(halves(mix[:, m, :]), p, ACT.Sigmoid,
                                         bias=pcol("b_ple", C * layer + m)).then_inc(act_freed, 1)

            act.wait_ge(consts_in, 32)
            for m in range(C):
                act.wait_ge(x_in[m // 2], 16)
                square(0, m, x[:, m, :])
            std(0)
            act.wait_ge(wg_in, 32)
            nc.scalar.activation(wg_hi[:, :], w_gates[:, :], ACT.Copy).then_inc(wg_hi_ready, 1)
            split_weight(0)
            norm_hi("conv", 0)
            def diagonals(first, last):
                for n in range(first, last):
                    if n >= 18:
                        used = n - 17
                        act.wait_ge(diag_used, used - (used >= TAPS))
                        if used == TAPS:
                            act.wait_ge(tile_done, FIRST["taps"] + 1)
                    nc.scalar.activation(diag[:, n % 18, :], tab("ident"), ACT.Copy,
                                         scale=pcol("w_dw", TAPS * (C - 2) + n)).then_inc(diag_ready, 1)

            for m in range(C):
                p = tile("pw1", 2 * m)
                if m >= 2:
                    act.wait_ge(glu_done, 2 * m - 2)
                nc.scalar.activation(halves(sig[:, m % 2, :]), p, ACT.Sigmoid,
                                     bias=pcol("b_pw1", 2 * m)).then_inc(act_freed, 1)
                p = tile("pw1", 2 * m + 1)
                nc.scalar.activation(halves(val[:, m % 2, :]), p, ACT.Identity,
                                     bias=pcol("b_pw1", 2 * m + 1)).then_inc(act_freed, 1)
                if m == C - 2:
                    act.wait_ge(lo_ready, C)
                    diagonals(0, 18)
            diagonals(18, 2 * TAPS)
            for i in range(2):
                t = FIRST["taps"] + i
                act.wait_ge(tile_done, t + 1)
                nc.scalar.activation(y[:, C - 2 + i, 0:SEQ], ps[:, 2 * (t % 3), :], ACT.Identity,
                                     bias=pcol("b_dw", C - 2 + i)).then_inc(act_freed, 1)
            for m in range(C):
                act.wait_ge(centred, m + 1)
                square(1, m, y[:, m, :])
            std(1)
            for m in range(C):
                act.wait_ge(normed, m + 1)
                i = STAGED["silu"] + m
                act.wait_ge(lo_ready, i - 3)
                if m == 0:
                    act.wait_ge(sq_summed, 2 * C)
                nc.scalar.activation(raw("silu", m), y[:, m, :], ACT.Silu, scale=pcol("ln_g", m),
                                     bias=pcol("ln_b", m)).then_inc(silu_done, 1)
                hi_part("silu", m, raw("silu", m), (silu_done, m + 1))
            to_mix("pw2", 2, "b_pw2")
            square_x(3, 0)
            norm_hi("mlp0", RAW_OF["mlp0"], FIRST["up00"])
            mlp(0, 4)
            ple(0)
            x_hi("x0", 1)
            gate(0)
            square_x(5, 2)
            norm_hi("nsa", RAW_OF["nsa"], FIRST["ple0"])
            for stage, dst in (("q", q), ("kv_cmp", kv_cmp), ("k_rot", k_rot)):
                for m in range(C if stage == "q" else 4):
                    p = tile(stage, m)
                    nc.scalar.activation(halves(dst[:, m, :]), p, ACT.Copy,
                                         scale=SCALE if stage == "q" else 1.0).then_inc(act_freed, 1)
            for n in range(2 * TT):
                i, part = n % TT, n // TT
                rows = P if i < PT else NS
                t = FIRST["v_tok"] + n
                tile("v_tok", n)
                nc.scalar.activation(v_tok[0:rows, i, 256 * part:256 * part + 256], ps[0:rows, 2 * (t % 3), 0:256],
                                     ACT.Copy).then_inc(act_freed, 1)
            for i in range(TT):
                rows = P if i < PT else NS
                t = FIRST["gates"] + i
                act.wait_ge(tile_done, t + 1)
                nc.scalar.activation(gates[0:rows, i, :], ps[0:rows, 2 * (t % 3), 0:48], ACT.Sigmoid).then_inc(act_freed, 1)

            act.wait_ge(c_mm, 2)
            nc.scalar.activation(c_vec[:, :], ps[:, 7, 0:2], ACT.Copy).then_inc(c_there, 1)
            act.wait_ge(c_there, 1)
            act.wait_ge(phid_zero, 1)
            act.wait_ge(phid_mm, 2)
            for v in range(2):
                nc.scalar.activation(hid_p[:, v, :, :, 0:NCP - 1].rearrange("p e g c -> p g e c"),
                                     ps[:, 6, 128 * v:128 * v + 124].rearrange("p (g e c) -> p g e c", g=2, e=2),
                                     ACT.Silu, bias=c_vec[:, v:v + 1]).then_inc(phid_ready, 1)
            act.wait_ge(pw2_mm, 1)
            act.wait_ge(bd_zero, 2)
            for e in range(2):
                part = slice(64 * e, 64 * e + 64)
                last = nc.scalar.activation(k_cmp_p[part, :, e, :], ps[part, 7, 0:64].rearrange("p (g c) -> p g c", g=2),
                                            ACT.Copy)
            last.then_inc(pw2_out, 1)
            for k in range(4):
                last = nc.scalar.activation(v_cmp_p[32 * k:32 * k + 32, :, 64 * k:64 * k + 64],
                                            ps[32 * k:32 * k + 32, 7, 64:192].rearrange("p (g f) -> p g f", g=2), ACT.Copy)
            last.then_inc(pw2_out, 1)
            act.wait_ge(rot_done, 12)

            def hid_silu(u):
                act.wait_ge(hid_ab, u + 1)
                nc.scalar.activation(hid_s[:, u % 2, :], hid_s[:, u % 2, :], ACT.Silu).then_inc(hid_ready, 1)

            for u in range(2 * NB):
                act.wait_ge(cmp_mm, u + 1)
                if u >= 2:
                    act.wait_ge(w2_mm, u - 1)
                nc.scalar.activation(hid_s[:, u % 2, :], ps[:, 2 * (u % 3), 0:256], ACT.Identity,
                                     bias=c_vec[:, u % 2:u % 2 + 1]).then_inc(hid_a, 1)
                hid_silu(u)

            for n in range(5):
                act.wait_ge(sc_sub, n + 1)
                nc.scalar.activation(pc[:, n, :], pc[:, n, :], ACT.Exp).then_inc(c_exp, 1)
            act.wait_ge(ct_mm, 1)
            nc.scalar.activation(pc_t_s, ps[:, 6, :].rearrange("p (j t) -> p j t", j=4), ACT.Copy).then_inc(ct_out, 1)
            act.wait_ge(w2_mm, 2 * NB)
            for n in range(PT):
                act.wait_ge(ct_mm, n + 2)
                if n >= 1:
                    act.wait_ge(co_mm, n)
                nc.scalar.activation(pc_t_p, ps[:, 4 + n % 2, :].rearrange("p (j t) -> p j t", j=4),
                                     ACT.Copy).then_inc(ct_out, 1)

            def window_out(b):
                act.wait_ge(s_mm, b + 1)
                if b == 0:
                    act.wait_ge(co_mm, PT)
                if b >= 2:
                    act.wait_ge(t_mm, t_group(b - 2, 3) + 1)
                nc.scalar.activation(p_s[:, b % 2, 1088:1600], ps[:, 2, :], ACT.Copy).then_inc(s_win, 1)

            act.wait_ge(co_mm, PT)
            window_out(0)
            for b in range(NB):
                pp = p_s[:, b % 2, :]
                act.wait_ge(s_max, 2 * b + 1)
                nc.scalar.activation(pp[:, 0:1088], pp[:, 0:1088], ACT.Exp, bias=stat_s[:, b, 0:1],
                                     accum_out=stat_s[:, b, 2:3])
                act.wait_ge(s_max, 2 * b + 2)
                nc.scalar.activation(pp[:, 1088:1664], pp[:, 1088:1664], ACT.Exp, bias=stat_s[:, b, 1:2],
                                     accum_out=stat_s[:, b, 3:4]).then_inc(s_exp, 1)
                if b + 1 < NB:
                    window_out(b + 1)
                for k in range(4):
                    act.wait_ge(t_mm, t_group(b, k) + 1)
                    if k == 0 and b >= 1:
                        act.wait_ge(o_mm, b)
                    w, n = (P, 512) if k < 3 else (NS, 256)
                    nc.scalar.activation(pt_s[0:w, 512 * k:512 * k + n], ps[0:w, 4 + t_group(b, k) % 2, 0:n],
                                         ACT.Copy).then_inc(t_out, 1)

            items = [(n, c, e, r) for n in range(PT) for c in range(C) for e in range(2) for r in range(2)]

            def p_move(i):
                n = items[i][0]
                act.wait_ge(pt_mm, i + 1)
                if i >= 2:
                    act.wait_ge(po_mm, i - 1)
                nc.scalar.activation(pt_p[:, i % 2, 0:(n + 1) * P], ps[:, 4 + i % 2, 0:(n + 1) * P],
                                     ACT.Copy).then_inc(pt_out, 1)

            act.wait_ge(t_mm, 5 * NB)
            for i, (n, c, e, r) in enumerate(items):
                act.wait_ge(p_max, i + 1)
                if i >= 4:
                    act.wait_ge(pt_mm, i - 3)
                    act.wait_ge(po_read, i - 3)
                nc.scalar.activation(p_p[:, i % 4, 0:(n + 1) * P], ps[:, i % 4, 0:(n + 1) * P], ACT.Exp,
                                     bias=nmax_p[:, i % 8:i % 8 + 1], accum_out=sum_p[:, i % 8:i % 8 + 1]).then_inc(p_exp, 1)
                if i >= 1:
                    p_move(i - 1)
            p_move(len(items) - 1)
            act.wait_ge(win_stored[0], 16 * (NB // 2))
            act.wait_ge(win_stored[1], 16 * (NB // 2))
            for i in range(2 * PT):
                n, k = i // 2, i % 2
                act.wait_ge(ft_mm, i + 1)
                nc.scalar.activation(attn_t[:, 4 * k:4 * k + 4, n * P:(n + 1) * P],
                                     ps[:, 4 + i % 2, :].rearrange("p (c t) -> p c t", c=4), ACT.Copy).then_inc(ft_out, 1)

            act.wait_ge(ft_out, 2 * PT)
            act.wait_ge(ft_mm, 2 * PT)
            for m in range(C):
                hi_part("attn", m, attn_t[:, m, :], (t_fin, NB))
            act.wait_ge(o_mm, NB)
            split_weight(W_OF["out"])
            to_mix("out", 6)
            square_x(7, 3)
            norm_hi("mlp1", RAW_OF["mlp1"], FIRST["up10"])
            mlp(1, 8)
            ple(1)
            x_hi("x1", 4)
            gate(1)

        @block.vector
        def _(dve):
            steps = [0]

            def step(ins):
                steps[0] += 1
                ins.then_inc(dve_step, 1)
                return steps[0]

            def after(n):
                dve.wait_ge(dve_step, n)

            def get_rstd(n):
                dve.wait_ge(std_ready, n + 1)
                nc.vector.reciprocal(rstd[:, :], rstd[:, :]).then_inc(rstd_ready, 1)
                dve.wait_ge(rstd_ready, n + 1)

            def lo_part(name, k, src):
                hi, lo = split_input(name)
                dve.wait_ge(hi_ready, STAGED[name] + k + 1)
                nc.vector.tensor_tensor(chunk(lo, k), src, chunk(hi, k).bitcast(F32), ALU.subtract).then_inc(lo_ready, 1)

            def raw(name, k):
                return sq[:, (STAGED[name] + k) % 4, :]

            def add_square(n, m):
                if m == 0:
                    return
                dve.wait_ge(sq_ready, C * n + m + 1)
                if m > 1:
                    dve.wait_ge(sq_added, adds(n) + m - 1)
                so_far = sq[:, C * n % 4, :] if m == 1 else rstd[:, :]
                nc.vector.tensor_tensor(rstd[:, :], so_far, sq[:, (C * n + m) % 4, :], ALU.add).then_inc(sq_added, 1)

            def pre_norm(n, g, name):
                get_rstd(n)
                for m in range(C + 1):
                    if m < C:
                        nc.vector.scalar_tensor_tensor(raw(name, m), x[:, m, :], pcol("norm_g", C * g + m), rstd[:, :],
                                                       ALU.mult, ALU.mult).then_inc(raw_ready, 1)
                    if m >= 1:
                        lo_part(name, m - 1, raw(name, m - 1))

            def mlp(layer, norm):
                for n in range(Q4):
                    name = f"hid{layer}{n}"
                    for m in range(C):
                        dve.wait_ge(act_freed, FREED[FIRST[f"up{layer}{n}"] + m][1])
                        r = raw(name, m)
                        nc.vector.tensor_tensor(r, r, r, ALU.mult).then_inc(raw_ready, 1)
                        lo_part(name, m, r)
                    for m in range(C if n else 0):
                        if n == Q4 - 1 and m >= 1:
                            add_square(norm, m - 1)
                        t = FIRST[f"down{layer}{n}"] + m
                        dve.wait_ge(tile_done, t + 1)
                        dve.wait_ge(act_freed, FREED[FIRST[f"down{layer}0"] + m][1])
                        if n >= 2:
                            dve.wait_ge(dve_freed, FREED[FIRST[f"down{layer}{n - 1}"] + m][1])
                        nc.vector.tensor_tensor(halves(mix[:, m, :]), slot(t), halves(mix[:, m, :]),
                                                ALU.add).then_inc(dve_freed, 1)
                add_square(norm, C - 1)

            def post_norm(n, g):
                get_rstd(n)
                done = []
                for m in range(C + 1):
                    if m < C:
                        done.append(step(nc.vector.scalar_tensor_tensor(
                            mix[:, m, :], mix[:, m, :], pcol("norm_g", C * g + m), rstd[:, :], ALU.mult, ALU.mult)))
                    if m >= 1:
                        after(done[m - 1])
                        nc.vector.tensor_tensor(x[:, m - 1, :], x[:, m - 1, :], mix[:, m - 1, :],
                                                ALU.add).then_inc(x_ready, 1)

            def ple(layer):
                for m in range(C):
                    dve.wait_ge(act_freed, FREED[FIRST[f"gate{layer}"] + m][1])
                    after(step(nc.vector.tensor_tensor(mix[:, m, :], mix[:, m, :], emb[:, m, :], ALU.mult)))
                    nc.vector.tensor_tensor(x[:, m, :], x[:, m, :], mix[:, m, :], ALU.add).then_inc(x_ready, 1)

            dve.wait_ge(consts_in, 32)
            for i in range(4):
                dve.wait_ge(x_in[i], 16)
            pre_norm(0, 0, "conv")
            dve.wait_ge(pad_done, 1)
            def conv_samples(m):
                dve.wait_ge(tap_products, m + 1)
                ys = y[:, m, SEQ:].rearrange("p (b t) -> p b t", t=DT)
                after(step(nc.vector.tensor_reduce(ys, tap_prod, AX.X, ALU.add)))
                nc.vector.tensor_scalar(ys, ys, pcol("b_dw", m), None, ALU.add).then_inc(sample_conv, 1)

            done = 0
            for m in range(C - 2):
                dve.wait_ge(glu_done, 2 * m + 1)
                yp = y[:, m, 0:SEQ]
                on_way = []
                for j in range(TAPS):
                    w, e = pcol("w_dw", TAPS * m + j), conv_in[:, m, j:j + SEQ]
                    to = odd_taps if j % 2 else yp
                    if j >= 2:
                        after(on_way[j - 2])
                    if j == 0:
                        on_way.append(step(nc.vector.tensor_scalar(to, e, w, pcol("b_dw", m), ALU.mult, ALU.add)))
                    elif j == 1:
                        on_way.append(step(nc.vector.tensor_scalar(to, e, w, None, ALU.mult)))
                    else:
                        on_way.append(step(nc.vector.scalar_tensor_tensor(to, e, w, to, ALU.mult, ALU.add)))
                    if m >= 3 and j == TAPS // 2:
                        conv_samples(done)
                        done += 1
                after(on_way[-1])
                nc.vector.tensor_tensor(yp, yp, odd_taps, ALU.add).then_inc(conv_done, 1)
                if m < C - 3:
                    conv_samples(done)
                    done += 1
            assert done == C
            dve.wait_ge(mean_ready, 1)
            for m in range(C):
                nc.vector.tensor_tensor(halves(y[:, m, :]), halves(y[:, m, :]), STAT, ALU.subtract).then_inc(centred, 1)
            get_rstd(1)
            for m in range(C):
                nc.vector.tensor_tensor(y[:, m, :], y[:, m, :], rstd[:, :], ALU.mult).then_inc(normed, 1)
            for m in range(C):
                dve.wait_ge(silu_done, m + 1)
                lo_part("silu", m, raw("silu", m))
            for m in range(C):
                add_square(2, m)
            post_norm(2, 1)
            pre_norm(3, 2, "mlp0")
            mlp(0, 4)
            post_norm(4, 3)
            for m in range(C):
                lo_part("x0", m, x[:, m, :])
            ple(0)
            pre_norm(5, 4, "nsa")
            for i in range(12):
                t = FIRST["swap"] + i
                before = q[:, i, :] if i < 8 else k_rot[:, i - 8, :]
                dst = q_rot[:, i, :] if i < 8 else before
                dve.wait_ge(tile_done, t + 1)
                nc.vector.tensor_tensor(halves(rope_tmp[:, i % 4, :]), slot(t), halves(tab("sin")), ALU.mult).then_inc(dve_freed, 1)
                k = step(nc.vector.tensor_tensor(dst, before, tab("cos"), ALU.mult))
                dve.wait_ge(dve_freed, FREED[t][1])
                after(k)
                nc.vector.tensor_tensor(dst, dst, rope_tmp[:, i % 4, :], ALU.add).then_inc(rot_done, 1)

            def chain(ins):
                after(step(ins))

            for u in range(2 * NB):
                b, v = u // 2, u % 2
                dve.wait_ge(hid_a, u + 1)
                nc.vector.tensor_tensor(hid_s[:, u % 2, 0:252], ps[:, 2 * (u % 3) + 1, 4:256], hid_s[:, u % 2, 0:252],
                                        ALU.add).then_inc(hid_ab, 1)
                for w in ([u - 1] if u >= 1 else []) + ([u] if u == 2 * NB - 1 else []):
                    b, v = w // 2, w % 2
                    dve.wait_ge(w2_mm, w + 1)
                    if v == 0:
                        nc.vector.tensor_copy(k_cmp_s[:, b, :, :].rearrange("p g c -> p (g c)"), ps[:, 6, 0:128]).then_inc(w2_out, 1)
                    else:
                        half = slice(64 * (b % 2), 64 * (b % 2) + 64)
                        nc.vector.tensor_copy(v_cmp_s[half, b // 2, :], ps[half, 7, 0:256]).then_inc(w2_out, 1)

            def block_queries(src):
                for g in range(2):
                    for e in range(2):
                        part = slice(64 * e, 64 * e + 64)
                        last = nc.vector.tensor_copy(
                            qbd[part, :, g, e, :].rearrange("p b (r i) -> p b r i", r=REP),
                            src[part, 4 * g:4 * g + 4, SEQ:T].rearrange("p r (b i) -> p b r i", b=NB))
                last.then_inc(qbd_ready, 1)

            dve.wait_ge(qbd_zero, 1)
            block_queries(q)

            dve.wait_ge(sc_mm, 5)
            def groups(n):
                k, w, at = (NB, NCS, 0) if n == 0 else (16, NCP, 8 + 16 * (n - 1))
                return (pc[:, n, :].rearrange("p (k w) -> p k w", k=k), cmax[:, at:at + k].rearrange("p (k o) -> p k o", o=1),
                        csum[:, at:at + k].rearrange("p (k o) -> p k o", o=1), (P, k, w))

            for n in range(5):
                pr, mx, _, shape = groups(n)
                if n == 0:
                    sc = ps[:, 4, :].rearrange("p (k w) -> p k w", k=NB)
                    chain(nc.vector.tensor_copy(pr, sc))
                    chain(nc.vector.memset(pr[:, :, NCS - 1:NCS], NEG))
                else:
                    a = CON["cmp_add"][0] + NCP * (n - 1)
                    m = con[:, a:a + NCP].rearrange("p (o w) -> p o w", o=1).to_broadcast(shape)
                    chain(nc.vector.tensor_tensor(pr, ps[:, n - 1, :].rearrange("p (k w) -> p k w", k=16), m, ALU.add))
                chain(nc.vector.tensor_reduce(mx, pr, AX.X, ALU.max))
                nc.vector.tensor_tensor(pr, pr, mx.to_broadcast(shape), ALU.subtract).then_inc(sc_sub, 1)
            for n in range(5):
                pr, mx, sm, shape = groups(n)
                dve.wait_ge(c_exp, n + 1)
                chain(nc.vector.tensor_reduce(sm, pr, AX.X, ALU.add))
                chain(nc.vector.reciprocal(sm, sm))
                if n == 0:
                    nc.vector.tensor_tensor(pr, pr, sm.to_broadcast(shape), ALU.mult).then_inc(pc_ready, 1)
                else:
                    g = gates[:, n - 1, :].rearrange("p (k o) -> p k o", o=3)[:, :, 0:1]
                    chain(nc.vector.tensor_tensor(sm, sm, g, ALU.mult))
                    a = CON["cmp_mul"][0] + NCP * (n - 1)
                    m = con[:, a:a + NCP].rearrange("p (o w) -> p o w", o=1).to_broadcast(shape)
                    nc.vector.tensor_tensor(pr, pr, m, ALU.mult).then_inc(pc_ready, 1)
                if n == 0:
                    dve.wait_ge(imp_mm, 1)
                    both = ps[:, 5, :].rearrange("p (b s w) -> p b s w", b=NB, w=4)
                    chain(nc.vector.tensor_reduce(imp.rearrange("p b (s o) -> p b s o", o=1), both, AX.X, ALU.add))
                    chain(nc.vector.tensor_tensor(imp[:, :, 1:16], both[:, :, 0:15, 3], imp[:, :, 1:16], ALU.add))
                    lo = least[:, 0:8].rearrange("p (b o) -> p b o", o=1)
                    hi = least[:, 8:16].rearrange("p (b o) -> p b o", o=1)
                    no = tab("block_no").rearrange("p (o s) -> p o s", o=1).to_broadcast((P, NB, 16))
                    chain(nc.vector.tensor_reduce(lo, imp[:, :, 1:15], AX.X, ALU.min))
                    chain(nc.vector.tensor_tensor(eq[:, :, 1:15], imp[:, :, 1:15], lo.to_broadcast((P, NB, 14)), ALU.is_equal))
                    chain(nc.vector.tensor_tensor(eq[:, :, 1:15], eq[:, :, 1:15], no[:, :, 1:15], ALU.mult))
                    chain(nc.vector.tensor_reduce(hi, eq[:, :, 1:15], AX.X, ALU.max))
                    chain(nc.vector.tensor_tensor(drop, no, hi.to_broadcast((P, NB, 16)), ALU.is_equal))
                    nc.vector.tensor_scalar(drop, drop, NEG, None, ALU.mult).then_inc(drop_ready, 1)
            for n in range(PT):
                dve.wait_ge(co_mm, n + 1)
                _, _, sm, _ = groups(n + 1)
                nc.vector.tensor_tensor(acc[:, n, :].rearrange("p (k d) -> p k d", d=HD),
                                        ps[:, 6:8, :].rearrange("p a (k d) -> p (a k) d", d=HD),
                                        sm.to_broadcast((P, 16, HD)), ALU.mult).then_inc(co_read, 1)
            block_queries(q_rot)

            def scores_out(b):
                pp = p_s[:, b % 2, :]
                dve.wait_ge(s_mm, b + 1)
                if b >= 2:
                    dve.wait_ge(t_mm, t_group(b - 2, 3) + 1)
                d = drop[:, b, :].rearrange("p (s o) -> p s o", o=1).to_broadcast((P, 16, HD))
                step(nc.vector.tensor_tensor(pp[:, 0:1024].rearrange("p (s w) -> p s w", w=HD),
                                             ps[:, 0:2, :].rearrange("p a (s w) -> p (a s) w", w=HD), d, ALU.add))
                a = CON["new_add"][0] + NS * b
                step(nc.vector.tensor_tensor(pp[:, 1024:1088], ps[:, 3, 0:NS], con[:, a:a + NS], ALU.add))
                nc.vector.tensor_tensor(pp[:, 1600:1664], ps[:, 3, NS:2 * NS], con[:, a:a + NS], ALU.add).then_inc(s_read, 1)
                after(steps[0])
                nc.vector.tensor_reduce(stat_s[:, b, 0:1], pp[:, 0:1088], AX.X, ALU.max, negate=True).then_inc(s_max, 1)
                dve.wait_ge(s_win, b + 1)
                chain(nc.vector.tensor_tensor(pp[:, 1088:1096], pp[:, 1088:1096], tab("win_add"), ALU.add))
                dve.wait_ge(s_read, b + 1)
                nc.vector.tensor_reduce(stat_s[:, b, 1:2], pp[:, 1088:1664], AX.X, ALU.max, negate=True).then_inc(s_max, 1)

            def rows_out(b):
                a = acc_s[:, b % 2, :]
                dve.wait_ge(gate_moved, 16 * 17)
                dve.wait_ge(s_exp, b + 1)
                chain(nc.vector.reciprocal(stat_s[:, b, 4:6], stat_s[:, b, 2:4]))
                chain(nc.vector.tensor_tensor(stat_s[:, b, 4:6], stat_s[:, b, 4:6], gate_s[:, b, 1:3], ALU.mult))
                dve.wait_ge(o_mm, b + 1)
                if b >= 2:
                    dve.wait_ge(t_fin, b - 1)
                chain(nc.vector.tensor_scalar(a, ps[:, 7, 0:256], gate_s[:, b, 0:1], None, ALU.mult))
                chain(nc.vector.scalar_tensor_tensor(a, ps[:, 6, 0:256], stat_s[:, b, 4:5], a, ALU.mult, ALU.add))
                nc.vector.scalar_tensor_tensor(a, ps[:, 6, 256:512], stat_s[:, b, 5:6], a, ALU.mult, ALU.add).then_inc(o_read, 1)
                dve.wait_ge(o_read, b + 1)
                nc.vector.tensor_tensor(a, a, tab("own_kv"), ALU.mult).then_inc(acc_ready, 1)

            def heads_out(b, n):
                dve.wait_ge(t_mm, n + 1)
                for g in range(2):
                    lo = 128 * g + 64 * g
                    src = ps[:, 4 + n % 2, lo:lo + 64].rearrange("p (e r i) -> p r i e", e=2, r=REP)
                    last = nc.vector.tensor_reduce(
                        attn_t[:, 4 * g:4 * g + 4, SEQ + DT * b:SEQ + DT * b + DT].rearrange("p r (i o) -> p r i o", o=1),
                        src, AX.X, ALU.add)
                last.then_inc(t_fin, 1)

            scores_out(0)
            for b in range(NB):
                if b + 1 < NB:
                    scores_out(b + 1)
                if b >= 1:
                    heads_out(b - 1, t_group(b, 4))
                rows_out(b)
            heads_out(NB - 1, t_group(NB, 0))

            items = [(n, c, e, r) for n in range(PT) for c in range(C) for e in range(2) for r in range(2)]

            def p_top(i):
                n = items[i][0]
                dve.wait_ge(p_mm, i + 1)
                s = ps[:, i % 4, :]
                chain(nc.vector.tensor_tensor(s[:, n * P:(n + 1) * P], s[:, n * P:(n + 1) * P], tab("causal"), ALU.add))
                nc.vector.tensor_reduce(nmax_p[:, i % 8:i % 8 + 1], s[:, 0:(n + 1) * P], AX.X, ALU.max,
                                        negate=True).then_inc(p_max, 1)

            def p_acc(i):
                n, c, e, r = items[i]
                f, s = f_p[:, i % 8:i % 8 + 1], sum_p[:, i % 8:i % 8 + 1]
                dve.wait_ge(p_exp, i + 1)
                chain(nc.vector.reciprocal(f, s))
                head = 2 * c + e
                g = gates[:, n, 3 * head + 1 + r:3 * head + 2 + r]
                chain(nc.vector.tensor_tensor(f, f, g, ALU.mult))
                dve.wait_ge(po_mm, i + 1)
                a = acc[:, n, HD * (2 * c + e):HD * (2 * c + e + 1)]
                if i >= 1:
                    dve.wait_ge(po_read, i)
                nc.vector.scalar_tensor_tensor(a, ps[:, 6 + i % 2, 0:HD], f, a, ALU.mult, ALU.add).then_inc(po_read, 1)

            LAG = 3
            for i in range(len(items) + LAG):
                if i < len(items):
                    p_top(i)
                if i >= LAG:
                    p_acc(i - LAG)

            for m in range(C):
                lo_part("attn", m, attn_t[:, m, :])
            for m in range(C):
                add_square(6, m)
            post_norm(6, 5)
            pre_norm(7, 6, "mlp1")
            mlp(1, 8)
            post_norm(8, 7)
            for m in range(C):
                lo_part("x1", m, x[:, m, :])
            ple(1)


def feature_major(a):
    a = np.asarray(a)
    r = a.reshape(a.shape[:-1] + (a.shape[-1] // P, P))
    n = a.ndim - 2
    return np.ascontiguousarray(np.moveaxis(r, [n, n + 1, n + 2], [n + 2, n + 1, n]))


def weight_blocks(w, width=256):
    k, m = w.shape
    return w.reshape(k // P, P, m // width, width).transpose(2, 1, 0, 3).reshape(m // width, P, -1)


def mlp_blocks(up, down):
    f = FF // Q4
    return [weight_blocks(part) for n in range(Q4) for part in (up[:, f * n:f * n + f], down[f * n:f * n + f])]


HEAD_ORDER = np.arange(D).reshape(2, 2, REP, HD).transpose(0, 2, 1, 3).reshape(-1)


def constants():
    t = np.zeros((P, NCON), np.float32)

    def put(name, v):
        a, b = CON[name]
        t[:v.shape[0], a:b] = v.reshape(v.shape[0], -1)

    p = np.arange(P)
    put("ident", np.eye(P))
    put("eps", np.full((P, 1), EPS))
    put("mean", np.full((P, P), 1.0 / D))
    d = p % HD
    half = 8
    partner = np.where(d < half, p + half, np.where(d < 2 * half, p - half, p))
    swap = np.zeros((P, P))
    swap[partner, p] = 1.0
    put("swap", swap)
    pos = np.concatenate([np.arange(SEQ), np.tile(PAST + np.arange(DT), NB)]).astype(np.float32)
    inv = np.power(np.float32(500000.0), -np.arange(half, dtype=np.float32) * np.float32(2.0 / 16))
    ang = (pos[None, :] * inv[:, None].astype(np.float32)).astype(np.float32)
    cos, sin = np.cos(ang), np.sin(ang)
    rot = d < 2 * half
    put("cos", np.where(rot[:, None], cos[d % half], 1.0))
    put("sin", np.where(rot[:, None], np.where(d < half, -1.0, 1.0)[:, None] * sin[d % half], 0.0))
    qq = np.arange(P)
    put("causal", np.where(qq[None, :] <= qq[:, None], 0.0, NEG))
    g, i = p // 32, p % DT
    put("same_q", (g[:, None] == g[None, :]) & (i[:, None] == i[None, :]))
    qpos = np.arange(PT)[None, :] * P + qq[:, None]
    c = np.arange(NCP)
    ok = (16 * c + 31)[None, None, :] <= qpos[:, :, None]
    put("cmp_add", np.where(ok, 0.0, NEG))
    put("cmp_mul", ok.astype(np.float32))
    kb, kj = np.arange(NS) // DT, np.arange(NS) % DT
    ok = (kb[None, None, :] == np.arange(NB)[None, :, None]) & (kj[None, None, :] <= i[:, None, None])
    put("new_add", np.where(ok, 0.0, NEG))
    put("win_add", np.where(np.arange(DT)[None, :] > i[:, None], 0.0, NEG))
    put("block_no", np.tile(np.arange(16), (P, 1)))
    put("own_kv", (np.arange(256) // HD)[None, :] == g[:, None])
    return t


def kernel(**inputs):
    import concourse.bacc as bacc
    from concourse.bass_utils import run_bass_kernel_spmd

    v = {k: np.asarray(a) for k, a in inputs.items()}
    tokens = np.concatenate([v["x_prompt"].reshape(SEQ, D), v["x_sample"].reshape(NS, D)])
    p_tokens = np.concatenate([v["p_prompt"].reshape(2, SEQ, 256), v["p_sample"].reshape(2, NS, 256)], axis=1)
    par = np.zeros((P, NPAR), np.float32)

    def put(name, a):
        lo, hi = PAR[name]
        par[:, lo:hi] = a.reshape(-1, P).T

    glu = np.arange(2 * D).reshape(2, C, P)[::-1].transpose(1, 0, 2).reshape(-1)
    put("norm_g", v["norm_g"])
    put("b_ple", v["b_ple_gate"])
    put("b_pw1", v["conv_b_pw1"][0][glu])
    lo, hi = PAR["w_dw"]
    par[:, lo:hi] = v["conv_w_dw"][0].reshape(TAPS, C, P).transpose(2, 1, 0).reshape(P, -1)
    put("b_dw", v["conv_b_dw"])
    put("ln_g", v["conv_ln_g"])
    put("ln_b", v["conv_ln_b"])
    put("b_pw2", v["conv_b_pw2"])
    lo, hi = PAR["pe"]
    par[:, lo:hi] = v["nsa_cmp_pe"][0].reshape(2, 16, 2, HD).transpose(2, 3, 0, 1).reshape(P, -1)
    w_in = v["nsa_w_in"][0]
    kv_at = lambda i: w_in[:, D + 256 * i:D + 256 * (i + 1)]
    w_g = w_in[:, D + 6 * 256:].reshape(D, 2, 2, REP, 3).transpose(0, 1, 3, 2, 4).reshape(D, 48)
    w_q = w_in[:, :D][:, HEAD_ORDER]
    kv_pair = lambda i, j: weight_blocks(np.concatenate([kv_at(i), kv_at(j)], 1))
    w = np.concatenate(
        [weight_blocks(v["conv_w_pw1"][0][:, glu]), weight_blocks(v["conv_w_pw2"][0])]
        + mlp_blocks(v["w_ff1"][0], v["w_ff2"][0]) + [weight_blocks(v["w_ple_gate"][0])]
        + [weight_blocks(w_q), kv_pair(0, 1), kv_pair(2, 4), kv_pair(3, 5), weight_blocks(v["nsa_w_out"][0][HEAD_ORDER])]
        + mlp_blocks(v["w_ff1"][1], v["w_ff2"][1]) + [weight_blocks(v["w_ple_gate"][1])])
    arrays = {
        "x": feature_major(tokens), "p": feature_major(p_tokens), "par": par, "con": constants(), "w": w,
        "ple": np.stack([weight_blocks(v["w_ple"][i], D)[0] for i in range(2)]),
        "state": np.ascontiguousarray(v["state_conv"][0].reshape(NB, TAPS - 1, C, P).transpose(3, 2, 0, 1)),
        "w_gates": weight_blocks(w_g, 48)[0],
    }
    cc = v["cache_cmp"][0].reshape(POOL, 8, 8, 2, 2, KV, HD).transpose(0, 3, 6, 4, 2, 1, 5)
    arrays["cmp_pages"] = cc.reshape(POOL, P, 512)
    cs = v["cache_sel"][0]
    keys = cs[:, :, 0].reshape(POOL, P, 2, 2, HD).transpose(0, 3, 4, 2, 1).reshape(POOL, P, 256)
    arrays["sel_pages"] = np.concatenate([keys, cs[:, :, 1].reshape(POOL, P, 256)], 2)
    cw = v["cache_win"][0]
    keys = cw[:, :, 0].reshape(NB, WIN, 2, 2, HD).transpose(0, 3, 4, 2, 1).reshape(NB, P, 1024)
    vals = cw[:, :, 1].reshape(NB, 4, P, 256).transpose(0, 2, 1, 3).reshape(NB, P, 1024)
    arrays["win"] = np.concatenate([keys, vals], 2)
    arrays["pages"] = v["page_table"].reshape(1, NB * PAGES)
    w1 = v["nsa_cmp_w1"][0].reshape(2, 16, 2, HD, P)
    arrays["w1"] = w1.transpose(2, 3, 0, 1, 4).reshape(P, 2, 16, P)
    arrays["w2"] = v["nsa_cmp_w2"][0].transpose(1, 0, 2)
    outs = {"win": (NB, P, BLK // 2), "y": (P, C, T), "conv_p": (P, C, TAPS - 1), "conv_s": (P, C, NB, TAPS - 1), "kv_cmp": (P, 4, T), "k_rot": (P, 4, T),
            "v_tok": (P, PT, 512), "v_tok_s": (NS, 512)}
    nc = bacc.Bacc("TRN2", target_bir_lowering=False, num_devices=1)
    arrays = {f"in_{k}": np.ascontiguousarray(a) for k, a in arrays.items()}
    ext = {k[3:]: nc.dram_tensor(k, a.shape, mybir.dt.from_np(a.dtype), kind="ExternalInput").ap()
           for k, a in arrays.items()}
    out = {k: nc.dram_tensor(f"out_{k}", s, F32, kind="ExternalOutput").ap() for k, s in outs.items()}
    program(nc, ext, out)
    r = run_bass_kernel_spmd(nc, [arrays], core_ids=[0]).results[0]
    got = {k: r[f"out_{k}"] for k in outs}

    def kv_rows(a, i):
        return a[:, 2 * i:2 * i + 2].transpose(2, 1, 0).reshape(T, KV, HD)

    v_all = np.concatenate([got["v_tok"].transpose(1, 0, 2).reshape(SEQ, 512), got["v_tok_s"]])
    cmp_rows = np.stack([kv_rows(got["kv_cmp"], 0), kv_rows(got["kv_cmp"], 1)], 1)
    sel_rows = np.stack([kv_rows(got["k_rot"], 0), v_all[:, :256].reshape(T, KV, HD)], 1)
    win_rows = np.stack([kv_rows(got["k_rot"], 1), v_all[:, 256:].reshape(T, KV, HD)], 1)
    split = lambda a: (a[:SEQ][None, None], a[SEQ:].reshape((1, NB, DT) + a.shape[1:]))
    cmp_p, cmp_s = split(cmp_rows)
    sel_p, sel_s = split(sel_rows)
    win_p, win_s = split(win_rows)
    y = got["y"].transpose(2, 1, 0).reshape(T, D)
    y_p, y_s = y[:SEQ].reshape(1, SEQ, D), y[SEQ:].reshape(NB, DT, D)
    wk = got["win"][:, :, :1024].reshape(NB, 2, HD, 2, WIN).transpose(0, 4, 3, 1, 2).reshape(NB, WIN, KV, HD)
    wv = got["win"][:, :, 1024:].reshape(NB, P, 4, KV, HD).transpose(0, 2, 1, 3, 4).reshape(NB, WIN, KV, HD)
    win_all = np.concatenate([np.stack([wk, wv], 2)[None][:, :, DT:], win_s], 2)
    conv_p = got["conv_p"].transpose(2, 1, 0).reshape(1, 1, TAPS - 1, D)
    conv_s = got["conv_s"].transpose(2, 3, 1, 0).reshape(1, NB, TAPS - 1, D)
    return y_p, y_s, cmp_p, cmp_s, sel_p, sel_s, win_p, win_all, conv_p, conv_s
```

```python
import numpy as np
import concourse.bass as bass
import concourse.mybir as mybir
from concourse.alu_op_type import AluOpType as ALU

F32 = mybir.dt.float32
F32R = mybir.dt.float32r
I32 = mybir.dt.int32
ACT = mybir.ActivationFunctionType
AX = mybir.AxisListType

P = 128
D = 1024
SEQ = 512
NB = 8
DT = 8
NS = NB * DT
T = SEQ + NS
HT = T // 2
C = D // P
TAPS = 31
PAST = 1024
PAGES = 8
POOL = 80
KV = 4
REP = 4
HD = 64
FF = 4096
FC = FF // P
WIN = 512
EPS = 1e-6
NEG = -1e30
SCALE = HD ** -0.5
WB = 2048
BLK = 4096
Q4 = 4
PT = SEQ // P
TT = PT + 1
EXT_P = SEQ + TAPS - 1
EXT_S = DT + TAPS - 1
EXT = EXT_P + NB * EXT_S
NCP = 32
NCS = 64

def columns(parts):
    at, n = {}, 0
    for name, width in parts:
        at[name] = (n, n + width)
        n += width
    return at, n

PAR, NPAR = columns([("norm_g", 64), ("b_ple", 16), ("b_pw1", 16), ("w_dw", 8 * TAPS), ("b_dw", 8), ("ln_g", 8),
                     ("ln_b", 8), ("b_pw2", 8), ("pe", 2 * 16)])
CON, NCON = columns([("ident", P), ("mean", P), ("pick", 4 * P), ("eps", 1), ("cos", T), ("sin", T), ("causal", P),
                     ("same_q", P), ("cmp_add", PT * NCP), ("cmp_mul", PT * NCP), ("new_add", NB * NS),
                     ("win_add", DT), ("block_no", 16), ("own_kv", 256)])

def mlp_stages(layer):
    return [s for n in range(Q4) for s in ((f"up{layer}{n}", C, "A" * C),
                                           (f"down{layer}{n}", C, ("A" if n == 0 else "D") * C))]


STAGES = ([("pw1", 16, "A" * 16), ("taps", 3, "DAA"), ("pw2", C, "A" * C)] + mlp_stages(0) + [("ple0", C, "A" * C), ("gate0", C, "A" * C),
          ("q", C, "A" * C), ("kv_cmp", 4, "A" * 4), ("k_rot", 4, "A" * 4), ("gates", 1, "A"), ("v_tok", 2 * TT, "A" * 2 * TT),
          ("gates_t", 1, "A"), ("out", C, "A" * C)] + mlp_stages(1)
          + [("ple1", C, "A" * C), ("gate1", C, "A" * C)])
FIRST, FREED = {}, []
_n = {"A": 0, "D": 0}
for _name, _count, _who in STAGES:
    FIRST[_name] = len(FREED)
    for _w in _who:
        _n[_w] += 1
        FREED.append((_w, _n[_w]))

STAGED = {name: C * n for n, name in enumerate(
    ["conv", "silu", "mlp0", "hid00", "hid01", "hid02", "hid03", "x0", "nsa", "attn",
     "mlp1", "hid10", "hid11", "hid12", "hid13", "x1"])}
INPUT = {"pw1": "conv", "pw2": "silu", "gate0": "x0", "gate1": "x1", "q": "nsa", "kv_cmp": "nsa", "k_rot": "nsa",
         "v_tok": "nsa", "out": "attn"}
for _l in range(2):
    for _q in range(Q4):
        INPUT[f"up{_l}{_q}"] = f"mlp{_l}"
        INPUT[f"down{_l}{_q}"] = f"hid{_l}{_q}"

RAW_OF = {name: C * n for n, name in enumerate(
    ["conv", "mlp0", "hid00", "hid01", "hid02", "hid03", "nsa", "mlp1", "hid10", "hid11", "hid12", "hid13"])}

W_STAGES = ([("pw1", 8), ("pw2", 4)] + [(s, 4) for s, _, _ in mlp_stages(0)] + [("gate0", 4), ("q", 4), ("kv_cmp", 2),
            ("k_rot", 2), ("v_tok", 2), ("out", 4)] + [(s, 4) for s, _, _ in mlp_stages(1)] + [("gate1", 4)])
W_OF, W_END, BLOCKS = {}, [], []
for _s, _c in W_STAGES:
    W_OF[_s] = len(W_END)
    _per = TT if _s == "v_tok" else 2
    if _s == "out":
        BLOCKS += [("w1", 0)] + [("cmp_pages", b) for b in range(NB)]
        BLOCKS += [("sel_pages", 0), ("sel_pages", 1)]
        BLOCKS += [("win_k", 0), ("win_k", 1), ("win_v", 0), ("sel_pages", 2), ("win_v", 1)]
        for _b in range(2, NB):
            BLOCKS += [("win_k", _b)] + [("sel_pages", _b + 1)] * (_b + 1 < NB) + [("win_v", _b)]
    if _s.startswith("gate"):
        BLOCKS.append(("ple", int(_s[-1])))
    for _i in range(_c):
        BLOCKS.append(("w", len(W_END)))
        W_END.append(FIRST[_s] + _per * (_i + 1))
QT = T // 4
WARM = 4
HALF = 8
SIZE = {"w": WB, "w1": BLK, "ple": WB, "cmp_pages": BLK, "sel_pages": BLK, "win_k": BLK // 4, "win_v": BLK // 4}
B_OF = {b: i for i, b in reversed(list(enumerate(BLOCKS)))}

RAW, SPLIT, RING = 0, 2 * WB, 6 * WB
PLACE, _raw = [], 0
for _src, _row in BLOCKS:
    if _src in ("w", "ple"):
        PLACE.append((WB * (_raw % 2), _raw % 2))
        _raw += 1
    elif _src == "cmp_pages":
        PLACE.append((BLK * (1 + _row % 2), 3 + _row % 2))
    elif _src == "w1":
        PLACE.append((0, 9))
    elif _src == "sel_pages":
        PLACE.append((BLK * ((_row + 2) % 3), 2 + (_row + 2) % 3))
    else:
        PLACE.append((None, {"win_k": 5, "win_v": 7}[_src] + _row % 2))
LAST_THERE, LOADED = [], []
_at, _holds = [0] * 10, {}
for _i, (_src, _row) in enumerate(BLOCKS):
    _lo, _sem = PLACE[_i]
    _parts = range(0) if _src.startswith("win") else range(_lo // WB, (_lo + SIZE[_src]) // WB)
    LAST_THERE.append(sorted({_holds[_k] for _k in _parts if _k in _holds}))
    for _k in _parts:
        _holds[_k] = ("loaded", _i)
    if _src == "w":
        for _k in (0, 1):
            _holds[SPLIT // WB + 2 * (_row % 2) + _k] = ("split", _row)
    _at[_sem] += 16 * (PAGES if _src.endswith("pages") else 1)
    LOADED.append(_at[_sem])


DIRECT = (3, 7)


def adds(n):
    return (C - 1) * sum((a in DIRECT) == (n in DIRECT) for a in range(n))


TAP_TILES = [(C - 3, 19, TAPS), (C - 2, 0, TAPS), (C - 1, 0, TAPS)]
LATE = [C - 3, C - 1]
EARLY = [m for m in range(C) if m not in LATE]
DIAGONALS = [(i, m, j) for i, (m, a, b) in enumerate(TAP_TILES) for j in range(a, b)]


ITEMS = [(n, c, e, r) for n in range(PT) for c in range(C) for e in range(2) for r in range(2)]
TRANSPOSED = []
for _i in range(len(ITEMS)):
    TRANSPOSED.append(("item", _i))
    for _k in range(2 * (PT - 1)):
        if _i == len(ITEMS) // PT * (_k // 2 + 1) + 6 + 2 * (_k % 2):
            TRANSPOSED.append(("rows", _k))
TRANSPOSED += [("rows", 2 * PT - 2), ("rows", 2 * PT - 1)]
TURN = {_what: _n for _n, _what in enumerate(TRANSPOSED)}


def t_group(b, k):
    return 5 * b + k - (b > 0)


def program(nc, ext, out):
    from contextlib import ExitStack
    with ExitStack() as ctx:
        def sb(name, shape, dt=F32):
            return ctx.enter_context(nc.sbuf_tensor(name, shape, dt))

        def sem(name):
            return ctx.enter_context(nc.semaphore(name))

        arena = [16512]

        def at_byte(name, shape, byte, dt=F32):
            return nc.alloc_sbuf_tensor_at(name, shape, dt, offset=byte)

        def sb(name, shape, dt=F32):
            n = 4 * int(np.prod(shape[1:]))
            byte = arena[0]
            arena[0] += (n + 31) // 32 * 32
            return at_byte(name, shape, byte, dt)

        ring_byte = arena[0]
        w_raw = sb("w_raw", [P, 2, WB])
        w_hi = [sb("w_hi0", [P, WB], F32R), None]
        w_lo = [sb("w_lo0", [P, WB], F32R), None]
        w_hi[1] = sb("w_hi1", [P, WB], F32R)
        w_lo[1] = sb("w_lo1", [P, WB], F32R)
        ring = at_byte("ring", [P, RING], ring_byte)
        x = sb("x", [P, C, T])
        ha_byte = arena[0]
        ha = sb("ha", [P, C * T + NS], F32R)
        hb_byte = arena[0]
        hb = sb("hb", [P, C * T + NS], F32R)
        big_byte = arena[0]
        big = sb("big", [P, 4 * C * T])
        hid_hi = at_byte("hid_hi", [P, C * T], big_byte, F32R)
        hid_lo = at_byte("hid_lo", [P, C * T], big_byte + 4 * C * T, F32R)
        mix = at_byte("mix", [P, C, T], big_byte + 8 * C * T)
        ple_in = at_byte("ple_in", [P, 2, T], big_byte + 12 * C * T)
        emb = at_byte("emb", [P, C, T], big_byte)
        diag = at_byte("diag", [P, 18, P], arena[0])
        sq = sb("sq", [P, 4, T])
        sq_sum = sb("sq_sum", [P, T])
        rstd_q = sb("rstd_q", [P, QT])
        par = sb("par", [P, NPAR])
        con = sb("con", [P, NCON])
        conv_in = big[:, 0:C * EXT].rearrange("p (c t) -> p c t", t=EXT)
        y = big[:, C * EXT:C * EXT + C * T].rearrange("p (c t) -> p c t", t=T)
        at = C * EXT + C * T
        sig = big[:, at:at + 2 * T].rearrange("p (c t) -> p c t", t=T)
        odd_taps = big[:, at + 2 * T:at + 2 * T + SEQ]
        at = 3 * C * T + 2 * T
        val = big[:, at:at + 2 * T].rearrange("p (c t) -> p c t", t=T)
        at += 2 * T
        tap_prod = big[:, at:at + NS * TAPS].rearrange("p (b t j) -> p b t j", b=NB, t=DT)
        at = 0
        q = big[:, at:at + C * T].rearrange("p (c t) -> p c t", t=T); at += C * T
        q_rot = big[:, at:at + C * T].rearrange("p (c t) -> p c t", t=T); at += C * T
        kv_cmp = big[:, at:at + 4 * T].rearrange("p (c t) -> p c t", t=T); at += 4 * T
        k_rot = big[:, at:at + 4 * T].rearrange("p (c t) -> p c t", t=T); at += 4 * T
        v_tok = big[:, at:at + TT * 512].rearrange("p (n f) -> p n f", f=512); at += TT * 512
        gates = sb("gates", [P, TT, 48])
        w_gates = sb("w_gates", [P, C * 48])
        wg_hi = sb("wg_hi", [P, C * 48], F32R)
        wg_lo = sb("wg_lo", [P, C * 48], F32R)
        gates_f = sq_sum[0:48, :]
        rope_tmp = big[:, at:at + 2 * T].rearrange("p (c t) -> p c t", t=T)
        k_cmp_s = big[:, at:at + NB * 2 * NCS].rearrange("p (b g c) -> p b g c", b=NB, g=2); at += NB * 2 * NCS
        v_cmp_s = big[:, at:at + NB // 2 * 256].rearrange("p (b f) -> p b f", f=256)
        w1 = at_byte("w1", [P, 2, 16, P], ring_byte)
        kv_pairs = at_byte("kv_pairs", [P, 2, KV, SEQ], hb_byte)
        acc = at_byte("acc", [P, PT, D], hb_byte)
        attn_t = at_byte("attn_t", [P, C, T], ha_byte)
        sq_flat = sq[:, :, :].rearrange("p c t -> p (c t)")
        hid_s = sq_flat[:, 0:512].rearrange("p (u n) -> p u n", u=2)
        hid_p = sq_flat[:, 512:768].rearrange("p (v e g c) -> p v e g c", v=2, e=2, g=2)
        v_cmp_p = sq_flat[:, 1792:2304].rearrange("p (g f) -> p g f", g=2)
        pc_t_p = sq_flat[:, 0:512].rearrange("p (j t) -> p j t", j=4)
        pt_s = sq_flat[:, 0:1792]
        q_flat = q.rearrange("p c t -> p (c t)")
        pc = [sq_flat[:, 768:1280], sq_flat[:, 1280:1792], q_flat[:, 0:512], q_flat[:, 512:1024]]
        c_row = sq_sum[0:1, 0:2 * P]
        pc_s = sq_sum[:, 0:NB * NCS]
        pc_t_s = q_flat[:, 4096:4608].rearrange("p (j t) -> p j t", j=4)
        p_s = q_flat[:, 0:3328].rearrange("p (u n) -> p u n", u=2)
        p_p = q_flat[:, 0:2048].rearrange("p (u n) -> p u n", u=4)
        pt_p = q_flat[:, 2048:3072].rearrange("p (u n) -> p u n", u=2)
        kvc_flat = kv_cmp.rearrange("p c t -> p (c t)")
        qbd = kvc_flat[:, 0:1024].rearrange("p (b g e m) -> p b g e m", b=NB, g=2, e=2)
        imp = kvc_flat[:, 1024:1152].rearrange("p (b s) -> p b s", b=NB)
        drop = kvc_flat[:, 1152:1280].rearrange("p (b s) -> p b s", b=NB)
        eq = kvc_flat[:, 1280:1408].rearrange("p (b s) -> p b s", b=NB)
        acc_s = kvc_flat[:, 1408:1920].rearrange("p (u n) -> p u n", u=2)
        cmax = kvc_flat[:, 1920:1992]
        csum = kvc_flat[:, 1992:2064]
        stat_s = kvc_flat[:, 2064:2128].rearrange("p (b c) -> p b c", b=NB)
        least = kvc_flat[:, 2128:2144]
        nmax_p = kvc_flat[:, 2144:2152]
        f_p = kvc_flat[:, 2152:2160]
        sum_p = kvc_flat[:, 2160:2168]
        k_cmp_p = sb("k_cmp_p", [P, 2, 2, NCP])
        w2 = sb("w2", [P, 2, HD])
        c_vec = sb("c_vec", [P, 2])
        gate_s = sb("gate_s", [P, NB, 3])
        pages = sb("pages", [1, NB * PAGES], I32)
        assert arena[0] <= 229344, arena[0]
        gate_rows = nc.dram_tensor("gate_rows", (NS, 48), F32, kind="Internal").ap()

        ps = ctx.enter_context(nc.psum_tensor("ps", [P, 8, 512], F32))
        STAT = ps[:, 6:8, 0:HT]

        def STAT_Q(n):
            if n in DIRECT:
                return ps[:, 2 * ((FIRST["up00" if n == 3 else "up10"] + 2) % 3), 0:QT]
            return ps[:, 6, HT:HT + QT]

        def split_input(name):
            return (hb, ha) if name == "attn" else (hid_hi, hid_lo) if name.startswith("hid") else (ha, hb)

        def chunk(a, k, lo=0, n=T):
            return a[:, k * T + lo:k * T + lo + n]

        def block_at(i, lo, n):
            return ring[:, PLACE[i][0] + lo:PLACE[i][0] + lo + n]

        def window(b):
            return attn_t[:, 4 * (b % 2):4 * (b % 2) + 4, 0:SEQ]

        def slot(t):
            return ps[:, 2 * (t % 3):2 * (t % 3) + 2, 0:HT]

        def halves(ap):
            return ap.rearrange("p (a t) -> p a t", a=2)

        def sample_rows(m):
            return conv_in[:, m, EXT_P:].rearrange("p (b t) -> p b t", t=EXT_S)

        def pcol(name, i):
            a = PAR[name][0] + i
            return par[:, a:a + 1]

        def tab(name):
            a, b = CON[name]
            return con[:, a:b]

        consts_in = sem("consts_in")
        tables_in = sem("tables_in")
        x_in = [sem(f"x_in{i}") for i in range(4)]
        state_in = sem("state_in")
        ple_loaded = sem("ple_loaded")
        wg_in = sem("wg_in")
        block_in = [sem(f"block_in{i}") for i in range(10)]
        tile_done = sem("tile_done")
        act_freed = sem("act_freed")
        dve_freed = sem("dve_freed")
        freed = {"A": act_freed, "D": dve_freed}
        sq_ready = sem("sq_ready")
        sq_added = sem("sq_added")
        sq_taken = sem("sq_taken")
        sq_summed = sem("sq_summed")
        y_added = sem("y_added")
        mean_ready = sem("mean_ready")
        std_ready = sem("std_ready")
        rstd_ready = sem("rstd_ready")
        rstd_out = sem("rstd_out")
        w_hi_ready = sem("w_hi_ready")
        w_ready = sem("w_ready")
        raw_ready = sem("raw_ready")
        hi_ready = sem("hi_ready")
        lo_ready = sem("lo_ready")
        wg_hi_ready, wg_ready = sem("wg_hi_ready"), sem("wg_ready")
        silu_done = sem("silu_done")
        pad_zero = sem("pad_zero")
        x_ready = sem("x_ready")
        glu_done = sem("glu_done")
        tap_products = sem("tap_products")
        sample_conv = sem("sample_conv")
        diag_ready = sem("diag_ready")
        diag_used = sem("diag_used")
        pad_done = sem("pad_done")
        conv_done = sem("conv_done")
        centred = sem("centred")
        normed = sem("normed")
        dve_step = sem("dve_step")
        stored = sem("stored")
        q_swapped, k_swapped = sem("q_swapped"), sem("k_swapped")
        rot_done = sem("rot_done")

        pages_in = sem("pages_in")
        pairs_in = sem("pairs_in")
        kv_cmp_stored = sem("kv_cmp_stored")
        gate_moved = sem("gate_moved")
        win_stored = [sem("win_stored0"), sem("win_stored1")]
        c_mm, c_there = sem("c_mm"), sem("c_there")
        cmp_mm, hid_a, hid_ab, hid_ready = sem("cmp_mm"), sem("hid_a"), sem("hid_ab"), sem("hid_ready")
        w2_mm, w2_out = sem("w2_mm"), sem("w2_out")
        phid_mm, phid_ready = sem("phid_mm"), sem("phid_ready")
        phid_zero = sem("phid_zero")
        pw2_mm, pw2_out = sem("pw2_mm"), sem("pw2_out")
        bd_zero = sem("bd_zero")
        qbd_zero, qbd_ready = sem("qbd_zero"), sem("qbd_ready")
        sc_mm = sem("sc_mm")
        sc_sub, c_exp = sem("sc_sub"), sem("c_exp")
        pc_ready = sem("pc_ready")
        imp_mm, drop_ready = sem("imp_mm"), sem("drop_ready")
        ct_mm, ct_out = sem("ct_mm"), sem("ct_out")
        co_mm, co_read = sem("co_mm"), sem("co_read")
        s_mm, s_read = sem("s_mm"), sem("s_read")
        s_win = sem("s_win")
        s_max, s_exp = sem("s_max"), sem("s_exp")
        t_mm, t_out, t_fin = sem("t_mm"), sem("t_out"), sem("t_fin")
        o_mm, o_read, acc_ready = sem("o_mm"), sem("o_read"), sem("acc_ready")
        p_mm, p_max, p_exp = sem("p_mm"), sem("p_max"), sem("p_exp")
        pt_mm, pt_out = sem("pt_mm"), sem("pt_out")
        po_mm, po_read = sem("po_mm"), sem("po_read")
        ft_mm, ft_out = sem("ft_mm"), sem("ft_out")

        block = ctx.enter_context(nc.Block())

        def prompt_convolved(engine, m):
            if m < C - 2:
                engine.wait_ge(conv_done, m + 1)
            else:
                engine.wait_ge(act_freed, FREED[FIRST["taps"] + m - (C - 3)][1])
            engine.wait_ge(sample_conv, m + 1)

        @block.sync
        def _(sp):
            for i in range(4):
                sp.dma_start(x[:, 2 * i:2 * i + 2, :], ext["x"][:, 2 * i:2 * i + 2, :]).then_inc(x_in[i], 16)
            late = CON["cos"][0]
            sp.dma_start(con[:, 0:late], ext["con"][:, 0:late]).then_inc(consts_in, 16)
            sp.dma_start(par[:, :], ext["par"]).then_inc(consts_in, 16)
            for i, (src, row) in enumerate(BLOCKS):
                for what, last in LAST_THERE[i]:
                    if what == "split":
                        sp.wait_ge(tile_done, W_END[last])
                        continue
                    was, n = BLOCKS[last]
                    if was == "w":
                        sp.wait_ge(w_ready, n + 1)
                    elif was == "ple":
                        sp.wait_ge(tile_done, FIRST[f"ple{n}"] + C)
                    elif was == "cmp_pages":
                        sp.wait_ge(hid_ab, 2 * n + 2)
                    elif was == "w1":
                        sp.wait_ge(cmp_mm, 2 * NB)
                    else:
                        sp.wait_ge(o_mm, n + 1)
                lo, k = PLACE[i]
                if src.startswith("win"):
                    if row >= 2:
                        sp.wait_ge(s_mm if src == "win_k" else o_mm, row - 1)
                        sp.wait_ge(win_stored[row % 2], 16 * (row // 2))
                if src in ("w", "ple"):
                    to = w_raw[:, k, :]
                elif src == "w1":
                    to = w1[:, :, :, :]
                elif src == "win_k":
                    to = window(row)[:, 0:2, :]
                elif src == "win_v":
                    to = window(row)[:, 2:4, :]
                else:
                    to = ring[:, lo:lo + SIZE[src]]
                if src.endswith("pages"):
                    sp.wait_ge(pages_in, 16)
                    for j in range(PAGES):
                        page = sp.value_load(pages[0:1, row * PAGES + j:row * PAGES + j + 1], min_val=0, max_val=POOL - 1)
                        sp.dma_start(to[:, j * 512:(j + 1) * 512],
                                     ext[src][bass.ds(page, 1), :, :].rearrange("o p n -> (o p) n")).then_inc(block_in[k], 16)
                else:
                    if src.startswith("win"):
                        rows = ext["win"][row].rearrange("p (c n) -> p c n", n=SEQ)
                        rows = rows[:, 0:2, :] if src == "win_k" else rows[:, 2:4, :]
                    else:
                        rows = ext["w1"] if src == "w1" else ext[src][row]
                    sp.dma_start(to, rows).then_inc(block_in[k], 16)
                if i == 0:
                    for m in range(C):
                        sp.dma_start(sample_rows(m)[:, :, 0:TAPS - 1], ext["state"][:, m]).then_inc(state_in, 16)
                    sp.dma_start(con[:, late:], ext["con"][:, late:]).then_inc(tables_in, 16)
                    sp.dma_start(pages[:, :], ext["pages"]).then_inc(pages_in, 16)
                    sp.dma_start(ple_in[:, :, :], ext["p"][0]).then_inc(ple_loaded, 16)
                    sp.dma_start(w_gates[:, :], ext["w_gates"]).then_inc(wg_in, 16)
                    sp.dma_start(w2[:, :, :], ext["w2"]).then_inc(wg_in, 16)
                if i == 9:
                    sp.wait_ge(glu_done, 2 * C)
                    sp.dma_start(out["conv_p"], conv_in[:, :, SEQ:EXT_P]).then_inc(stored, 16)
                    for m in range(C):
                        sp.dma_start(out["conv_s"][:, m], sample_rows(m)[:, :, DT:]).then_inc(stored, 16)
                if (src, row) == ("w", W_OF["out"] + 3):
                    sp.wait_ge(tile_done, FIRST["out"] + 1)
                    sp.dma_start(ple_in[:, :, :], ext["p"][1]).then_inc(ple_loaded, 16)
                if (src, row) == ("cmp_pages", 0):
                    sp.wait_ge(tile_done, FIRST["v_tok"] + 2 * TT)
                    sp.wait_ge(act_freed, FREED[FIRST["v_tok"] + 2 * TT - 1][1])
                    for e in range(2):
                        for later in range(2):
                            sp.dma_start(kv_pairs[64 * later:64 * later + 64, :, e:e + 3:2, 0:SEQ - later].rearrange(
                                             "p v g t -> p (v g) t"),
                                         kv_cmp[64 * e:64 * e + 64, :, later:SEQ]).then_inc(pairs_in, 16)
                    sp.dma_start(out["kv_cmp"], kv_cmp[:, :, :]).then_inc(kv_cmp_stored, 16)
                    sp.dma_start(out["v_tok"], v_tok[:, 0:PT, :]).then_inc(stored, 16)
                    sp.dma_start(out["v_tok_s"], v_tok[0:NS, PT, :]).then_inc(stored, 16)
                    sp.wait_ge(rot_done, 12)
                    sp.dma_start(out["k_rot"], k_rot[:, :, :]).then_inc(stored, 16)
            sp.wait_ge(kv_cmp_stored, 16)
            sp.wait_ge(win_stored[0], 16 * (NB // 2))
            sp.wait_ge(win_stored[1], 16 * (NB // 2))
            for m in range(C):
                sp.wait_ge(x_ready, 5 * C + m + 1)
                sp.dma_start(out["y"][:, m], x[:, m, :]).then_inc(stored, 16)
            sp.wait_ge(stored, 16 * (12 + C))

        @block.gpsimd
        def _(pool):
            nc.gpsimd.memset(conv_in[:, :, 0:TAPS - 1], 0.0).then_inc(pad_done, 1)
            nc.gpsimd.memset(ha[:, C * T:].bitcast(F32), 0.0).then_inc(pad_zero, 1)
            nc.gpsimd.memset(hb[:, C * T:].bitcast(F32), 0.0).then_inc(pad_zero, 1)

            def sample_products(m):
                pool.wait_ge(glu_done, 2 * m + 2)
                pool.wait_ge(state_in, 16 * C)
                if m > 0:
                    pool.wait_ge(sample_conv, m)
                es = sample_rows(m)
                rows = es[:, :, 0:TAPS]
                windows = bass.AP(tensor=rows.tensor, offset=rows.offset,
                                  ap=[rows.ap[0], rows.ap[1], [1, DT], [1, TAPS]])
                a = PAR["w_dw"][0] + TAPS * m
                taps = par[:, a:a + TAPS].rearrange("p (b t j) -> p b t j", b=1, t=1).to_broadcast((P, NB, DT, TAPS))
                nc.gpsimd.tensor_tensor(tap_prod, windows, taps, ALU.mult).then_inc(tap_products, 1)

            pool.wait_ge(consts_in, 32)

            def split_weights(first, last):
                for j in range(first, last):
                    k = PLACE[B_OF["w", j]][1]
                    pool.wait_ge(w_hi_ready, j + 1)
                    nc.gpsimd.tensor_tensor(w_lo[j % 2][:, :], w_raw[:, k, :], w_hi[j % 2][:, :].bitcast(F32),
                                            ALU.subtract).then_inc(w_ready, 1)

            split_weights(0, 1)
            pool.wait_ge(wg_hi_ready, 1)
            nc.gpsimd.tensor_tensor(wg_lo[:, :], w_gates[:, :], wg_hi[:, :].bitcast(F32), ALU.subtract).then_inc(wg_ready, 1)
            for m in range(C):
                split_weights(m + 1, m + 2)
                t = FIRST["pw1"] + 2 * m + 1
                pool.wait_ge(act_freed, FREED[t][1])
                e, es = conv_in[:, m, :], sample_rows(m)
                nc.gpsimd.tensor_tensor(e[:, TAPS - 1:EXT_P], val[:, m % 2, 0:SEQ], sig[:, m % 2, 0:SEQ],
                                        ALU.mult).then_inc(glu_done, 1)
                split_s = lambda a: a[:, m % 2, SEQ:].rearrange("p (b t) -> p b t", t=DT)
                nc.gpsimd.tensor_tensor(es[:, :, TAPS - 1:], split_s(val), split_s(sig), ALU.mult).then_inc(glu_done, 1)
                if m in (0, 3, 5, 7):
                    sample_products(m // 2)
            for m in range(4, C):
                sample_products(m)
            for i, m in enumerate(EARLY):
                prompt_convolved(pool, m)
                if i >= 2:
                    pool.wait_ge(y_added, i - 1)
                if i >= 1:
                    so_far = y[:, EARLY[0], :] if i == 1 else sq_sum[:, :]
                    nc.gpsimd.tensor_tensor(sq_sum[:, :], so_far, y[:, m, :], ALU.add).then_inc(y_added, 1)
            split_weights(C + 1, W_OF["out"])
            pool.wait_ge(rot_done, 12)
            nc.gpsimd.memset(hid_p[:, :, :, :, NCP - 1:NCP], 0.0).then_inc(phid_zero, 1)
            nc.gpsimd.memset(v_cmp_p, 0.0).then_inc(bd_zero, 1)
            nc.gpsimd.memset(k_cmp_p[:, :, :, :], 0.0).then_inc(bd_zero, 1)
            pool.wait_ge(act_freed, FREED[FIRST["gates_t"]][1])
            pool.dma_start(gate_rows, gates[0:NS, PT, :]).then_inc(gate_moved, 16)
            pool.wait_ge(gate_moved, 16)
            for n in range(KV * REP):
                g, r = n // REP, n % REP
                at = 3 * (2 * (g // 2 * REP + r) + g % 2)
                pool.dma_start(gate_s[n * DT:(n + 1) * DT, :, :],
                               gate_rows.rearrange("(b i) c -> i b c", i=DT)[:, :, at:at + 3]).then_inc(gate_moved, 16)
            pool.wait_ge(kv_cmp_stored, 16)
            pool.wait_ge(phid_mm, 2)
            nc.gpsimd.memset(qbd, 0.0).then_inc(qbd_zero, 1)
            for b in range(NB):
                for src in ("win_k", "win_v"):
                    i = B_OF[src, b]
                    pool.wait_ge(block_in[PLACE[i][1]], LOADED[i])
                pool.dma_start(out["win"][b].rearrange("p (c n) -> p c n", n=SEQ), window(b)).then_inc(win_stored[b % 2], 16)
            split_weights(W_OF["out"], len(W_END))

        @block.tensor
        def _(pe):
            def slot_free(t):
                if t >= 3:
                    who, n = FREED[t - 3]
                    pe.wait_ge(freed[who], n)

            def block_there(i):
                pe.wait_ge(block_in[PLACE[i][1]], LOADED[i])

            def dense(stage):
                name = INPUT[stage]
                hi, lo = split_input(name)

                def products(m, k, a):
                    j = W_OF[stage] + m // 2
                    at = 2 * P * k + P * (m % 2)
                    wh, wl = w_hi[j % 2][:, at:at + P], w_lo[j % 2][:, at:at + P]
                    to = slot(FIRST[stage] + m)[:, a, :]
                    nc.tensor.matmul(to, wh, chunk(hi, k, a * HT, HT), start=k == 0, stop=False)
                    nc.tensor.matmul(to, wh, chunk(lo, k, a * HT, HT), start=False, stop=False)
                    return nc.tensor.matmul(to, wl, chunk(hi, k, a * HT, HT), start=False, stop=k == C - 1)

                pe.wait_ge(w_ready, W_OF[stage] + 1)
                slot_free(FIRST[stage])
                slot_free(FIRST[stage] + 1)
                for k in range(C):
                    pe.wait_ge(lo_ready, STAGED[name] + k + 1)
                    for m in range(2):
                        for a in range(2):
                            last = products(m, k, a)
                        if k == C - 1:
                            last.then_inc(tile_done, 1)
                for m in range(2, dict((s[0], s[1]) for s in STAGES)[stage]):
                    if m % 2 == 0:
                        pe.wait_ge(w_ready, W_OF[stage] + m // 2 + 1)
                    slot_free(FIRST[stage] + m)
                    for a in range(2):
                        for k in range(C):
                            last = products(m, k, a)
                    last.then_inc(tile_done, 1)

            def ple(layer, norm):
                i = B_OF["ple", layer]
                block_there(i)
                pe.wait_ge(ple_loaded, 16 * (layer + 1))
                w = w_raw[:, PLACE[i][1], :].rearrange("p (k c) -> p k c", k=2)
                for m in range(C):
                    if m == 1:
                        spread(norm)
                    t = FIRST[f"ple{layer}"] + m
                    slot_free(t)
                    for a in range(2):
                        for k in range(2):
                            last = nc.tensor.matmul(slot(t)[:, a, :], w[:, k, m * P:(m + 1) * P],
                                                    ple_in[:, k, a * HT:(a + 1) * HT], start=k == 0, stop=k == 1)
                    last.then_inc(tile_done, 1)

            def mlp(layer):
                for n in range(Q4):
                    dense(f"up{layer}{n}")
                    dense(f"down{layer}{n}")

            def stats(n):
                if n >= 1:
                    pe.wait_ge(std_ready, n)
                if n not in DIRECT:
                    pe.wait_ge(sq_added, adds(n) + C - 1)
                for m in range(C if n in DIRECT else 1):
                    src, end = sq_sum[:, :], 0
                    if n in DIRECT:
                        pe.wait_ge(sq_ready, C * n + m + 1)
                        src, end = sq[:, (C * n + m) % 4, :], C - 1
                    for i in range(4):
                        last = nc.tensor.matmul(STAT_Q(n)[32 * i:32 * i + 32, :], tab("mean")[:, 0:32],
                                                src[:, QT * i:QT * (i + 1)], start=m == 0, stop=m == end)
                    last.then_inc(sq_summed if m == end else sq_taken, 1)

            def spread(n):
                pe.wait_ge(rstd_ready, n + 1)
                for i in range(4):
                    at = QT * (i % 2)
                    last = nc.tensor.matmul(STAT[:, i // 2, at:at + QT], tab("pick")[:, P * i:P * (i + 1)], rstd_q[:, :],
                                            start=True, stop=True)
                last.then_inc(rstd_out, 1)

            pe.wait_ge(consts_in, 32)
            stats(0)
            spread(0)
            dense("pw1")
            pe.wait_ge(rstd_ready, 1)
            for n, (i, m, j) in enumerate(DIAGONALS):
                t = FIRST["taps"] + i
                first, end = j == TAP_TILES[i][1], j == TAPS - 1
                if first:
                    slot_free(t)
                    pe.wait_ge(glu_done, 2 * m + 1)
                pe.wait_ge(diag_ready, n + 1)
                nc.tensor.matmul(ps[:, 2 * (t % 3), :], diag[:, n % 18, :], conv_in[:, m, j:j + SEQ], start=first,
                                 stop=end).then_inc(tile_done if end else diag_used, 1)
            pe.wait_ge(y_added, len(EARLY) - 1)
            for i, m in enumerate([None] + LATE):
                src = sq_sum[:, :] if m is None else y[:, m, :]
                if m is not None:
                    prompt_convolved(pe, m)
                for a in range(2):
                    last = nc.tensor.matmul(STAT[:, a, :], tab("mean"), src[:, a * HT:(a + 1) * HT],
                                            start=i == 0, stop=i == len(LATE))
            last.then_inc(mean_ready, 1)
            stats(1)
            spread(1)
            dense("pw2")
            stats(2)
            spread(2)
            stats(3)
            spread(3)
            mlp(0)
            stats(4)
            ple(0, 4)
            dense("gate0")
            stats(5)
            spread(5)
            dense("q")
            dense("kv_cmp")
            dense("k_rot")
            pe.wait_ge(wg_ready, 1)
            t = FIRST["gates"]
            slot_free(t)
            for a in range(2):
                for k in range(C):
                    for w, h in ((wg_hi, ha), (wg_lo, ha), (wg_hi, hb)):
                        last = nc.tensor.matmul(slot(t)[0:48, a, :], w[:, 48 * k:48 * k + 48], chunk(h, k, a * HT, HT),
                                                start=k == 0 and (w, h) == (wg_hi, ha), stop=k == C - 1 and h is hb)
            last.then_inc(tile_done, 1)
            pe.wait_ge(pad_zero, 2)
            for part in range(2):
                j = W_OF["v_tok"] + part
                wh, wl = w_hi[j % 2], w_lo[j % 2]
                pe.wait_ge(w_ready, j + 1)
                for i in range(TT):
                    t = FIRST["v_tok"] + TT * part + i
                    slot_free(t)
                    to = ps[:, 2 * (t % 3), 0:256]
                    for k in range(C):
                        nc.tensor.matmul(to, chunk(ha, k, i * P, P), wh[:, 256 * k:256 * k + 256], start=k == 0, stop=False)
                        nc.tensor.matmul(to, chunk(ha, k, i * P, P), wl[:, 256 * k:256 * k + 256], start=False, stop=False)
                        last = nc.tensor.matmul(to, chunk(hb, k, i * P, P), wh[:, 256 * k:256 * k + 256], start=False,
                                                stop=k == C - 1)
                    last.then_inc(tile_done, 1)
            t = FIRST["gates_t"]
            slot_free(t)
            pe.wait_ge(act_freed, FREED[FIRST["gates"]][1])
            for i in range(TT):
                rows = P if i < PT else NS
                last = nc.tensor.transpose(ps[0:rows, 2 * (t % 3), 48 * i:48 * i + 48], gates_f[:, i * P:i * P + rows],
                                           tab("ident")[0:48, 0:48])
            last.then_inc(tile_done, 1)

            block_there(B_OF["w1", 0])
            lo, _ = PAR["pe"]
            for v in range(2):
                for j in range(16):
                    last = nc.tensor.matmul(ps[0:1, 7, P * v:P * (v + 1)], par[:, lo + 16 * v + j:lo + 16 * v + j + 1],
                                            w1[:, v, j, :], start=j == 0, stop=j == 15)
            last.then_inc(c_mm, 1)
            pe.wait_ge(pairs_in, 16 * 4)
            for v in range(2):
                for j in range(16):
                    last = nc.tensor.matmul(ps[:, 6, 128 * v:128 * v + 124].rearrange("p (g c) -> p g c", g=KV),
                                            w1[:, v, j, :], kv_pairs[:, v, :, 2 * j:2 * j + 16 * (NCP - 2) + 1:16],
                                            start=j == 0, stop=j == 15)
                last.then_inc(phid_mm, 1)
            pe.wait_ge(c_there, 1)
            for v in range(2):
                last = nc.tensor.transpose(ps[:, 7, 256 + v:257 + v], c_row[:, P * v:P * (v + 1)], tab("ident")[0:1, 0:1])
            last.then_inc(c_mm, 1)
            pe.wait_ge(c_there, 2)
            pe.wait_ge(phid_ready, 2)
            for e in range(2):
                nc.tensor.matmul(ps[64 * e:64 * e + 64, 7, 0:64].rearrange("p (g c) -> p g c", g=2), w2[:, 0, :],
                                 hid_p[:, 0, e, :, :], start=True, stop=True)
            for g in range(2):
                for k in range(4):
                    last = nc.tensor.matmul(ps[32 * k:32 * k + 32, 7, 64 + 64 * g:128 + 64 * g],
                                            hid_p[:, 1, k % 2, g, :], w2[:, 1, :], start=True, stop=True)
            last.then_inc(pw2_mm, 1)

            def compress_out(u):
                b, v = u // 2, u % 2
                pe.wait_ge(hid_ready, u + 1)
                if u == 1:
                    pe.wait_ge(pw2_out, 2)
                if u >= 2:
                    pe.wait_ge(w2_out, u - 1)
                hid = hid_s[:, u % 2, :].rearrange("p (c g) -> p g c", g=KV)
                if v == 0:
                    for e in range(2):
                        last = nc.tensor.matmul(ps[64 * e:64 * e + 64, 6, 0:128].rearrange("p (g c) -> p g c", g=2),
                                                w2[:, 0, :], hid[:, e:e + 3:2, :], start=True, stop=True)
                else:
                    lo = 64 * (b % 2)
                    for g in range(KV):
                        last = nc.tensor.matmul(ps[lo:lo + 64, 7, 64 * g:64 * g + 64], hid[:, g, :], w2[:, 1, :],
                                                start=True, stop=True)
                last.then_inc(w2_mm, 1)

            slot_free(FIRST["out"] + 0)
            slot_free(FIRST["out"] + 1)
            slot_free(FIRST["out"] + 2)
            for u in range(2 * NB):
                b, v = u // 2, u % 2
                i = B_OF["cmp_pages", b]
                block_there(i)
                if u >= 3:
                    pe.wait_ge(hid_ab, u - 2)
                for half in range(2):
                    for j in range(8):
                        rhs = block_at(i, 0, BLK).rearrange("p (a n) -> p a n", a=PAGES)[:, :, 256 * v + 32 * j:256 * v + 32 * j + 32]
                        last = nc.tensor.matmul(ps[:, 2 * (u % 3) + half, 0:256], w1[:, v, 8 * half + j, :], rhs,
                                                start=j == 0, stop=j == 7)
                last.then_inc(cmp_mm, 1)
                if u >= 1:
                    compress_out(u - 1)
            compress_out(2 * NB - 1)

            pe.wait_ge(w2_out, 2 * NB - 1)
            pe.wait_ge(hid_ab, 2 * NB)
            pe.wait_ge(qbd_ready, 1)
            for b in range(NB):
                for g in range(2):
                    last = nc.tensor.matmul(ps[64 * g:64 * g + 64, 4, 64 * b:64 * b + 64],
                                            qbd[:, b, g, :, :].rearrange("p e m -> p (e m)"), k_cmp_s[:, b, g, :],
                                            start=True, stop=True)
            last.then_inc(sc_mm, 1)
            for n in range(PT):
                for c in range(C):
                    last = nc.tensor.matmul(ps[:, n, 2 * NCP * c:2 * NCP * (c + 1)], q[:, c, n * P:(n + 1) * P],
                                            k_cmp_p[:, c // 4, :, :].rearrange("p e c -> p (e c)"), start=True, stop=True)
                last.then_inc(sc_mm, 1)
                if n == 1:
                    pe.wait_ge(pc_ready, 1)
                    pe.wait_ge(w2_out, 2 * NB)
                    pe.wait_ge(tables_in, 16)
                    nc.tensor.matmul(ps[:, 5, :], tab("same_q"), pc_s, start=True, stop=True).then_inc(imp_mm, 1)
                    for j in range(4):
                        last = nc.tensor.transpose(ps[:, 6, 128 * j:128 * j + 128], pc_s[:, 128 * j:128 * j + 128], tab("ident"))
                    last.then_inc(ct_mm, 1)
            for n in range(PT):
                pe.wait_ge(pc_ready, n + 2)
                pe.wait_ge(sc_sub, n + 2)
                if n == 0:
                    pe.wait_ge(drop_ready, 1)
                pe.wait_ge(ct_out, n + 1)
                if n >= 1:
                    pe.wait_ge(co_read, n)
                for j in range(4):
                    last = nc.tensor.transpose(ps[:, 4 + n % 2, 128 * j:128 * j + 128], pc[n][:, 128 * j:128 * j + 128],
                                               tab("ident"))
                last.then_inc(ct_mm, 1)
                pe.wait_ge(ct_out, n + 2)
                for j in range(4):
                    last = nc.tensor.matmul(ps[:, 6 + j // 2, 256 * (j % 2):256 * (j % 2) + 256], pc_t_p[:, j, :],
                                            v_cmp_p[:, j // 2, :], start=True, stop=True)
                last.then_inc(co_mm, 1)

            def scores_s(b):
                i = B_OF["sel_pages", b]
                block_there(i)
                block_there(B_OF["win_k", b])
                if b >= 1:
                    pe.wait_ge(s_read, b)
                    pe.wait_ge(s_win, b)
                sel = block_at(i, 0, BLK).rearrange("p (a n) -> p a n", a=PAGES)
                win = window(b)
                for g in range(2):
                    part = slice(64 * g, 64 * g + 64)
                    qq = qbd[:, b, g, :, :].rearrange("p e m -> p (e m)")
                    for a in range(2):
                        nc.tensor.matmul(ps[part, a, :], qq, sel[:, 4 * a:4 * a + 4, P * g:P * g + P], start=True, stop=True)
                    nc.tensor.matmul(ps[part, 2, :], qq, win[:, g, :], start=True, stop=True)
                    nc.tensor.matmul(ps[part, 3, 0:NS], qq, k_rot[:, g, SEQ:T], start=True, stop=True)
                    last = nc.tensor.matmul(ps[part, 3, NS:2 * NS], qq, k_rot[:, 2 + g, SEQ:T], start=True, stop=True)
                last.then_inc(s_mm, 1)

            def t_slot(n):
                if n >= 2:
                    b, k = [(b, k) for b in range(NB + 1) for k in range(5) if (b, k) != (0, 4)][n - 2]
                    if k == 4:
                        pe.wait_ge(t_fin, b)
                    else:
                        pe.wait_ge(t_out, 4 * b + k + 1)
                return ps[:, 4 + n % 2, :]

            def finish_s(b, n):
                to = t_slot(n)
                pe.wait_ge(acc_ready, b + 1)
                for g in range(2):
                    last = nc.tensor.transpose(to[:, 128 * g:128 * g + 128], acc_s[:, b % 2, 128 * g:128 * g + 128], tab("ident"))
                last.then_inc(t_mm, 1)

            pe.wait_ge(co_read, PT)
            pe.wait_ge(qbd_ready, 2)
            pe.wait_ge(rot_done, 12)
            scores_s(0)
            for b in range(NB):
                if b + 1 < NB:
                    scores_s(b + 1)
                i = B_OF["sel_pages", b]
                sel = block_at(i, 0, BLK).rearrange("p (a n) -> p a n", a=PAGES)[:, :, 256:512]
                win = window(b)
                pp = p_s[:, b % 2, :]
                pe.wait_ge(s_exp, b + 1)
                for k, tiles in enumerate(([0, 128, 256, 384], [512, 640, 768, 896], [1088, 1216, 1344, 1472], [1024, 1600])):
                    to = t_slot(t_group(b, k))
                    w = P if k < 3 else NS
                    for j, at in enumerate(tiles):
                        last = nc.tensor.transpose(to[0:w, 128 * j:128 * j + 128], pp[:, at:at + w], tab("ident"))
                    last.then_inc(t_mm, 1)
                if b >= 1:
                    finish_s(b - 1, t_group(b, 4))
                if b >= 1:
                    pe.wait_ge(o_read, b)
                pe.wait_ge(t_out, 4 * b + 4)
                block_there(B_OF["win_v", b])
                for j in range(8):
                    nc.tensor.matmul(ps[:, 6, 0:256], pt_s[:, 128 * j:128 * j + 128], sel[:, j, :], start=j == 0, stop=False)
                nc.tensor.matmul(ps[:, 6, 0:256], pt_s[0:NS, 1536:1664], v_tok[0:NS, PT, 0:256], start=False, stop=True)
                for j in range(4):
                    nc.tensor.matmul(ps[:, 6, 256:512], pt_s[:, 1024 + 128 * j:1152 + 128 * j],
                                     win[:, 2 + j // 2, 256 * (j % 2):256 * (j % 2) + 256],
                                     start=j == 0, stop=False)
                nc.tensor.matmul(ps[:, 6, 256:512], pt_s[0:NS, 1664:1792], v_tok[0:NS, PT, 256:512], start=False, stop=True)
                half = slice(64 * (b % 2), 64 * (b % 2) + 64)
                nc.tensor.matmul(ps[:, 7, 0:256], pc_t_s[half, b // 2, :], v_cmp_s[half, b // 2, :],
                                 start=True, stop=True).then_inc(o_mm, 1)
            finish_s(NB - 1, t_group(NB, 0))

            items = ITEMS

            def p_scores(i):
                n, c, e, r = items[i]
                if i >= 4:
                    pe.wait_ge(p_exp, i - 3)
                part = slice(64 * e, 64 * e + 64)
                nc.tensor.matmul(ps[:, i % 4, 0:(n + 1) * P], q_rot[part, c, n * P:(n + 1) * P],
                                 k_rot[part, 2 * r + c // 4, 0:(n + 1) * P], start=True, stop=True).then_inc(p_mm, 1)

            def turn(what):
                t = TURN[what]
                if t >= 2:
                    kind, was = TRANSPOSED[t - 2]
                    pe.wait_ge(pt_out if kind == "item" else ft_out, was + 1)
                return 4 + t % 2

            def rows_transpose(k):
                n = k // 2
                pe.wait_ge(po_read, len(items) // PT * (n + 1))
                bank = turn(("rows", k))
                for c in range(4):
                    at = 512 * (k % 2) + 128 * c
                    last = nc.tensor.transpose(ps[:, bank, 128 * c:128 * c + 128], acc[:, n, at:at + 128], tab("ident"))
                last.then_inc(ft_mm, 1)

            def p_transpose(i):
                n = items[i][0]
                pe.wait_ge(p_exp, i + 1)
                bank = turn(("item", i))
                for j in range(n + 1):
                    last = nc.tensor.transpose(ps[:, bank, 128 * j:128 * j + 128], p_p[:, i % 4, 128 * j:128 * j + 128],
                                               tab("ident"))
                last.then_inc(pt_mm, 1)

            def p_out(i):
                n, c, e, r = items[i]
                pe.wait_ge(pt_out, i + 1)
                if i >= 2:
                    pe.wait_ge(po_read, i - 1)
                at = 256 * r + 64 * (2 * (c // 4) + e)
                for j in range(n + 1):
                    last = nc.tensor.matmul(ps[:, 6 + i % 2, 0:HD], pt_p[:, i % 2, 128 * j:128 * j + 128],
                                            v_tok[:, j, at:at + HD], start=j == 0, stop=j == n)
                last.then_inc(po_mm, 1)

            pe.wait_ge(t_fin, NB)
            N = len(items)
            p_scores(0)
            p_scores(1)
            for i in range(N):
                if i + 2 < N:
                    p_scores(i + 2)
                p_transpose(i)
                if i >= 1:
                    p_out(i - 1)
                if i == N // PT:
                    pe.wait_ge(po_read, i - 1)
                    for _ in range(WARM):
                        nc.tensor.matmul(ps[:, 6 + i % 2, :], tab("ident"), tab("cos")[:, 0:SEQ], start=True, stop=True)
                for kind, k in TRANSPOSED[TURN["item", i] + 1:TURN["item", i] + 2]:
                    if kind == "rows" and i < N - 1:
                        rows_transpose(k)
            p_out(N - 1)
            rows_transpose(2 * PT - 2)
            rows_transpose(2 * PT - 1)

            dense("out")
            stats(6)
            spread(6)
            stats(7)
            spread(7)
            mlp(1)
            stats(8)
            ple(1, 8)
            dense("gate1")

        @block.scalar
        def _(act):
            split_done = set()

            def split_weight(j):
                i = B_OF["w", j]
                k = PLACE[i][1]
                if j >= 2:
                    act.wait_ge(tile_done, W_END[j - 2])
                act.wait_ge(block_in[k], LOADED[i])
                nc.scalar.activation(w_hi[j % 2][:, :], w_raw[:, k, :], ACT.Copy).then_inc(w_hi_ready, 1)
                split_done.add(j)

            def tile(stage, m):
                t = FIRST[stage] + m
                per = TT if stage == "v_tok" else 2
                if stage in W_OF and m % per == 0:
                    j = W_OF[stage] + m // per + 1
                    if j != W_OF["out"] and j < len(W_END) and j not in split_done:
                        split_weight(j)
                act.wait_ge(tile_done, t + 1)
                return slot(t)

            def hi_part(name, k, src, src_ready=None):
                hi, _ = split_input(name)
                if src_ready is not None:
                    act.wait_ge(*src_ready)
                nc.scalar.activation(chunk(hi, k), src, ACT.Copy).then_inc(hi_ready, 1)

            def raw(name, k):
                i = STAGED[name] + k
                return sq[:, i % 4, :]

            def norm_hi(name, count, last_reader=None):
                if last_reader is not None:
                    act.wait_ge(tile_done, last_reader)
                for k in range(C):
                    hi_part(name, k, raw(name, k), (raw_ready, count + k + 1))
                    if k == 3 and name in ("mlp0", "mlp1"):
                        split_weight(W_OF["up" + name[3:] + "0"] + 1)

            def square(n, m, src):
                i = C * n + m
                if i >= 4:
                    was_n, was_m = (i - 4) // C, (i - 4) % C
                    if was_n not in DIRECT:
                        act.wait_ge(sq_added, adds(was_n) + max(was_m, 1))
                    elif was_m < C - 1:
                        act.wait_ge(sq_taken, adds(was_n) + was_m + 1)
                    else:
                        act.wait_ge(sq_summed, was_n + 1)
                dst = sq[:, i % 4, :]
                if len(src.shape) == 3:
                    dst = halves(dst)
                nc.scalar.activation(dst, src, ACT.Square).then_inc(sq_ready, 1)

            def std(n):
                act.wait_ge(sq_summed, n + 1)
                nc.scalar.activation(rstd_q[:, :], STAT_Q(n), ACT.Sqrt, bias=tab("eps")).then_inc(std_ready, 1)

            def square_x_chunk(n, update, m):
                act.wait_ge(x_ready, C * update + m + 1)
                square(n, m, x[:, m, :])

            def square_x(n, update):
                for m in range(C):
                    square_x_chunk(n, update, m)
                std(n)

            def to_mix(stage, n, bias=None):
                for m in range(C):
                    p = tile(stage, m)
                    if bias is None:
                        nc.scalar.activation(halves(mix[:, m, :]), p, ACT.Copy).then_inc(act_freed, 1)
                    else:
                        nc.scalar.activation(halves(mix[:, m, :]), p, ACT.Identity, bias=pcol(bias, m)).then_inc(act_freed, 1)
                    act.wait_ge(act_freed, FREED[FIRST[stage] + m][1])
                    square(n, m, mix[:, m, :])
                std(n)

            def mlp(layer, norm):
                for n in range(Q4):
                    name = f"hid{layer}{n}"
                    for m in range(C):
                        p = tile(f"up{layer}{n}", m)
                        i = STAGED[name] + m
                        act.wait_ge(lo_ready, i - 3)
                        nc.scalar.activation(halves(raw(name, m)), p, ACT.Relu).then_inc(act_freed, 1)
                        hi_part(name, m, raw(name, m), (raw_ready, RAW_OF[name] + m + 1))
                    for m in range(C):
                        p = tile(f"down{layer}{n}", m)
                        if n == 0:
                            nc.scalar.activation(halves(mix[:, m, :]), p, ACT.Copy).then_inc(act_freed, 1)
                        if n == Q4 - 1:
                            act.wait_ge(dve_freed, FREED[FIRST[f"down{layer}{n}"] + m][1])
                            square(norm, m, mix[:, m, :])
                std(norm)

            def x_hi(name, update):
                for k in range(C):
                    hi_part(name, k, x[:, k, :], (x_ready, C * update + k + 1))

            def ple(layer):
                for m in range(C):
                    p = tile(f"ple{layer}", m)
                    nc.scalar.activation(halves(emb[:, m, :]), p, ACT.Copy).then_inc(act_freed, 1)

            def gate(layer, norm=None):
                for m in range(C):
                    if m >= 1 and norm is not None:
                        square_x_chunk(norm, 2, m - 1)
                    p = tile(f"gate{layer}", m)
                    nc.scalar.activation(halves(mix[:, m, :]), p, ACT.Sigmoid,
                                         bias=pcol("b_ple", C * layer + m)).then_inc(act_freed, 1)

            for m in range(C):
                act.wait_ge(x_in[m // 2], 16)
                square(0, m, x[:, m, :])
            act.wait_ge(consts_in, 32)
            std(0)
            split_weight(0)
            norm_hi("conv", 0)
            act.wait_ge(wg_in, 32)
            nc.scalar.activation(wg_hi[:, :], w_gates[:, :], ACT.Copy).then_inc(wg_hi_ready, 1)
            def diagonals(first, last):
                for n in range(first, last):
                    i, m, j = DIAGONALS[n]
                    if n >= 18:
                        was, _, tap = DIAGONALS[n - 18]
                        act.wait_ge(diag_used, n - 17 - sum(d[2] == TAPS - 1 for d in DIAGONALS[:n - 17]))
                        if tap == TAPS - 1:
                            act.wait_ge(tile_done, FIRST["taps"] + was + 1)
                    nc.scalar.activation(diag[:, n % 18, :], tab("ident"), ACT.Copy,
                                         scale=pcol("w_dw", TAPS * m + j)).then_inc(diag_ready, 1)

            for m in range(C):
                p = tile("pw1", 2 * m)
                if m >= 2:
                    act.wait_ge(glu_done, 2 * m - 2)
                nc.scalar.activation(halves(sig[:, m % 2, :]), p, ACT.Sigmoid,
                                     bias=pcol("b_pw1", 2 * m)).then_inc(act_freed, 1)
                p = tile("pw1", 2 * m + 1)
                nc.scalar.activation(halves(val[:, m % 2, :]), p, ACT.Identity,
                                     bias=pcol("b_pw1", 2 * m + 1)).then_inc(act_freed, 1)
                if m == C - 2:
                    act.wait_ge(lo_ready, C)
                    diagonals(0, 18)
            diagonals(18, len(DIAGONALS))
            for i in range(2):
                t = FIRST["taps"] + 1 + i
                act.wait_ge(tile_done, t + 1)
                nc.scalar.activation(y[:, C - 2 + i, 0:SEQ], ps[:, 2 * (t % 3), :], ACT.Identity,
                                     bias=pcol("b_dw", C - 2 + i)).then_inc(act_freed, 1)
            for m in range(C):
                act.wait_ge(centred, m + 1)
                square(1, m, y[:, m, :])
            std(1)
            for m in range(C):
                act.wait_ge(normed, m + 1)
                i = STAGED["silu"] + m
                act.wait_ge(lo_ready, i - 3)
                nc.scalar.activation(raw("silu", m), y[:, m, :], ACT.Silu, scale=pcol("ln_g", m),
                                     bias=pcol("ln_b", m)).then_inc(silu_done, 1)
                hi_part("silu", m, raw("silu", m), (silu_done, m + 1))
                if m == 3:
                    split_weight(W_OF["pw2"] + 1)
            to_mix("pw2", 2, "b_pw2")
            square_x(3, 0)
            norm_hi("mlp0", RAW_OF["mlp0"], FIRST["up00"])
            mlp(0, 4)
            ple(0)
            x_hi("x0", 1)
            gate(0, 5)
            square_x_chunk(5, 2, C - 1)
            std(5)
            norm_hi("nsa", RAW_OF["nsa"], FIRST["ple0"])
            for stage, dst in (("q", q), ("kv_cmp", kv_cmp), ("k_rot", k_rot)):
                for m in range(C if stage == "q" else 4):
                    p = tile(stage, m)
                    scale = SCALE if stage == "q" else 1.0
                    if stage != "kv_cmp":
                        partners = q_rot[:, m, :] if stage == "q" else sq[:, m, :]
                        if stage == "k_rot" and m == 0:
                            act.wait_ge(lo_ready, STAGED["nsa"] + C)
                        nc.scalar.activation(halves(partners), p, ACT.Copy, scale=scale)
                    nc.scalar.activation(halves(dst[:, m, :]), p, ACT.Copy, scale=scale).then_inc(act_freed, 1)
                if stage != "kv_cmp":
                    act.wait_ge(act_freed, FREED[FIRST[stage] + (C if stage == "q" else 4) - 1][1])
                    partners, done = (q_rot, q_swapped) if stage == "q" else (sq, k_swapped)
                    for lo in range(0, P, HD):
                        for h in range(2):
                            act.dma_start(partners[lo + HALF * h:lo + HALF * (h + 1), :, :],
                                          dst[lo + HALF * (1 - h):lo + HALF * (2 - h), :, :]).then_inc(done, 16)
            act.wait_ge(tile_done, FIRST["gates"] + 1)
            nc.scalar.activation(halves(gates_f), slot(FIRST["gates"])[0:48], ACT.Sigmoid).then_inc(act_freed, 1)
            for n in range(2 * TT):
                i, part = n % TT, n // TT
                rows = P if i < PT else NS
                t = FIRST["v_tok"] + n
                tile("v_tok", n)
                nc.scalar.activation(v_tok[0:rows, i, 256 * part:256 * part + 256], ps[0:rows, 2 * (t % 3), 0:256],
                                     ACT.Copy).then_inc(act_freed, 1)
            t = FIRST["gates_t"]
            act.wait_ge(tile_done, t + 1)
            for rows, i, n in ((P, 0, PT), (NS, PT, 1)):
                last = nc.scalar.activation(gates[0:rows, i:i + n, :], ps[0:rows, 2 * (t % 3), 48 * i:48 * (i + n)].rearrange(
                                                "p (i c) -> p i c", c=48), ACT.Copy)
            last.then_inc(act_freed, 1)
            act.wait_ge(c_mm, 1)
            nc.scalar.activation(c_row, ps[0:1, 7, 0:2 * P], ACT.Copy).then_inc(c_there, 1)
            act.wait_ge(c_mm, 2)
            nc.scalar.activation(c_vec[:, :], ps[:, 7, 256:258], ACT.Copy).then_inc(c_there, 1)
            act.wait_ge(c_there, 2)
            act.wait_ge(phid_zero, 1)
            act.wait_ge(phid_mm, 2)
            for v in range(2):
                nc.scalar.activation(hid_p[:, v, :, :, 0:NCP - 1].rearrange("p e g c -> p g e c"),
                                     ps[:, 6, 128 * v:128 * v + 124].rearrange("p (g e c) -> p g e c", g=2, e=2),
                                     ACT.Silu, bias=c_vec[:, v:v + 1]).then_inc(phid_ready, 1)
            act.wait_ge(pw2_mm, 1)
            act.wait_ge(bd_zero, 2)
            for e in range(2):
                part = slice(64 * e, 64 * e + 64)
                last = nc.scalar.activation(k_cmp_p[part, :, e, :], ps[part, 7, 0:64].rearrange("p (g c) -> p g c", g=2),
                                            ACT.Copy)
            last.then_inc(pw2_out, 1)
            for k in range(4):
                last = nc.scalar.activation(v_cmp_p[32 * k:32 * k + 32, :, 64 * k:64 * k + 64],
                                            ps[32 * k:32 * k + 32, 7, 64:192].rearrange("p (g f) -> p g f", g=2), ACT.Copy)
            last.then_inc(pw2_out, 1)
            act.wait_ge(rot_done, 12)

            def hid_silu(u):
                act.wait_ge(hid_ab, u + 1)
                nc.scalar.activation(hid_s[:, u % 2, :], hid_s[:, u % 2, :], ACT.Silu).then_inc(hid_ready, 1)

            for u in range(2 * NB):
                act.wait_ge(cmp_mm, u + 1)
                if u >= 2:
                    act.wait_ge(w2_mm, u - 1)
                nc.scalar.activation(hid_s[:, u % 2, :], ps[:, 2 * (u % 3), 0:256], ACT.Identity,
                                     bias=c_vec[:, u % 2:u % 2 + 1]).then_inc(hid_a, 1)
                hid_silu(u)

            def probs_transposed(n):
                act.wait_ge(w2_mm, 2 * NB)
                act.wait_ge(ct_mm, n + 2)
                if n >= 1:
                    act.wait_ge(co_mm, n)
                nc.scalar.activation(pc_t_p, ps[:, 4 + n % 2, :].rearrange("p (j t) -> p j t", j=4),
                                     ACT.Copy).then_inc(ct_out, 1)

            for n in range(5):
                act.wait_ge(sc_sub, n + 1)
                pr = pc[n - 1] if n else pc_s
                nc.scalar.activation(pr, pr, ACT.Exp).then_inc(c_exp, 1)
                if n == 2:
                    act.wait_ge(ct_mm, 1)
                    act.wait_ge(sc_mm, 5)
                    nc.scalar.activation(pc_t_s, ps[:, 6, :].rearrange("p (j t) -> p j t", j=4), ACT.Copy).then_inc(ct_out, 1)
                    probs_transposed(0)
            for n in range(1, PT):
                probs_transposed(n)

            def window_out(b):
                act.wait_ge(s_mm, b + 1)
                if b == 0:
                    act.wait_ge(co_mm, PT)
                if b >= 2:
                    act.wait_ge(t_mm, t_group(b - 2, 3) + 1)
                nc.scalar.activation(p_s[:, b % 2, 1088:1600], ps[:, 2, :], ACT.Copy).then_inc(s_win, 1)

            act.wait_ge(co_mm, PT)
            window_out(0)
            for b in range(NB):
                pp = p_s[:, b % 2, :]
                act.wait_ge(s_max, 2 * b + 1)
                nc.scalar.activation(pp[:, 0:1088], pp[:, 0:1088], ACT.Exp, bias=stat_s[:, b, 0:1],
                                     accum_out=stat_s[:, b, 2:3])
                act.wait_ge(s_max, 2 * b + 2)
                nc.scalar.activation(pp[:, 1088:1664], pp[:, 1088:1664], ACT.Exp, bias=stat_s[:, b, 1:2],
                                     accum_out=stat_s[:, b, 3:4]).then_inc(s_exp, 1)
                if b + 1 < NB:
                    window_out(b + 1)
                for k in range(4):
                    act.wait_ge(t_mm, t_group(b, k) + 1)
                    if k == 0 and b >= 1:
                        act.wait_ge(o_mm, b)
                    w, n = (P, 512) if k < 3 else (NS, 256)
                    nc.scalar.activation(pt_s[0:w, 512 * k:512 * k + n], ps[0:w, 4 + t_group(b, k) % 2, 0:n],
                                         ACT.Copy).then_inc(t_out, 1)

            items = ITEMS

            def p_move(i):
                n = items[i][0]
                act.wait_ge(pt_mm, i + 1)
                if i >= 2:
                    act.wait_ge(po_mm, i - 1)
                nc.scalar.activation(pt_p[:, i % 2, 0:(n + 1) * P], ps[:, 4 + TURN["item", i] % 2, 0:(n + 1) * P],
                                     ACT.Copy).then_inc(pt_out, 1)
                for kind, k in TRANSPOSED[TURN["item", i] + 1:TURN["item", i] + 2]:
                    if kind == "rows":
                        rows_move(k)

            def rows_move(k):
                n, h = k // 2, k % 2
                if k == 0:
                    act.wait_ge(win_stored[0], 16 * (NB // 2))
                    act.wait_ge(win_stored[1], 16 * (NB // 2))
                act.wait_ge(ft_mm, k + 1)
                nc.scalar.activation(attn_t[:, 4 * h:4 * h + 4, n * P:(n + 1) * P],
                                     ps[:, 4 + TURN["rows", k] % 2, :].rearrange("p (c t) -> p c t", c=4),
                                     ACT.Copy).then_inc(ft_out, 1)

            act.wait_ge(t_mm, 5 * NB)
            for i, (n, c, e, r) in enumerate(items):
                act.wait_ge(p_max, i + 1)
                if i >= 4:
                    act.wait_ge(pt_mm, i - 3)
                    act.wait_ge(po_read, i - 3)
                nc.scalar.activation(p_p[:, i % 4, 0:(n + 1) * P], ps[:, i % 4, 0:(n + 1) * P], ACT.Exp,
                                     bias=nmax_p[:, i % 8:i % 8 + 1], accum_out=sum_p[:, i % 8:i % 8 + 1]).then_inc(p_exp, 1)
                if i >= 1:
                    p_move(i - 1)
                if i in (64, 80):
                    act.wait_ge(o_mm, NB)
                    split_weight(W_OF["out"] + (i - 64) // 16)
            p_move(len(items) - 1)
            rows_move(2 * PT - 1)
            act.wait_ge(ft_out, 2 * PT)
            act.wait_ge(ft_mm, 2 * PT)
            for m in range(C):
                hi_part("attn", m, attn_t[:, m, :], (t_fin, NB))
            to_mix("out", 6)
            square_x(7, 3)
            norm_hi("mlp1", RAW_OF["mlp1"], FIRST["up10"])
            mlp(1, 8)
            ple(1)
            x_hi("x1", 4)
            gate(1)

        @block.vector
        def _(dve):
            steps = [0]

            def step(ins):
                steps[0] += 1
                ins.then_inc(dve_step, 1)
                return steps[0]

            def after(n):
                dve.wait_ge(dve_step, n)

            def get_rstd(n):
                dve.wait_ge(std_ready, n + 1)
                nc.vector.reciprocal(rstd_q[:, :], rstd_q[:, :]).then_inc(rstd_ready, 1)
                dve.wait_ge(rstd_out, n + 1)

            def lo_part(name, k, src):
                hi, lo = split_input(name)
                dve.wait_ge(hi_ready, STAGED[name] + k + 1)
                nc.vector.tensor_tensor(chunk(lo, k), src, chunk(hi, k).bitcast(F32), ALU.subtract).then_inc(lo_ready, 1)

            def raw(name, k):
                return sq[:, (STAGED[name] + k) % 4, :]

            def add_square(n, m):
                if m == 0:
                    return
                dve.wait_ge(sq_ready, C * n + m + 1)
                if m > 1:
                    dve.wait_ge(sq_added, adds(n) + m - 1)
                so_far = sq[:, C * n % 4, :] if m == 1 else sq_sum[:, :]
                nc.vector.tensor_tensor(sq_sum[:, :], so_far, sq[:, (C * n + m) % 4, :], ALU.add).then_inc(sq_added, 1)

            def pre_norm(n, g, name):
                get_rstd(n)
                for m in range(C + 1):
                    if m < C:
                        nc.vector.scalar_tensor_tensor(halves(raw(name, m)), halves(x[:, m, :]),
                                                       pcol("norm_g", C * g + m), STAT, ALU.mult, ALU.mult).then_inc(raw_ready, 1)
                    if m >= 1:
                        lo_part(name, m - 1, raw(name, m - 1))

            def mlp(layer, norm):
                for n in range(Q4):
                    name = f"hid{layer}{n}"
                    for m in range(C):
                        dve.wait_ge(act_freed, FREED[FIRST[f"up{layer}{n}"] + m][1])
                        r = raw(name, m)
                        nc.vector.tensor_tensor(r, r, r, ALU.mult).then_inc(raw_ready, 1)
                        lo_part(name, m, r)
                    for m in range(C if n else 0):
                        if n == Q4 - 1 and m >= 1:
                            add_square(norm, m - 1)
                        t = FIRST[f"down{layer}{n}"] + m
                        dve.wait_ge(tile_done, t + 1)
                        dve.wait_ge(act_freed, FREED[FIRST[f"down{layer}0"] + m][1])
                        if n >= 2:
                            dve.wait_ge(dve_freed, FREED[FIRST[f"down{layer}{n - 1}"] + m][1])
                        nc.vector.tensor_tensor(halves(mix[:, m, :]), slot(t), halves(mix[:, m, :]),
                                                ALU.add).then_inc(dve_freed, 1)
                add_square(norm, C - 1)

            def post_norm(n, g):
                get_rstd(n)
                done = []
                for m in range(C + 1):
                    if m < C:
                        done.append(step(nc.vector.scalar_tensor_tensor(
                            halves(mix[:, m, :]), halves(mix[:, m, :]), pcol("norm_g", C * g + m), STAT,
                            ALU.mult, ALU.mult)))
                    if m >= 1:
                        after(done[m - 1])
                        nc.vector.tensor_tensor(x[:, m - 1, :], x[:, m - 1, :], mix[:, m - 1, :],
                                                ALU.add).then_inc(x_ready, 1)

            def ple(layer, norm=None):
                for m in range(C):
                    dve.wait_ge(act_freed, FREED[FIRST[f"gate{layer}"] + m][1])
                    after(step(nc.vector.tensor_tensor(mix[:, m, :], mix[:, m, :], emb[:, m, :], ALU.mult)))
                    nc.vector.tensor_tensor(x[:, m, :], x[:, m, :], mix[:, m, :], ALU.add).then_inc(x_ready, 1)
                    if norm is not None and m >= 1:
                        add_square(norm, m - 1)
                if norm is not None:
                    add_square(norm, C - 1)

            for i in range(4):
                dve.wait_ge(x_in[i], 16)
            for m in range(C):
                add_square(0, m)
            dve.wait_ge(consts_in, 32)
            pre_norm(0, 0, "conv")
            dve.wait_ge(pad_done, 1)
            def conv_samples(m):
                dve.wait_ge(tap_products, m + 1)
                ys = y[:, m, SEQ:].rearrange("p (b t) -> p b t", t=DT)
                after(step(nc.vector.tensor_reduce(ys, tap_prod, AX.X, ALU.add)))
                nc.vector.tensor_scalar(ys, ys, pcol("b_dw", m), None, ALU.add).then_inc(sample_conv, 1)

            done = 0
            for m in range(C - 2):
                dve.wait_ge(glu_done, 2 * m + 1)
                yp = y[:, m, 0:SEQ]
                on_way = []
                for j in range(TAPS if m < TAP_TILES[0][0] else TAP_TILES[0][1]):
                    w, e = pcol("w_dw", TAPS * m + j), conv_in[:, m, j:j + SEQ]
                    to = odd_taps if j % 2 else yp
                    if j >= 2:
                        after(on_way[j - 2])
                    if j == 0:
                        on_way.append(step(nc.vector.tensor_scalar(to, e, w, pcol("b_dw", m), ALU.mult, ALU.add)))
                    elif j == 1:
                        on_way.append(step(nc.vector.tensor_scalar(to, e, w, None, ALU.mult)))
                    else:
                        on_way.append(step(nc.vector.scalar_tensor_tensor(to, e, w, to, ALU.mult, ALU.add)))
                    if m >= 3 and j == TAPS // 2:
                        conv_samples(done)
                        done += 1
                after(on_way[-1])
                if m == TAP_TILES[0][0]:
                    t = FIRST["taps"]
                    dve.wait_ge(tile_done, t + 1)
                    nc.vector.tensor_tensor(yp, yp, ps[:, 2 * (t % 3), :], ALU.add).then_inc(dve_freed, 1)
                    dve.wait_ge(dve_freed, FREED[t][1])
                nc.vector.tensor_tensor(yp, yp, odd_taps, ALU.add).then_inc(conv_done, 1)
                if m < C - 3:
                    conv_samples(done)
                    done += 1
            assert done == C
            dve.wait_ge(mean_ready, 1)
            for m in range(C + 2):
                if m < C:
                    nc.vector.tensor_tensor(halves(y[:, m, :]), halves(y[:, m, :]), STAT, ALU.subtract).then_inc(centred, 1)
                if m >= 2:
                    add_square(1, m - 2)
            get_rstd(1)
            for m in range(C + 2):
                if m < C:
                    nc.vector.tensor_tensor(halves(y[:, m, :]), halves(y[:, m, :]), STAT, ALU.mult).then_inc(normed, 1)
                if m >= 2:
                    dve.wait_ge(silu_done, m - 1)
                    lo_part("silu", m - 2, raw("silu", m - 2))
            for m in range(C):
                add_square(2, m)
            post_norm(2, 1)
            pre_norm(3, 2, "mlp0")
            mlp(0, 4)
            post_norm(4, 3)
            for m in range(C):
                lo_part("x0", m, x[:, m, :])
            ple(0, 5)
            pre_norm(5, 4, "nsa")
            dve.wait_ge(tables_in, 16)
            dve.wait_ge(q_swapped, 16 * 4)
            for i in range(C):
                tmp, to = rope_tmp[:, i % 2, :], q_rot[:, i, :]
                step(nc.vector.tensor_tensor(tmp, q[:, i, :], tab("cos"), ALU.mult))
                after(step(nc.vector.tensor_tensor(to, to, tab("sin"), ALU.mult)))
                nc.vector.tensor_tensor(to, to, tmp, ALU.add).then_inc(rot_done, 1)
            dve.wait_ge(k_swapped, 16 * 4)
            for i in range(4):
                to, other = k_rot[:, i, :], sq[:, i, :]
                step(nc.vector.tensor_tensor(other, other, tab("sin"), ALU.mult))
                after(step(nc.vector.tensor_tensor(to, to, tab("cos"), ALU.mult)))
                nc.vector.tensor_tensor(to, to, other, ALU.add).then_inc(rot_done, 1)

            def chain(ins):
                after(step(ins))

            for u in range(2 * NB):
                b, v = u // 2, u % 2
                dve.wait_ge(hid_a, u + 1)
                nc.vector.tensor_tensor(hid_s[:, u % 2, 0:252], ps[:, 2 * (u % 3) + 1, 4:256], hid_s[:, u % 2, 0:252],
                                        ALU.add).then_inc(hid_ab, 1)
                for w in ([u - 1] if u >= 1 else []) + ([u] if u == 2 * NB - 1 else []):
                    b, v = w // 2, w % 2
                    dve.wait_ge(w2_mm, w + 1)
                    if v == 0:
                        nc.vector.tensor_copy(k_cmp_s[:, b, :, :].rearrange("p g c -> p (g c)"), ps[:, 6, 0:128]).then_inc(w2_out, 1)
                    else:
                        half = slice(64 * (b % 2), 64 * (b % 2) + 64)
                        nc.vector.tensor_copy(v_cmp_s[half, b // 2, :], ps[half, 7, 0:256]).then_inc(w2_out, 1)

            def block_queries(src):
                for g in range(2):
                    for e in range(2):
                        part = slice(64 * e, 64 * e + 64)
                        last = nc.vector.tensor_copy(
                            qbd[part, :, g, e, :].rearrange("p b (r i) -> p b r i", r=REP),
                            src[part, 4 * g:4 * g + 4, SEQ:T].rearrange("p r (b i) -> p b r i", b=NB))
                last.then_inc(qbd_ready, 1)

            dve.wait_ge(qbd_zero, 1)
            block_queries(q)

            def groups(n):
                k, w, at = (NB, NCS, 0) if n == 0 else (16, NCP, 8 + 16 * (n - 1))
                pr = pc[n - 1] if n else pc_s
                return (pr.rearrange("p (k w) -> p k w", k=k), cmax[:, at:at + k].rearrange("p (k o) -> p k o", o=1),
                        csum[:, at:at + k].rearrange("p (k o) -> p k o", o=1), (P, k, w))

            def less_max(n):
                pr, mx, _, shape = groups(n)
                dve.wait_ge(sc_mm, 5 if n > 2 else n + 1)
                if n == 0:
                    sc = ps[:, 4, :].rearrange("p (k w) -> p k w", k=NB)
                    chain(nc.vector.tensor_copy(pr, sc))
                    chain(nc.vector.memset(pr[:, :, NCS - 1:NCS], NEG))
                else:
                    a = CON["cmp_add"][0] + NCP * (n - 1)
                    m = con[:, a:a + NCP].rearrange("p (o w) -> p o w", o=1).to_broadcast(shape)
                    chain(nc.vector.tensor_tensor(pr, ps[:, n - 1, :].rearrange("p (k w) -> p k w", k=16), m, ALU.add))
                chain(nc.vector.tensor_reduce(mx, pr, AX.X, ALU.max))
                nc.vector.tensor_tensor(pr, pr, mx.to_broadcast(shape), ALU.subtract).then_inc(sc_sub, 1)
            def over_sum(n):
                pr, mx, sm, shape = groups(n)
                dve.wait_ge(c_exp, n + 1)
                chain(nc.vector.tensor_reduce(sm, pr, AX.X, ALU.add))
                chain(nc.vector.reciprocal(sm, sm))
                if n == 0:
                    nc.vector.tensor_tensor(pr, pr, sm.to_broadcast(shape), ALU.mult).then_inc(pc_ready, 1)
                else:
                    g = gates[:, n - 1, :].rearrange("p (k o) -> p k o", o=3)[:, :, 0:1]
                    chain(nc.vector.tensor_tensor(sm, sm, g, ALU.mult))
                    a = CON["cmp_mul"][0] + NCP * (n - 1)
                    m = con[:, a:a + NCP].rearrange("p (o w) -> p o w", o=1).to_broadcast(shape)
                    nc.vector.tensor_tensor(pr, pr, m, ALU.mult).then_inc(pc_ready, 1)

            def dropped_blocks():
                dve.wait_ge(imp_mm, 1)
                both = ps[:, 5, :].rearrange("p (b s w) -> p b s w", b=NB, w=4)
                chain(nc.vector.tensor_reduce(imp.rearrange("p b (s o) -> p b s o", o=1), both, AX.X, ALU.add))
                chain(nc.vector.tensor_tensor(imp[:, :, 1:16], both[:, :, 0:15, 3], imp[:, :, 1:16], ALU.add))
                lo = least[:, 0:8].rearrange("p (b o) -> p b o", o=1)
                hi = least[:, 8:16].rearrange("p (b o) -> p b o", o=1)
                no = tab("block_no").rearrange("p (o s) -> p o s", o=1).to_broadcast((P, NB, 16))
                chain(nc.vector.tensor_reduce(lo, imp[:, :, 1:15], AX.X, ALU.min))
                chain(nc.vector.tensor_tensor(eq[:, :, 1:15], imp[:, :, 1:15], lo.to_broadcast((P, NB, 14)), ALU.is_equal))
                chain(nc.vector.tensor_tensor(eq[:, :, 1:15], eq[:, :, 1:15], no[:, :, 1:15], ALU.mult))
                chain(nc.vector.tensor_reduce(hi, eq[:, :, 1:15], AX.X, ALU.max))
                chain(nc.vector.tensor_tensor(drop, no, hi.to_broadcast((P, NB, 16)), ALU.is_equal))
                nc.vector.tensor_scalar(drop, drop, NEG, None, ALU.mult).then_inc(drop_ready, 1)

            def rows_started(n):
                dve.wait_ge(co_mm, n + 1)
                _, _, sm, _ = groups(n + 1)
                nc.vector.tensor_tensor(acc[:, n, :].rearrange("p (k d) -> p k d", d=HD),
                                        ps[:, 6:8, :].rearrange("p a (k d) -> p (a k) d", d=HD),
                                        sm.to_broadcast((P, 16, HD)), ALU.mult).then_inc(co_read, 1)

            less_max(0)
            over_sum(0)
            less_max(1)
            less_max(2)
            over_sum(1)
            dropped_blocks()
            over_sum(2)
            less_max(3)
            less_max(4)
            over_sum(3)
            rows_started(0)
            over_sum(4)
            for n in range(1, PT):
                rows_started(n)
            block_queries(q_rot)

            def scores_out(b):
                pp = p_s[:, b % 2, :]
                dve.wait_ge(s_mm, b + 1)
                if b >= 2:
                    dve.wait_ge(t_mm, t_group(b - 2, 3) + 1)
                d = drop[:, b, :].rearrange("p (s o) -> p s o", o=1).to_broadcast((P, 16, HD))
                step(nc.vector.tensor_tensor(pp[:, 0:1024].rearrange("p (s w) -> p s w", w=HD),
                                             ps[:, 0:2, :].rearrange("p a (s w) -> p (a s) w", w=HD), d, ALU.add))
                a = CON["new_add"][0] + NS * b
                step(nc.vector.tensor_tensor(pp[:, 1024:1088], ps[:, 3, 0:NS], con[:, a:a + NS], ALU.add))
                nc.vector.tensor_tensor(pp[:, 1600:1664], ps[:, 3, NS:2 * NS], con[:, a:a + NS], ALU.add).then_inc(s_read, 1)
                after(steps[0])
                nc.vector.tensor_reduce(stat_s[:, b, 0:1], pp[:, 0:1088], AX.X, ALU.max, negate=True).then_inc(s_max, 1)
                dve.wait_ge(s_win, b + 1)
                chain(nc.vector.tensor_tensor(pp[:, 1088:1096], pp[:, 1088:1096], tab("win_add"), ALU.add))
                dve.wait_ge(s_read, b + 1)
                nc.vector.tensor_reduce(stat_s[:, b, 1:2], pp[:, 1088:1664], AX.X, ALU.max, negate=True).then_inc(s_max, 1)

            def rows_out(b):
                a = acc_s[:, b % 2, :]
                dve.wait_ge(gate_moved, 16 * 17)
                dve.wait_ge(s_exp, b + 1)
                chain(nc.vector.reciprocal(stat_s[:, b, 4:6], stat_s[:, b, 2:4]))
                chain(nc.vector.tensor_tensor(stat_s[:, b, 4:6], stat_s[:, b, 4:6], gate_s[:, b, 1:3], ALU.mult))
                dve.wait_ge(o_mm, b + 1)
                if b >= 2:
                    dve.wait_ge(t_fin, b - 1)
                chain(nc.vector.tensor_scalar(a, ps[:, 7, 0:256], gate_s[:, b, 0:1], None, ALU.mult))
                chain(nc.vector.scalar_tensor_tensor(a, ps[:, 6, 0:256], stat_s[:, b, 4:5], a, ALU.mult, ALU.add))
                nc.vector.scalar_tensor_tensor(a, ps[:, 6, 256:512], stat_s[:, b, 5:6], a, ALU.mult, ALU.add).then_inc(o_read, 1)
                dve.wait_ge(o_read, b + 1)
                nc.vector.tensor_tensor(a, a, tab("own_kv"), ALU.mult).then_inc(acc_ready, 1)

            def heads_out(b, n):
                dve.wait_ge(t_mm, n + 1)
                for g in range(2):
                    lo = 128 * g + 64 * g
                    src = ps[:, 4 + n % 2, lo:lo + 64].rearrange("p (e r i) -> p r i e", e=2, r=REP)
                    last = nc.vector.tensor_reduce(
                        attn_t[:, 4 * g:4 * g + 4, SEQ + DT * b:SEQ + DT * b + DT].rearrange("p r (i o) -> p r i o", o=1),
                        src, AX.X, ALU.add)
                last.then_inc(t_fin, 1)

            scores_out(0)
            for b in range(NB):
                if b + 1 < NB:
                    scores_out(b + 1)
                if b >= 1:
                    heads_out(b - 1, t_group(b, 4))
                rows_out(b)
            heads_out(NB - 1, t_group(NB, 0))

            items = ITEMS

            def p_top(i):
                n = items[i][0]
                dve.wait_ge(p_mm, i + 1)
                s = ps[:, i % 4, :]
                chain(nc.vector.tensor_tensor(s[:, n * P:(n + 1) * P], s[:, n * P:(n + 1) * P], tab("causal"), ALU.add))
                nc.vector.tensor_reduce(nmax_p[:, i % 8:i % 8 + 1], s[:, 0:(n + 1) * P], AX.X, ALU.max,
                                        negate=True).then_inc(p_max, 1)

            def p_acc(i):
                n, c, e, r = items[i]
                f, s = f_p[:, i % 8:i % 8 + 1], sum_p[:, i % 8:i % 8 + 1]
                dve.wait_ge(p_exp, i + 1)
                chain(nc.vector.reciprocal(f, s))
                head = 2 * c + e
                g = gates[:, n, 3 * head + 1 + r:3 * head + 2 + r]
                chain(nc.vector.tensor_tensor(f, f, g, ALU.mult))
                dve.wait_ge(po_mm, i + 1)
                a = acc[:, n, HD * (2 * c + e):HD * (2 * c + e + 1)]
                if i >= 1:
                    dve.wait_ge(po_read, i)
                nc.vector.scalar_tensor_tensor(a, ps[:, 6 + i % 2, 0:HD], f, a, ALU.mult, ALU.add).then_inc(po_read, 1)

            LAG = 3
            for i in range(len(items) + LAG):
                if i < len(items):
                    p_top(i)
                if i >= LAG:
                    p_acc(i - LAG)

            for m in range(C):
                lo_part("attn", m, attn_t[:, m, :])
            for m in range(C):
                add_square(6, m)
            post_norm(6, 5)
            pre_norm(7, 6, "mlp1")
            mlp(1, 8)
            post_norm(8, 7)
            for m in range(C):
                lo_part("x1", m, x[:, m, :])
            ple(1)


def feature_major(a):
    a = np.asarray(a)
    r = a.reshape(a.shape[:-1] + (a.shape[-1] // P, P))
    n = a.ndim - 2
    return np.ascontiguousarray(np.moveaxis(r, [n, n + 1, n + 2], [n + 2, n + 1, n]))


def weight_blocks(w, width=256):
    k, m = w.shape
    return w.reshape(k // P, P, m // width, width).transpose(2, 1, 0, 3).reshape(m // width, P, -1)


def mlp_blocks(up, down):
    f = FF // Q4
    return [weight_blocks(part) for n in range(Q4) for part in (up[:, f * n:f * n + f], down[f * n:f * n + f])]


HEAD_ORDER = np.arange(D).reshape(2, 2, REP, HD).transpose(0, 2, 1, 3).reshape(-1)


def constants():
    t = np.zeros((P, NCON), np.float32)

    def put(name, v):
        a, b = CON[name]
        t[:v.shape[0], a:b] = v.reshape(v.shape[0], -1)

    p = np.arange(P)
    put("ident", np.eye(P))
    put("eps", np.full((P, 1), EPS))
    put("mean", np.full((P, P), 1.0 / D))
    pick = np.zeros((P, 4, P))
    for i in range(4):
        pick[32 * i, i] = 1.0
    put("pick", pick)
    d = p % HD
    half = HALF
    pos = np.concatenate([np.arange(SEQ), np.tile(PAST + np.arange(DT), NB)]).astype(np.float32)
    inv = np.power(np.float32(500000.0), -np.arange(half, dtype=np.float32) * np.float32(2.0 / 16))
    ang = (pos[None, :] * inv[:, None].astype(np.float32)).astype(np.float32)
    cos, sin = np.cos(ang), np.sin(ang)
    rot = d < 2 * half
    put("cos", np.where(rot[:, None], cos[d % half], 1.0))
    put("sin", np.where(rot[:, None], np.where(d < half, -1.0, 1.0)[:, None] * sin[d % half], 0.0))
    qq = np.arange(P)
    put("causal", np.where(qq[None, :] <= qq[:, None], 0.0, NEG))
    g, i = p // 32, p % DT
    put("same_q", (g[:, None] == g[None, :]) & (i[:, None] == i[None, :]))
    qpos = np.arange(PT)[None, :] * P + qq[:, None]
    c = np.arange(NCP)
    ok = (16 * c + 31)[None, None, :] <= qpos[:, :, None]
    put("cmp_add", np.where(ok, 0.0, NEG))
    put("cmp_mul", ok.astype(np.float32))
    kb, kj = np.arange(NS) // DT, np.arange(NS) % DT
    ok = (kb[None, None, :] == np.arange(NB)[None, :, None]) & (kj[None, None, :] <= i[:, None, None])
    put("new_add", np.where(ok, 0.0, NEG))
    put("win_add", np.where(np.arange(DT)[None, :] > i[:, None], 0.0, NEG))
    put("block_no", np.tile(np.arange(16), (P, 1)))
    put("own_kv", (np.arange(256) // HD)[None, :] == g[:, None])
    return t


def kernel(**inputs):
    import concourse.bacc as bacc
    from concourse.bass_utils import run_bass_kernel_spmd

    v = {k: np.asarray(a) for k, a in inputs.items()}
    tokens = np.concatenate([v["x_prompt"].reshape(SEQ, D), v["x_sample"].reshape(NS, D)])
    p_tokens = np.concatenate([v["p_prompt"].reshape(2, SEQ, 256), v["p_sample"].reshape(2, NS, 256)], axis=1)
    par = np.zeros((P, NPAR), np.float32)

    def put(name, a):
        lo, hi = PAR[name]
        par[:, lo:hi] = a.reshape(-1, P).T

    glu = np.arange(2 * D).reshape(2, C, P)[::-1].transpose(1, 0, 2).reshape(-1)
    put("norm_g", v["norm_g"])
    put("b_ple", v["b_ple_gate"])
    put("b_pw1", v["conv_b_pw1"][0][glu])
    lo, hi = PAR["w_dw"]
    par[:, lo:hi] = v["conv_w_dw"][0].reshape(TAPS, C, P).transpose(2, 1, 0).reshape(P, -1)
    put("b_dw", v["conv_b_dw"])
    put("ln_g", v["conv_ln_g"])
    put("ln_b", v["conv_ln_b"])
    put("b_pw2", v["conv_b_pw2"])
    lo, hi = PAR["pe"]
    par[:, lo:hi] = v["nsa_cmp_pe"][0].reshape(2, 16, 2, HD).transpose(2, 3, 0, 1).reshape(P, -1)
    w_in = v["nsa_w_in"][0]
    kv_at = lambda i: w_in[:, D + 256 * i:D + 256 * (i + 1)]
    w_g = w_in[:, D + 6 * 256:].reshape(D, 2, 2, REP, 3).transpose(0, 1, 3, 2, 4).reshape(D, 48)
    w_q = w_in[:, :D][:, HEAD_ORDER]
    kv_pair = lambda i, j: weight_blocks(np.concatenate([kv_at(i), kv_at(j)], 1))
    w = np.concatenate(
        [weight_blocks(v["conv_w_pw1"][0][:, glu]), weight_blocks(v["conv_w_pw2"][0])]
        + mlp_blocks(v["w_ff1"][0], v["w_ff2"][0]) + [weight_blocks(v["w_ple_gate"][0])]
        + [weight_blocks(w_q), kv_pair(0, 1), kv_pair(2, 4), kv_pair(3, 5), weight_blocks(v["nsa_w_out"][0][HEAD_ORDER])]
        + mlp_blocks(v["w_ff1"][1], v["w_ff2"][1]) + [weight_blocks(v["w_ple_gate"][1])])
    arrays = {
        "x": feature_major(tokens), "p": feature_major(p_tokens), "par": par, "con": constants(), "w": w,
        "ple": np.stack([weight_blocks(v["w_ple"][i], D)[0] for i in range(2)]),
        "state": np.ascontiguousarray(v["state_conv"][0].reshape(NB, TAPS - 1, C, P).transpose(3, 2, 0, 1)),
        "w_gates": weight_blocks(w_g, 48)[0],
    }
    cc = v["cache_cmp"][0].reshape(POOL, 8, 8, 2, 2, KV, HD).transpose(0, 3, 6, 4, 2, 1, 5)
    arrays["cmp_pages"] = cc.reshape(POOL, P, 512)
    cs = v["cache_sel"][0]
    keys = cs[:, :, 0].reshape(POOL, P, 2, 2, HD).transpose(0, 3, 4, 2, 1).reshape(POOL, P, 256)
    arrays["sel_pages"] = np.concatenate([keys, cs[:, :, 1].reshape(POOL, P, 256)], 2)
    cw = v["cache_win"][0]
    keys = cw[:, :, 0].reshape(NB, WIN, 2, 2, HD).transpose(0, 3, 4, 2, 1).reshape(NB, P, 1024)
    vals = cw[:, :, 1].reshape(NB, 4, P, 256).transpose(0, 2, 1, 3).reshape(NB, P, 1024)
    arrays["win"] = np.concatenate([keys, vals], 2)
    arrays["pages"] = v["page_table"].reshape(1, NB * PAGES)
    w1 = v["nsa_cmp_w1"][0].reshape(2, 16, 2, HD, P)
    arrays["w1"] = w1.transpose(2, 3, 0, 1, 4).reshape(P, 2, 16, P)
    arrays["w2"] = v["nsa_cmp_w2"][0].transpose(1, 0, 2)
    outs = {"win": (NB, P, BLK // 2), "y": (P, C, T), "conv_p": (P, C, TAPS - 1), "conv_s": (P, C, NB, TAPS - 1), "kv_cmp": (P, 4, T), "k_rot": (P, 4, T),
            "v_tok": (P, PT, 512), "v_tok_s": (NS, 512)}
    nc = bacc.Bacc("TRN2", target_bir_lowering=False, num_devices=1)
    arrays = {f"in_{k}": np.ascontiguousarray(a) for k, a in arrays.items()}
    ext = {k[3:]: nc.dram_tensor(k, a.shape, mybir.dt.from_np(a.dtype), kind="ExternalInput").ap()
           for k, a in arrays.items()}
    out = {k: nc.dram_tensor(f"out_{k}", s, F32, kind="ExternalOutput").ap() for k, s in outs.items()}
    program(nc, ext, out)
    r = run_bass_kernel_spmd(nc, [arrays], core_ids=[0]).results[0]
    got = {k: r[f"out_{k}"] for k in outs}

    def kv_rows(a, i):
        return a[:, 2 * i:2 * i + 2].transpose(2, 1, 0).reshape(T, KV, HD)

    v_all = np.concatenate([got["v_tok"].transpose(1, 0, 2).reshape(SEQ, 512), got["v_tok_s"]])
    cmp_rows = np.stack([kv_rows(got["kv_cmp"], 0), kv_rows(got["kv_cmp"], 1)], 1)
    sel_rows = np.stack([kv_rows(got["k_rot"], 0), v_all[:, :256].reshape(T, KV, HD)], 1)
    win_rows = np.stack([kv_rows(got["k_rot"], 1), v_all[:, 256:].reshape(T, KV, HD)], 1)
    split = lambda a: (a[:SEQ][None, None], a[SEQ:].reshape((1, NB, DT) + a.shape[1:]))
    cmp_p, cmp_s = split(cmp_rows)
    sel_p, sel_s = split(sel_rows)
    win_p, win_s = split(win_rows)
    y = got["y"].transpose(2, 1, 0).reshape(T, D)
    y_p, y_s = y[:SEQ].reshape(1, SEQ, D), y[SEQ:].reshape(NB, DT, D)
    wk = got["win"][:, :, :1024].reshape(NB, 2, HD, 2, WIN).transpose(0, 4, 3, 1, 2).reshape(NB, WIN, KV, HD)
    wv = got["win"][:, :, 1024:].reshape(NB, P, 4, KV, HD).transpose(0, 2, 1, 3, 4).reshape(NB, WIN, KV, HD)
    win_all = np.concatenate([np.stack([wk, wv], 2)[None][:, :, DT:], win_s], 2)
    conv_p = got["conv_p"].transpose(2, 1, 0).reshape(1, 1, TAPS - 1, D)
    conv_s = got["conv_s"].transpose(2, 3, 1, 0).reshape(1, NB, TAPS - 1, D)
    return y_p, y_s, cmp_p, cmp_s, sel_p, sel_s, win_p, win_all, conv_p, conv_s
```
